# Optimizing a Trainium2 kernel written in Bass

```python
import jax, jax.numpy as jnp
from jax import lax
import numpy as np
import jax
import jax.numpy as jnp

D_MODEL = 1024
BATCH = 1
SEQ = 256
DEPTH = 2

CHUNK = 64
Q_BLOCK = 128
HEAD_DIM = 64
N_HEADS_FOX = 6
N_HEADS_SB = 5
N_HEADS_DSA = 5
W_FOX = N_HEADS_FOX * HEAD_DIM
W_SB = N_HEADS_SB * HEAD_DIM
W_DSA = N_HEADS_DSA * HEAD_DIM
KV_LATENT = 128
N_IDX_HEADS = 4
IDX_DIM = 64
TOPK_MAX = 256
ROPE_THETA = 500000.0
ROPE_DIM = HEAD_DIM // 4
D_FF = 2816
N_BRANCH = 3
EPS = 1e-6
D_IN = 3 * W_FOX + N_HEADS_FOX + 3 * W_SB + W_DSA + KV_LATENT + N_IDX_HEADS * IDX_DIM + IDX_DIM + N_IDX_HEADS + N_BRANCH * D_MODEL


def _in_sizes():
    return [W_FOX, W_FOX, W_FOX, N_HEADS_FOX,
            W_SB, W_SB, W_SB,
            W_DSA, KV_LATENT, N_IDX_HEADS * IDX_DIM, IDX_DIM, N_IDX_HEADS,
            N_BRANCH * D_MODEL]

def _split_points():
    pts, acc = [], 0
    for s in _in_sizes()[:-1]:
        acc += s
        pts.append(acc)
    return pts

def rmsnorm(x, g):
    xf = x.astype(jnp.float32)
    y = xf * lax.rsqrt(jnp.mean(xf * xf, axis=-1, keepdims=True) + EPS)
    return (y * g.astype(jnp.float32)).astype(x.dtype)

def swiglu(h, w_gu, w_down):
    g, u = jnp.split(h @ w_gu, 2, axis=-1)
    return (jax.nn.silu(g) * u) @ w_down

def rope_tables(seq):
    pos = jnp.arange(seq, dtype=jnp.float32)
    inv = ROPE_THETA ** (-jnp.arange(0, ROPE_DIM, 2, dtype=jnp.float32) / ROPE_DIM)
    ang = pos[:, None] * inv[None, :]
    return jnp.cos(ang), jnp.sin(ang)

def partial_rope(x, cos, sin):
    half = ROPE_DIM // 2
    x1 = x[..., :half].astype(jnp.float32)
    x2 = x[..., half:ROPE_DIM].astype(jnp.float32)
    c = cos[None, :, None, :]
    s = sin[None, :, None, :]
    r1 = (x1 * c - x2 * s).astype(x.dtype)
    r2 = (x2 * c + x1 * s).astype(x.dtype)
    return jnp.concatenate([r1, r2, x[..., ROPE_DIM:]], axis=-1)

def forgetting_attention(q, k, v, f_logit):
    B, S, H, Dh = q.shape
    scale = Dh ** -0.5
    c = jnp.cumsum(jax.nn.log_sigmoid(f_logit.astype(jnp.float32)), axis=1)
    c = c.transpose(0, 2, 1)
    outs = []
    for start in range(0, S, Q_BLOCK):
        end = start + Q_BLOCK
        s = jnp.einsum('bqhd,bkhd->bhqk', q[:, start:end], k[:, :end]).astype(jnp.float32) * scale
        bias = c[:, :, start:end, None] - c[:, :, None, :end]
        t_pos = jnp.arange(start, end)
        s_pos = jnp.arange(end)
        mask = s_pos[None, :] <= t_pos[:, None]
        p = jax.nn.softmax(jnp.where(mask, s + bias, -jnp.inf), axis=-1)
        outs.append(jnp.einsum('bhqk,bkhd->bqhd', p.astype(v.dtype), v[:, :end]))
    return jnp.concatenate(outs, axis=1)

def stick_breaking_attention(q, k, v):
    B, S, H, Dh = q.shape
    scale = Dh ** -0.5
    outs = []
    for start in range(0, S, Q_BLOCK):
        end = start + Q_BLOCK
        z = jnp.einsum('bqhd,bkhd->bhqk', q[:, start:end], k[:, :end]).astype(jnp.float32) * scale
        t_pos = jnp.arange(start, end)
        s_pos = jnp.arange(end)
        mask = s_pos[None, :] < t_pos[:, None]
        log_1m = jnp.where(mask, jax.nn.log_sigmoid(-z), 0.0)
        acc = lax.cumsum(log_1m, axis=3, reverse=True) - log_1m
        a = jnp.where(mask, jnp.exp(jax.nn.log_sigmoid(z) + acc), 0.0)
        outs.append(jnp.einsum('bhqk,bkhd->bqhd', a.astype(v.dtype), v[:, :end]))
    return jnp.concatenate(outs, axis=1)

def dsa_attention(q, k, v, iq, ik, iw):
    B, S, H, Dh = q.shape
    scale = Dh ** -0.5
    chunk_id = jnp.arange(S) // CHUNK
    topk = min(TOPK_MAX, S // 4)
    outs = []
    for start in range(0, S, Q_BLOCK):
        end = start + Q_BLOCK
        kk = min(topk, end)
        q_chunk = chunk_id[start:end]
        rel = jax.nn.relu(jnp.einsum('bqhd,bkd->bqhk', iq[:, start:end], ik[:, :end]).astype(jnp.float32))
        score = jnp.einsum('bqhk,bqh->bqk', rel, iw[:, start:end].astype(jnp.float32))
        admissible = chunk_id[None, :end] <= q_chunk[:, None]
        score = jnp.where(admissible[None], score, -jnp.inf)
        _, sel = lax.top_k(score, kk)
        valid = chunk_id[sel] <= q_chunk[None, :, None]
        k_sel = jax.vmap(lambda kb, ib: kb[ib])(k[:, :end], sel)
        v_sel = jax.vmap(lambda vb, ib: vb[ib])(v[:, :end], sel)
        s = jnp.einsum('bqhd,bqkd->bqhk', q[:, start:end], k_sel).astype(jnp.float32) * scale
        p = jax.nn.softmax(jnp.where(valid[:, :, None, :], s, -jnp.inf), axis=-1)
        outs.append(jnp.einsum('bqhk,bqkd->bqhd', p.astype(v.dtype), v_sel))
    return jnp.concatenate(outs, axis=1)

def hybrid_mixer(h, w_in, b_forget, g_kv, w_kv_up, g_idx_k, w_up_fox, w_up_sb, w_up_dsa, w_out, cos, sin):
    B, S, _ = h.shape
    (q_a, k_a, v_a, f_a, q_b, k_b, v_b, q_c, c_kv, q_i, k_i, w_i, gates) = jnp.split(h @ w_in, _split_points(), axis=-1)
    heads = lambda t, n: t.reshape(B, S, n, HEAD_DIM)
    y_a = forgetting_attention(heads(q_a, N_HEADS_FOX), heads(k_a, N_HEADS_FOX), heads(v_a, N_HEADS_FOX), f_a + b_forget)
    y_b = stick_breaking_attention(heads(q_b, N_HEADS_SB), heads(k_b, N_HEADS_SB), heads(v_b, N_HEADS_SB))
    k_c, v_c = jnp.split(rmsnorm(c_kv, g_kv) @ w_kv_up, 2, axis=-1)
    q_c = partial_rope(heads(q_c, N_HEADS_DSA), cos, sin)
    k_c = partial_rope(k_c[:, :, None, :], cos, sin)[:, :, 0]
    q_i = partial_rope(q_i.reshape(B, S, N_IDX_HEADS, IDX_DIM), cos, sin)
    k_i = partial_rope(rmsnorm(k_i, g_idx_k)[:, :, None, :], cos, sin)[:, :, 0]
    y_c = dsa_attention(q_c, k_c, v_c, q_i, k_i, w_i)
    g_a, g_b, g_c = jnp.split(jax.nn.sigmoid(gates), N_BRANCH, axis=-1)
    merged = (g_a * (y_a.reshape(B, S, W_FOX) @ w_up_fox)
              + g_b * (y_b.reshape(B, S, W_SB) @ w_up_sb)
              + g_c * (y_c.reshape(B, S, W_DSA) @ w_up_dsa))
    return merged @ w_out

def first_inputs(seed: int = 0) -> dict:
    key = jax.random.key(seed)
    ks = jax.random.split(key, 20)
    f32 = jnp.float32
    nrm = lambda k, shape, fan_in: jax.random.normal(k, shape, f32) * (fan_in ** -0.5)
    gain = lambda k, shape: 1.0 + 0.02 * jax.random.normal(k, shape, f32)
    return {
        "x": jax.random.normal(ks[0], (BATCH, SEQ, D_MODEL), f32),
        "g_ffn1": gain(ks[1], (DEPTH, D_MODEL)),
        "w_ffn1_gu": nrm(ks[2], (DEPTH, D_MODEL, 2 * D_FF), D_MODEL),
        "w_ffn1_down": nrm(ks[3], (DEPTH, D_FF, D_MODEL), D_FF),
        "g_mix": gain(ks[4], (DEPTH, D_MODEL)),
        "w_in": nrm(ks[5], (DEPTH, D_MODEL, D_IN), D_MODEL),
        "b_forget": 2.0 + 0.5 * jax.random.normal(ks[6], (DEPTH, N_HEADS_FOX), f32),
        "g_kv_latent": gain(ks[7], (DEPTH, KV_LATENT)),
        "w_kv_up": nrm(ks[8], (DEPTH, KV_LATENT, 2 * HEAD_DIM), KV_LATENT),
        "g_idx_k": gain(ks[9], (DEPTH, IDX_DIM)),
        "w_up_fox": nrm(ks[10], (DEPTH, W_FOX, D_MODEL), W_FOX),
        "w_up_sb": nrm(ks[11], (DEPTH, W_SB, D_MODEL), W_SB),
        "w_up_dsa": nrm(ks[12], (DEPTH, W_DSA, D_MODEL), W_DSA),
        "w_out": nrm(ks[13], (DEPTH, D_MODEL, D_MODEL), D_MODEL),
        "g_ffn2": gain(ks[14], (DEPTH, D_MODEL)),
        "w_ffn2_gu": nrm(ks[15], (DEPTH, D_MODEL, 2 * D_FF), D_MODEL),
        "w_ffn2_down": nrm(ks[16], (DEPTH, D_FF, D_MODEL), D_FF),
        "g_final": gain(ks[17], (D_MODEL,)),
    }

def first_block(x, g_ffn1, w_ffn1_gu, w_ffn1_down, g_mix, w_in, b_forget, g_kv_latent, w_kv_up, g_idx_k,
              w_up_fox, w_up_sb, w_up_dsa, w_out, g_ffn2, w_ffn2_gu, w_ffn2_down, g_final):
    cos, sin = rope_tables(x.shape[1])
    for l in range(DEPTH):
        x = x + 0.5 * swiglu(rmsnorm(x, g_ffn1[l]), w_ffn1_gu[l], w_ffn1_down[l])
        x = x + hybrid_mixer(rmsnorm(x, g_mix[l]), w_in[l], b_forget[l], g_kv_latent[l], w_kv_up[l], g_idx_k[l],
                             w_up_fox[l], w_up_sb[l], w_up_dsa[l], w_out[l], cos, sin)
        x = x + 0.5 * swiglu(rmsnorm(x, g_ffn2[l]), w_ffn2_gu[l], w_ffn2_down[l])
    return rmsnorm(x, g_final)


GRID_W = 64
CTX_LEN = 256
N_MOD = 9
NA_HEADS = 8
NA_HEAD_DIM = 64
NA_WIDTH = NA_HEADS * NA_HEAD_DIM
NA_KH = 8
NA_KW = 16
POOL_WINDOWS = (2, 4, 8, 16)
POOL_GROUPS = len(POOL_WINDOWS)
POOL_WIDTH = D_MODEL - NA_WIDTH
POOL_GROUP_DIM = POOL_WIDTH // POOL_GROUPS
EVEN_IN_WIDTH = 3 * NA_WIDTH + POOL_WIDTH
EVEN_MIX_WIDTH = NA_WIDTH + POOL_WIDTH
CONV_WIDTH = D_MODEL
CONV_K = 3
N_EVEN = (DEPTH + 1) // 2
N_ODD = DEPTH // 2
RMS_EPS = 1e-6
NEG_INF = -1e30


def rms_norm(x, g):
    x32 = x.astype(jnp.float32)
    y = x32 * lax.rsqrt(jnp.mean(x32 * x32, axis=-1, keepdims=True) + RMS_EPS)
    return (y * g.astype(jnp.float32)).astype(x.dtype)

def modulate(h, shift, scale):
    return h * (1 + scale) + shift

def adaln(cond, w, b):
    m = jax.nn.silu(cond) @ w + b
    return m.reshape(m.shape[:-1] + (N_MOD, D_MODEL))

def swiglu_2(h, w13, w2):
    a, b = jnp.split(h @ w13, 2, axis=-1)
    return (jax.nn.silu(a) * b) @ w2

def ffn_sublayer(h, m, g, w13, w2, base):
    hn = modulate(rms_norm(h, g), m[:, :, base], m[:, :, base + 1])
    return h + 0.5 * m[:, :, base + 2] * swiglu_2(hn, w13, w2)

def split_heads(t):
    return t.reshape(t.shape[:2] + (NA_HEADS, NA_HEAD_DIM))

def neighbourhood_attention(q, k, v, k_ctx, v_ctx, rpb):
    B, L, H, dh = q.shape
    R = L // GRID_W
    kh = min(NA_KH, R)
    kw = NA_KW
    scale = dh ** -0.5
    qg = q.reshape(B, R, GRID_W, H, dh)
    kg = k.reshape(B, R, GRID_W, H, dh)
    vg = v.reshape(B, R, GRID_W, H, dh)
    r = jnp.arange(R)
    row_start = jnp.clip(r - kh // 2, 0, R - kh)
    ridx = row_start[:, None] + jnp.arange(kh)[None, :]
    k_blk = kg[:, ridx]
    v_blk = vg[:, ridx]
    col = jnp.arange(GRID_W)
    col_start = jnp.clip(col - kw // 2, 0, GRID_W - kw)
    col_ok = (col[None, :] >= col_start[:, None]) & (col[None, :] < col_start[:, None] + kw)
    ri = ridx - r[:, None] + (NA_KH - 1)
    ci = jnp.clip(col[None, :] - col[:, None] + (NA_KW - 1), 0, 2 * NA_KW - 2)
    bias = rpb[:, ri[:, None, :, None], ci[None, :, None, :]].astype(jnp.float32)
    s_win = jnp.einsum('brqhd,brkwhd->bhrqkw', qg, k_blk).astype(jnp.float32) * scale + bias
    s_win = jnp.where(col_ok[:, None, :], s_win, NEG_INF)
    n_win = kh * GRID_W
    s_win = s_win.reshape(B, H, R, GRID_W, n_win)
    s_ctx = jnp.einsum('brqhd,bchd->bhrqc', qg, k_ctx).astype(jnp.float32) * scale
    p = jax.nn.softmax(jnp.concatenate([s_win, s_ctx], axis=-1), axis=-1).astype(v.dtype)
    p_win = p[..., :n_win].reshape(B, H, R, GRID_W, kh, GRID_W)
    o = (jnp.einsum('bhrqkw,brkwhd->brqhd', p_win, v_blk)
         + jnp.einsum('bhrqc,bchd->brqhd', p[..., n_win:], v_ctx))
    return o.reshape(B, L, H * dh)

def context_attention(q, k, v):
    B, C, H, dh = q.shape
    s = jnp.einsum('bqhd,bkhd->bhqk', q, k).astype(jnp.float32) * dh ** -0.5
    p = jax.nn.softmax(s, axis=-1).astype(v.dtype)
    return jnp.einsum('bhqk,bkhd->bqhd', p, v).reshape(B, C, H * dh)

def multiscale_pool(u, pool_w, pool_scale):
    B, L, _ = u.shape
    t = jnp.arange(L)
    ug = u.reshape(B, L, POOL_GROUPS, POOL_GROUP_DIM)
    outs = []
    for g, w in enumerate(POOL_WINDOWS):
        xg = ug[:, :, g].astype(jnp.float32)
        cs = jnp.pad(jnp.cumsum(xg, axis=1), ((0, 0), (1, 0), (0, 0)))
        lo = jnp.clip(t - w // 2, 0, L)
        hi = jnp.clip(t - w // 2 + w, 0, L)
        cnt = (hi - lo).astype(jnp.float32)[None, :, None]
        mean = (jnp.take(cs, hi, axis=1) - jnp.take(cs, lo, axis=1)) / cnt
        outs.append((mean - xg).astype(u.dtype) @ pool_w[g])
    return jnp.concatenate(outs, axis=-1) * pool_scale

def even_mixer(hl, hc, w_in, w_out, rpb, pool_w, pool_scale, ctx_out):
    q, k, v, u = jnp.split(hl @ w_in, [NA_WIDTH, 2 * NA_WIDTH, 3 * NA_WIDTH], axis=-1)
    k_c, v_c = jnp.split(hc @ w_in[:, NA_WIDTH:3 * NA_WIDTH], 2, axis=-1)
    k_c, v_c = split_heads(k_c), split_heads(v_c)
    att = neighbourhood_attention(split_heads(q), split_heads(k), split_heads(v), k_c, v_c, rpb)
    pool = multiscale_pool(u, pool_w, pool_scale)
    y_lat = jnp.concatenate([att, pool], axis=-1) @ w_out
    y_ctx = None
    if ctx_out:
        q_c = split_heads(hc @ w_in[:, :NA_WIDTH])
        u_c = hc @ w_in[:, 3 * NA_WIDTH:]
        att_c = context_attention(q_c, k_c, v_c)
        pool_c = multiscale_pool(u_c, pool_w, pool_scale)
        y_ctx = jnp.concatenate([att_c, pool_c], axis=-1) @ w_out
    return y_lat, y_ctx

def short_conv_mixer(h, w_in, conv_w, w_out):
    bg, cg, xin = jnp.split(h @ w_in, 3, axis=-1)
    z = cg * xin
    L = h.shape[1]
    zp = jnp.pad(z, ((0, 0), (1, 1), (0, 0)))
    y = zp[:, 0:L] * conv_w[0] + zp[:, 1:L + 1] * conv_w[1] + zp[:, 2:L + 2] * conv_w[2]
    return (bg * y) @ w_out

def second_inputs(seed: int = 0) -> dict:
    key = jax.random.key(seed)
    ks = jax.random.split(key, 18)
    D = D_MODEL

    def nrm(k, shape, s):
        return jax.random.normal(k, shape, jnp.float32) * s

    return {
        "x": nrm(ks[0], (BATCH, SEQ, D), 1.0),
        "c": nrm(ks[1], (BATCH, D), 1.0),
        "ctx": nrm(ks[2], (BATCH, CTX_LEN, D), 1.0),
        "c_ctx": nrm(ks[3], (D,), 1.0),
        "mod_w": nrm(ks[4], (DEPTH, D, N_MOD * D), 0.5 * D ** -0.5),
        "mod_b": nrm(ks[5], (DEPTH, N_MOD * D), 0.01),
        "norm_g": 1.0 + nrm(ks[6], (DEPTH, 3, D), 0.02),
        "ffn_w13": nrm(ks[7], (DEPTH, 2, D, 2 * D_FF), D ** -0.5),
        "ffn_w2": nrm(ks[8], (DEPTH, 2, D_FF, D), D_FF ** -0.5),
        "even_w_in": nrm(ks[9], (N_EVEN, D, EVEN_IN_WIDTH), D ** -0.5),
        "even_w_out": nrm(ks[10], (N_EVEN, EVEN_MIX_WIDTH, D), EVEN_MIX_WIDTH ** -0.5),
        "na_rpb": nrm(ks[11], (N_EVEN, NA_HEADS, 2 * NA_KH - 1, 2 * NA_KW - 1), 0.1),
        "pool_w": nrm(ks[12], (N_EVEN, POOL_GROUPS, POOL_GROUP_DIM, POOL_GROUP_DIM), POOL_GROUP_DIM ** -0.5),
        "pool_scale": 1.0 + nrm(ks[13], (N_EVEN, POOL_WIDTH), 0.1),
        "conv_w_in": nrm(ks[14], (N_ODD, D, 3 * CONV_WIDTH), D ** -0.5),
        "conv_w": nrm(ks[15], (N_ODD, CONV_K, CONV_WIDTH), CONV_K ** -0.5),
        "conv_w_out": nrm(ks[16], (N_ODD, CONV_WIDTH, D), CONV_WIDTH ** -0.5),
        "final_g": 1.0 + nrm(ks[17], (D,), 0.02),
    }

def second_block(x, c, ctx, c_ctx, mod_w, mod_b, norm_g, ffn_w13, ffn_w2, even_w_in, even_w_out,
              na_rpb, pool_w, pool_scale, conv_w_in, conv_w, conv_w_out, final_g):
    for i in range(DEPTH):
        even = (i % 2 == 0)
        ctx_out = any(j % 2 == 0 for j in range(i + 1, DEPTH))
        ctx_here = even or ctx_out
        m_l = adaln(c[:, None, :], mod_w[i], mod_b[i])
        m_c = adaln(c_ctx[None, None, :], mod_w[i], mod_b[i])

        x = ffn_sublayer(x, m_l, norm_g[i, 0], ffn_w13[i, 0], ffn_w2[i, 0], 0)
        if ctx_here:
            ctx = ffn_sublayer(ctx, m_c, norm_g[i, 0], ffn_w13[i, 0], ffn_w2[i, 0], 0)

        xn = modulate(rms_norm(x, norm_g[i, 1]), m_l[:, :, 3], m_l[:, :, 4])
        y_c = None
        if even:
            e = i // 2
            cn = modulate(rms_norm(ctx, norm_g[i, 1]), m_c[:, :, 3], m_c[:, :, 4])
            y_l, y_c = even_mixer(xn, cn, even_w_in[e], even_w_out[e], na_rpb[e],
                                  pool_w[e], pool_scale[e], ctx_out)
        else:
            o = i // 2
            y_l = short_conv_mixer(xn, conv_w_in[o], conv_w[o], conv_w_out[o])
            if ctx_out:
                cn = modulate(rms_norm(ctx, norm_g[i, 1]), m_c[:, :, 3], m_c[:, :, 4])
                y_c = short_conv_mixer(cn, conv_w_in[o], conv_w[o], conv_w_out[o])
        x = x + m_l[:, :, 5] * y_l

        x = ffn_sublayer(x, m_l, norm_g[i, 2], ffn_w13[i, 1], ffn_w2[i, 1], 6)
        if ctx_out:
            ctx = ctx + m_c[:, :, 5] * y_c
            ctx = ffn_sublayer(ctx, m_c, norm_g[i, 2], ffn_w13[i, 1], ffn_w2[i, 1], 6)

    return rms_norm(x, final_g)


def setup_inputs(seed=0):
    out = dict(first_inputs(seed))
    for name, value in second_inputs(seed + 1).items():
        if name != "x":
            out[name + "_2"] = value
    return out


def reference(
    x, g_ffn1, w_ffn1_gu, w_ffn1_down, g_mix, w_in, b_forget, g_kv_latent, w_kv_up, g_idx_k,
    w_up_fox, w_up_sb, w_up_dsa, w_out, g_ffn2, w_ffn2_gu, w_ffn2_down, g_final, c_2, ctx_2,
    c_ctx_2, mod_w_2, mod_b_2, norm_g_2, ffn_w13_2, ffn_w2_2, even_w_in_2, even_w_out_2,
    na_rpb_2, pool_w_2, pool_scale_2, conv_w_in_2, conv_w_2, conv_w_out_2, final_g_2,
):
    x = first_block(
        x, g_ffn1, w_ffn1_gu, w_ffn1_down, g_mix, w_in, b_forget, g_kv_latent, w_kv_up, g_idx_k,
        w_up_fox, w_up_sb, w_up_dsa, w_out, g_ffn2, w_ffn2_gu, w_ffn2_down, g_final,
    )
    return second_block(
        x, c_2, ctx_2, c_ctx_2, mod_w_2, mod_b_2, norm_g_2, ffn_w13_2, ffn_w2_2, even_w_in_2,
        even_w_out_2, na_rpb_2, pool_w_2, pool_scale_2, conv_w_in_2, conv_w_2, conv_w_out_2,
        final_g_2,
    )


_drawn_inputs = setup_inputs


def setup_inputs(seed=0):
    import zlib

    import numpy as np

    out = dict(_drawn_inputs(seed))
    spreads = {}
    factors = {'g_kv_latent': 6.521,
     'g_idx_k': 2.759,
     'g_ffn2': 3.691,
     'mod_b_2': 3.161,
     'norm_g_2': 3.961,
     'na_rpb_2': 8.0,
     'final_g_2': 2.828}
    for name, (base, spread) in spreads.items():
        noise = np.random.default_rng([zlib.crc32(name.encode()), seed]).standard_normal(out[name].shape)
        drawn = base * np.exp(spread * noise) if base else spread * noise
        out[name] = jnp.asarray(drawn.astype(out[name].dtype))
    for name, factor in factors.items():
        out[name] = (out[name] * factor).astype(out[name].dtype)
    return out
```

```python
from contextlib import ExitStack

import concourse.bass as bass
import numpy as np
from concourse import mybir

ALU = mybir.AluOpType
ACT = mybir.ActivationFunctionType
F32 = mybir.dt.float32
F32R = mybir.dt.float32r
AX_X = mybir.AxisListType.X

P = 128
SEQ = 256
NB = SEQ // P
D = 1024
DC = D // P
DFF = 2816
GW = 256
GROUPS = DFF // GW
DEPTH = 2
EPS = 1e-6
HD = 64
HF, HS, HX = 6, 5, 5
HI = 4
CHUNK = 64
TOPK = 64
NEG = -1e30
UNIT = 2048
RING = 3
QA, KA, VA, FA = 0, 384, 768, 1152
QB, KB, VB = 1158, 1478, 1798
QC, CKV, QI, KI, WI, GATES = 2118, 2438, 2566, 2822, 2886, 2890
NPJ = GATES
NA_H = 8
NMOD = 9
SCALE = HD ** -0.5

CONSTS = {}


def constants():
    i = np.arange(P)
    parts = []

    def add(name, a):
        a = np.asarray(a, np.float32)
        full = np.zeros((P, a.shape[1]), np.float32)
        full[:a.shape[0]] = a
        at = sum(p.shape[1] for p in parts)
        CONSTS[name] = (at, a.shape[1])
        parts.append(full)

    add("ident", np.eye(P))
    add("upto", i[:, None] <= i[None, :])
    add("ones", np.ones((P, P)))
    add("causal", np.where(i[None, :] > i[:, None], NEG, 0.0))
    add("before", i[:, None] < i[None, :])
    add("after", i[:, None] > i[None, :])
    add("flip8", 8.0 * np.kron(np.eye(2), np.eye(64)[::-1]))
    k = np.arange(SEQ)
    for b in range(NB):
        q = b * P + i
        add(f"chunks{b}", np.where(k[None, :(b + 1) * P] // CHUNK > q[:, None] // CHUNK, NEG, 0.0))
    col = np.arange(64)
    start = np.clip(col - 8, 0, 64 - 16)
    ok = (col[None, :] >= start[:, None]) & (col[None, :] < start[:, None] + 16)
    add("window", np.tile(np.where(ok, 0.0, NEG), (2, 4)))
    pos = np.arange(SEQ, dtype=np.float32)
    inv = np.float32(500000.0) ** (-np.arange(0, 16, 2, dtype=np.float32) / np.float32(16))
    ang = (pos[:, None] * inv[None, :].astype(np.float32)).astype(np.float32)
    for name, f in (("cos", np.cos), ("sin", np.sin)):
        t = f(ang).astype(np.float32).reshape(NB, P, 8)
        add(name, t.transpose(1, 0, 2).reshape(P, NB * 8))
    fold = np.zeros((4, 2))
    fold[[0, 2], 0] = fold[[1, 3], 1] = 1.0
    add("fold", fold)
    return np.concatenate(parts, 1)


def pool_matrices():
    t = np.arange(SEQ)
    out = np.zeros((P, 4, NB, SEQ), np.float32)
    for g, w in enumerate((2, 4, 8, 16)):
        lo, hi = np.clip(t - w // 2, 0, SEQ), np.clip(t - w // 2 + w, 0, SEQ)
        s = np.arange(SEQ)
        a = ((s[:, None] >= lo[None]) & (s[:, None] < hi[None])) / (hi - lo)[None].astype(np.float64)
        a = (a - (s[:, None] == t[None])).astype(np.float32)
        out[:, g] = a.reshape(NB, P, SEQ).transpose(1, 0, 2)
    return out.reshape(P, -1)


VEC_ROWS = {}


def program(nc, t, out):
    with ExitStack() as ctx:
        made = {}

        def sem(name):
            if name not in made:
                made[name] = ctx.enter_context(nc.semaphore(name))
            return made[name]

        def sb(name, shape, dt=F32):
            return ctx.enter_context(nc.sbuf_tensor(name, shape, dt))

        ps = ctx.enter_context(nc.psum_tensor("ps", [P, 8, 512], F32))

        raw = sb("raw", [P, RING, UNIT])
        whi = sb("whi", [P, RING, UNIT], F32R)
        wlo = sb("wlo", [P, RING, UNIT], F32R)
        X = sb("X", [P, NB, D])
        C = sb("C", [P, NB, D])
        HThi = sb("HThi", [P, DC + 1, SEQ], F32R)
        HTlo = sb("HTlo", [P, DC + 1, SEQ], F32R)
        AThi = sb("AThi", [P, 2, SEQ], F32R)
        ATlo = sb("ATlo", [P, 2, SEQ], F32R)
        NCST = t["consts"].shape[1]
        cst = sb("cst", [P, NCST])
        W0 = 5120
        arena = sb("arena", [P, W0 + 2 * NPJ + 6 * 1024])
        NV = P * len(t["vector_chunks"])
        vec = sb("vec", [P, NV])
        small = sb("small", [P, 512])
        work = sb("work", [P, 4096])
        modc = sb("modc", [P, NMOD * DC, 2])

        def cc(name, rows=P):
            at, n = CONSTS[name]
            return cst[0:rows, at:at + n]

        ident, ones = cc("ident"), cc("ones")
        xn = arena[:, 0:2048].rearrange("p (b d) -> p b d", b=NB)
        hf = arena[:, 2048:4096].rearrange("p (c t) -> p c t", c=DC)
        sg = arena[:, 4096:4608].rearrange("p (b f) -> p b f", b=NB)
        av = arena[:, 4608:5120].rearrange("p (b f) -> p b f", b=NB)
        PJ = arena[:, W0:W0 + 2 * NPJ].rearrange("p (b n) -> p b n", b=NB)
        GT = arena[:, W0 + 2 * NPJ:].rearrange("p (b n) -> p b n", b=NB)
        TT = arena[:, 0:20 * 256].rearrange("p (c t) -> p c t", c=20)

        def vcol(name, k=0):
            r = VEC_ROWS[name] + k
            return vec[:, r:r + 1]

        units = []

        def add_unit(*parts):
            units.append(parts)
            return len(units) - 1

        def kn1(w, row0, rows, n0, n):
            return w[row0:row0 + rows, n0:n0 + n]

        def kn(w, k0, nk, n0, n):
            return w[k0 * P:(k0 + nk) * P, n0:n0 + n].rearrange("(c p) n -> p c n", p=P)

        phases = []

        def phase(kind, **kw):
            phases.append(dict(kind=kind, **kw))

        def gate(j, s, coef):
            phase("gate", j=j, s=s, coef=coef)

        def ffn(w_gu, w_down, x, gated):
            u0 = len(units)
            units.extend([None] * (3 * GROUPS))
            phase("ffn", u0=u0, gu=w_gu, down=w_down, x=x, gated=gated,
                  f=sum(p["kind"] == "ffn" for p in phases))

        def norm(x, gain, shift=None):
            phase("norm", x=x, gain=gain, shift=shift)

        def wide_group(w, n0, n, evac):
            us = []
            for k0 in (0, 4):
                u = add_unit((kn(w, k0, 4, n0, n), 0, 4, n, P))
                us.append((u, [(k0 + c, P, c * n) for c in range(4)]))
            return us, n, evac

        for l in range(DEPTH):
            norm(X, [vcol("g_ffn1", l * DC + k) for k in range(DC)])
            ffn(t["w_ffn1_gu"][l], t["w_ffn1_down"][l], X, False)
            norm(X, [vcol("g_mix", l * DC + k) for k in range(DC)])
            w = t["w_in"][l]
            gs = []
            for n0 in range(0, NPJ, 512):
                n = min(512, NPJ - n0)
                gs.append(wide_group(w, n0, n, ("copy", [PJ[:, b, n0:n0 + n] for b in range(NB)])))
            for n0 in range(0, 3 * D, 512):
                gs.append(wide_group(w, GATES + n0, 512,
                                     ("sigmoid", [GT[:, b, n0:n0 + 512] for b in range(NB)])))
            phase("dense", groups=gs)
            for kind in ("prepare", "latent", "turn_heads", "index", "softmax", "stick"):
                phase(kind, l=l)
            phase("turn", src=[[PJ[:, b, at + c:at + min(c + P, n)] for b in range(NB)]
                               for at, n in ((QA, HF * HD), (QB, HS * HD), (QC, HX * HD)) for c in range(0, n, P)])
            gs = []
            for n0 in (0, 512):
                for r, (name, rows) in enumerate((("w_up_fox", HF * HD), ("w_up_sb", HS * HD), ("w_up_dsa", HX * HD))):
                    w = t[name][l]
                    full = rows // P
                    parts = [(kn(w, 0, full, n0, 512), 0, full, 512, P)]
                    ks = [(3 * r + c, P, c * 512) for c in range(full)]
                    if rows % P:
                        parts.append((kn1(w, full * P, rows % P, n0, 512), full * 512, 1, 512, rows % P))
                        ks.append((3 * r + full, rows % P, full * 512))
                    gs.append(([(add_unit(*parts), ks)], 512, ("merge", r, n0)))
            phase("dense", groups=gs)
            phase("turn", src=[[C[:, b, k * P:(k + 1) * P] for b in range(NB)] for k in range(DC)])
            phase("dense", groups=[wide_group(t["w_out"][l], n0, 512, ("add", n0)) for n0 in (0, 512)])
            norm(X, [vcol("g_ffn2", l * DC + k) for k in range(DC)])
            ffn(t["w_ffn2_gu"][l], t["w_ffn2_down"][l], X, False)
        phase("final", second=False)

        def mcol(j, k, s):
            return modc[:, j * DC + k, s:s + 1]

        def mcols(j, s):
            return [mcol(j, k, s) for k in range(DC)]

        for l in range(DEPTH):
            phase("modvec", l=l, groups=[wide_group(t["mod_w_2"][l], n0, 512, ("mod", l, n0 // P))
                                         for n0 in range(0, NMOD * D, 512)])
            gate(2, 0, 0.5)
            norm(X, mcols(1, 0), mcols(0, 0))
            ffn(t["ffn_w13_2"][l, 0], t["ffn_w2_2"][l, 0], X, True)
            if l == 0:
                gate(2, 1, 0.5)
                norm(C, mcols(1, 1), mcols(0, 1))
                ffn(t["ffn_w13_2"][l, 0], t["ffn_w2_2"][l, 0], C, True)
            norm(X, mcols(4, 0), mcols(3, 0))
            if l == 0:
                w = t["even_w_in_2"][0]
                phase("dense", groups=[wide_group(w, n0, 512, ("copy", [PJ[:, b, n0:n0 + 512] for b in range(NB)]))
                                       for n0 in range(0, 2048, 512)])
                norm(C, mcols(4, 1), mcols(3, 1))
                phase("dense", groups=[wide_group(w, n0, 512, ("copy", [GT[:, b, n0 - 512:n0] for b in range(NB)]))
                                       for n0 in (512, 1024)])
                phase("near_turn")
                phase("near")
                phase("turn", src=[[work[:, 2048 + b * 512 + k * P:2048 + b * 512 + (k + 1) * P] for b in range(NB)]
                                   for k in range(4)])
                wo = t["even_w_out_2"][0]
            else:
                w = t["conv_w_in_2"][0]
                phase("dense", groups=[wide_group(w, n0, 512, ("copy", [GT[:, b, n0:n0 + 512] for b in range(NB)]))
                                       for n0 in range(0, 3072, 512)])
                phase("conv")
                wo = t["conv_w_out_2"][0]
            gate(5, 0, 1.0)
            phase("dense", groups=[wide_group(wo, n0, 512, ("addgate", n0)) for n0 in (0, 512)])
            gate(8, 0, 0.5)
            norm(X, mcols(7, 0), mcols(6, 0))
            ffn(t["ffn_w13_2"][l, 1], t["ffn_w2_2"][l, 1], X, True)
        phase("final", second=True)

        NU = len(units)
        s_raw = [sem(f"raw_landed{r}") for r in range(RING)]
        s_hi, s_lo, s_used = sem("unit_hi"), sem("unit_lo"), sem("unit_used")

        first_unit, u = [], 0
        for ph in phases:
            first_unit.append(u)
            if ph["kind"] == "ffn":
                u = ph["u0"] + 3 * GROUPS
            elif "groups" in ph:
                u = ph["groups"][-1][0][-1][0] + 1

        def close_phase(e, eng):
            eng.drain().then_inc(sem(f"phases_{e}"), 1)

        def open_phase(e, eng, n):
            if n:
                for o in ("pe", "act", "dve"):
                    if o != e:
                        eng.wait_ge(sem(f"phases_{o}"), n)

        def taker(eng):
            seen = {}

            def take(name, n=1):
                seen[name] = seen.get(name, 0) + n
                eng.wait_ge(sem(name), seen[name])
            return take

        def linker(eng, name):
            n = [0]

            def link(i):
                n[0] += 1
                i.then_inc(sem(name), 1)
                eng.wait_ge(sem(name), n[0])
            return link

        def regions(u):
            return [(P, 0, UNIT)] if units[u] is None else [(rows, at, at + c * n) for _, at, c, n, rows in units[u]]

        def raw_count(u):
            return sum(2 if units[v] is None else len(units[v]) for v in range(u % RING, u + 1, RING))

        def reads_before(n):
            return sum(len(p["groups"]) for p in phases[:n] if p["kind"] == "dense")

        def split_hi(act, u, lead=0):
            r = u % RING
            act.wait_ge(s_raw[r], lead * 32 + 16 * raw_count(u))
            if u >= RING:
                act.wait_ge(s_used, lead * RING + (u - RING + 1))
            for rows, a, b in regions(u):
                i = nc.scalar.activation(whi[0:rows, r, a:b], raw[0:rows, r, a:b], ACT.Copy)
            i.then_inc(s_hi, 1)

        def split_lo(dve, u, lead=0):
            r = u % RING
            dve.wait_ge(s_hi, lead * RING + (u + 1))
            for rows, a, b in regions(u):
                i = nc.vector.tensor_tensor(wlo[0:rows, r, a:b], raw[0:rows, r, a:b],
                                            whi[0:rows, r, a:b].bitcast(F32), ALU.subtract)
            i.then_inc(s_lo, 1)

        class Splitter:
            def __init__(self, eng, fn):
                self.eng, self.fn, self.at = eng, fn, 0

            def upto(self, n):
                while self.at < min(n, NU):
                    self.fn(self.eng, self.at)
                    self.at += 1

        KV = small[:, 0:256].rearrange("p (b n) -> p b n", b=NB)
        mx, nmx, rsum = small[:, 256:288], small[:, 288:320], small[:, 320:352]
        rinv = small[:, 352:384]
        ssq, ssq2 = small[:, 384:392], small[:, 392:400]
        fl = small[:, 400:412].rearrange("p (b h) -> p b h", b=NB)
        fl2 = small[:, 412:424].rearrange("p (b h) -> p b h", b=NB)
        bfr = small[:, 424:430]
        csum = small[:, 436:448].rearrange("p (b h) -> p b h", b=NB)
        score_add = work[:, 3584:4096].rearrange("p (b k) -> p b k", b=NB)
        csT = work[0:HF, 3328:3584]
        prob = [work[:, 0:512], work[:, 512:1024]]
        probT = [work[:, 1024:1536], work[:, 1536:2048]]
        near_bias = [GT.rearrange("p b n -> p (b n)")[:, (1024 if n < 8 else 4096) + (n % 8) * 256:][:, 0:256]
                     for n in range(16)]
        poolA = arena[:, 3072:5120].rearrange("p (g s t) -> p g s t", g=4, s=NB)
        poolW = work[:, 3072:3584].rearrange("p (g f) -> p g f", g=4)

        def half(h):
            return slice(64 * (h % 2), 64 * (h % 2) + 64)

        def softmax_items():
            items = []
            for h in range(HF):
                for b in range(NB):
                    n = (b + 1) * P
                    adds = [(ident, cc("causal"), b * P, P),
                            (ident[0:HF, h:h + 1].broadcast_to([HF, P]), csT[:, 0:n], 0, n)]
                    items.append(dict(q=TT[half(h), h // 2, b * P:(b + 1) * P],
                                      k=[(TT[half(h), 3 + h // 2, 0:n], 0, n)], adds=adds, n=n,
                                      v=[PJ[:, c, VA + HD * h:VA + HD * (h + 1)] for c in range(b + 1)],
                                      y=ps[:, 4 + b, HD * h:HD * (h + 1)]))
            for h in range(HX):
                for b in range(NB):
                    n = (b + 1) * P
                    items.append(dict(q=TT[half(h), 12 + h // 2, b * P:(b + 1) * P],
                                      k=[(TT[half(h), 15, 0:n], 0, n)],
                                      adds=[(ident, score_add[:, b, 0:n], 0, n)], n=n,
                                      v=[KV[:, c, HD:2 * HD] for c in range(b + 1)],
                                      y=ps[:, 6 + b, HD * h:HD * (h + 1)]))
            return items

        def near_items():
            items = []
            for h in range(NA_H):
                for b in range(NB):
                    items.append(dict(q=TT[half(h), h // 2, b * P:(b + 1) * P],
                                      k=[(TT[half(h), 4 + h // 2, :], 0, SEQ), (TT[half(h), 8 + h // 2, :], SEQ, SEQ)],
                                      adds=[(cc("flip8"), near_bias[2 * h + b], 0, SEQ), (ident, cc("window"), 0, SEQ)],
                                      n=2 * SEQ,
                                      v=[PJ[:, c, 1024 + HD * h:1024 + HD * (h + 1)] for c in range(NB)]
                                      + [GT[:, c, 512 + HD * h:512 + HD * (h + 1)] for c in range(NB)],
                                      y=ps[:, 4 + b, HD * h:HD * (h + 1)]))
            return items

        def head_chunks():
            out = []
            for at, n in ((QA, 384), (KA, 384), (QB, 320), (KB, 320), (QC, 320)):
                for c in range(0, n, P):
                    out.append([PJ[:, b, at + c:at + min(c + P, n)] for b in range(NB)])
            dup = work[:, 0:512].rearrange("p (j b n) -> p j b n", j=2, b=NB)
            out.append([dup[:, 0, b, :] for b in range(NB)])
            out += [[PJ[:, b, QI + c:QI + c + P] for b in range(NB)] for c in (0, P)]
            out.append([dup[:, 1, b, :] for b in range(NB)])
            return out

        def near_chunks():
            out = [[PJ[:, b, c:c + P] for b in range(NB)] for c in range(0, 1024, P)]
            return out + [[GT[:, b, c:c + P] for b in range(NB)] for c in range(0, 512, P)]

        SBW = SEQ + P
        sb_abs = work[:, 0:SBW]
        sb_L = [work[:, SBW * (1 + j):SBW * (2 + j)] for j in range(2)]
        sb_l1 = [work[:, SBW * (3 + j):SBW * (4 + j)] for j in range(2)]
        sb_ls = [work[:, SBW * (5 + j):SBW * (6 + j)] for j in range(2)]
        sb_a = [work[:, SBW * (7 + j):SBW * (8 + j)] for j in range(2)]
        gateB = GT.rearrange("p b n -> p (b n)")[:, 5120:6144]
        gB = GT.rearrange("p b n -> p (b n)")[:, 4096:5120]
        mrow = [work[0:4, 0:512], work[0:4, 512:1024]]
        CThi = AThi.rearrange("p c t -> p (c t)")[:, 0:4 * DC].rearrange("p (k m) -> p k m", m=4)
        csil = small[:, 448:464].rearrange("p (k s) -> p k s", s=2)

        block = ctx.enter_context(nc.Block())

        @block.sync
        def _(sp):
            sp.dma_start(cst[:], t["consts"]).then_inc(sem("consts_in"), 16)
            sp.dma_start(X[:], t["x"][0].rearrange("(b p) d -> p b d", p=P)).then_inc(sem("x_in"), 16)
            for src, chunk, row in t["vectors"]:
                sp.dma_start(work[row:row + src.shape[0], chunk * P:(chunk + 1) * P], src).then_inc(sem("vectors_in"), 16)

            def free(u, lead=0):
                if u >= RING or not isinstance(lead, int):
                    sp.wait_ge(s_lo, lead * RING + (u - RING + 1))

            def load(u):
                free(u)
                for src, at, c, n, rows in units[u]:
                    dst = raw[0:rows, u % RING, at:at + c * n]
                    if c > 1:
                        dst = dst.rearrange("p (c n) -> p c n", c=c)
                    sp.dma_start(dst, src).then_inc(s_raw[u % RING], 16)

            def load_gu(ph, u, h, g0, lead=0):
                free(u, lead)
                src = ph["gu"].rearrange("(c p) (s n) -> p c s n", p=P, s=2)
                dst = raw[:, u % RING, :].rearrange("p (c s n) -> p c s n", c=4, s=2)
                for s in range(2):
                    sp.dma_start(dst[:, :, s, :], src[:, 4 * h:4 * h + 4, s, bass.ds(g0, GW)]).then_inc(s_raw[u % RING], 16)

            def load_down(ph, u, r0, lead=0):
                free(u, lead)
                for c in range(2):
                    sp.dma_start(raw[:, u % RING, c * D:(c + 1) * D],
                                 ph["down"][bass.ds(r0 + c * P, P), :]).then_inc(s_raw[u % RING], 16)

            for ph in phases:
                if ph["kind"] == "ffn":
                    u0 = ph["u0"]
                    load_gu(ph, u0, 0, 0)
                    load_gu(ph, u0 + 1, 1, 0)

                    def load_step(i):
                        load_gu(ph, u0 + 2, 0, i * GW + GW, i)
                        load_gu(ph, u0 + 3, 1, i * GW + GW, i)
                        load_down(ph, u0 + 4, i * GW, i)

                    load_step(0)
                    with sp.Fori(1, GROUPS - 1) as i:
                        load_step(i)
                    load_down(ph, u0 + 3 * GROUPS - 1, DFF - GW)
                elif "groups" in ph:
                    for us, _, _ in ph["groups"]:
                        for u, _ in us:
                            load(u)
            sp.wait_ge(sem("out_written"), 16)

        @block.gpsimd
        def _(pool):
            def bcast(src):
                return src.partition_broadcast(P)

            def through(n):
                for o in ("pe", "act", "dve"):
                    pool.wait_ge(sem(f"phases_{o}"), n)

            for n, ph in enumerate(phases):
                if ph["kind"] == "prepare":
                    l = ph["l"]
                    through(n - 1)
                    pool.dma_start(bfr, bcast(t["b_forget"][l])).then_inc(sem("prep_in"), 16)
                    pool.dma_start(work[:, 0:P], bcast(t["g_kv_latent"][l])).then_inc(sem("prep_in"), 16)
                    pool.dma_start(work[:, P:P + HD], bcast(t["g_idx_k"][l])).then_inc(sem("prep_in"), 16)
                    pool.dma_start(work[:, 1024:1024 + P], t["w_kv_up"][l]).then_inc(sem("prep_in"), 16)
                elif ph["kind"] == "final":
                    through(n - 1)
                    pool.dma_start(gB, bcast(t["final_g_2" if ph["second"] else "g_final"])).then_inc(sem("g_in"), 16)
                    if not ph["second"]:
                        pool.dma_start(C[:], t["ctx_2"][0].rearrange("(b p) d -> p b d", p=P)).then_inc(sem("g_in"), 16)
                elif ph["kind"] == "near_turn":
                    through(n - 1)
                    rpb = t["na_rpb_2"]
                    for m in range(16):
                        h, b = m // 2, m % 2
                        for r in range(2):
                            rq = 2 * b + r
                            at = (h * 15 + 7 - rq) * 31 + 15 - 63
                            src = bass.AP(rpb.tensor, at, [[1, 64], [31, 4], [1, 64]])
                            pool.dma_start(near_bias[m][64 * r:64 * r + 64, :].rearrange("p (k c) -> p k c", k=4),
                                           src).then_inc(sem("near_in"), 16)
                    pool.dma_start(poolA.rearrange("p g s t -> p (g s t)"), t["pool_mats"]).then_inc(sem("near_in"), 16)
                    pool.dma_start(poolW, t["pool_w_2"][0].rearrange("g p f -> p g f")).then_inc(sem("near_in"), 16)

        @block.tensor
        def _(pe):
            take = taker(pe)

            def mm(o, lhsT, rhs, first=True, last=True):
                return nc.tensor.matmul(o, lhsT, rhs, start=first, stop=last)

            def three(o, lh, ll, wh, wl, first, last):
                mm(o, lh, wh, first, False)
                mm(o, ll, wh, False, False)
                return mm(o, lh, wl, False, last)

            def turn(chunks, done, freed, first=0):
                for m, blocks in enumerate(chunks):
                    bank = (m // 2) % 4
                    if m % 2 == 0 and m // 2 >= 4:
                        take(freed)
                    for b, src in enumerate(blocks):
                        w = src.shape[-1]
                        i = nc.tensor.transpose(ps[0:w, bank, (m % 2) * SEQ + b * P:(m % 2) * SEQ + (b + 1) * P], src, ident)
                    if m % 2 or m == len(chunks) - 1:
                        i.then_inc(sem(done), 1)
                for _ in range(min(4, (len(chunks) + 1) // 2)):
                    take(freed)

            def run_items(items):
                N = len(items)
                for n in range(N + 2):
                    if n < N:
                        it = items[n]
                        S = ps[:, n % 2, :]
                        for m, (k, at, w) in enumerate(it["k"]):
                            mine = [a for a in it["adds"] if at <= a[2] < at + w]
                            i = mm(S[:, at:at + w], it["q"], k, True, not mine)
                            for j, (lh, rh, o, ow) in enumerate(mine):
                                i = nc.tensor.matmul(S[:, o:o + ow], lh, rh, start=False, stop=j == len(mine) - 1)
                        i.then_inc(sem("item_scores"), 1)
                    if 1 <= n <= N:
                        it = items[n - 1]
                        take("item_exp")
                        T = ps[:, 2 + (n - 1) % 2, :]
                        for c in range(it["n"] // P):
                            i = nc.tensor.transpose(T[:, c * P:(c + 1) * P], prob[(n - 1) % 2][:, c * P:(c + 1) * P], ident)
                        i.then_inc(sem("item_turned"), 1)
                    if n >= 2:
                        it = items[n - 2]
                        take("item_copied")
                        nk = it["n"] // P
                        for c in range(nk):
                            i = mm(it["y"], probT[n % 2][:, c * P:(c + 1) * P], it["v"][c], c == 0, c == nk - 1)
                        i.then_inc(sem("item_pv"), 1)

            def dense(ph, n):
                gs = ph["groups"]
                mod = ph["kind"] == "modvec"

                def mod_cols(g):
                    take("mod_row")
                    for j in range(4):
                        i = mm(ps[:, 4 + g % 2, 2 * j:2 * j + 2], mrow[g % 2][:, j * P:(j + 1) * P], cc("fold", 4))
                    i.then_inc(sem("mod_cols"), 1)

                for g, (us, w, ev) in enumerate(gs):
                    if g >= 2 and not mod:
                        take("group_read")
                    if mod and g >= 2:
                        mod_cols(g - 2)
                    bank = 2 * (g % 2)
                    for u, ks in us:
                        pe.wait_ge(s_lo, u + 1)
                        r = u % RING
                        for kc, rows, at in ks:
                            first = u == us[0][0] and kc == ks[0][0]
                            last = u == us[-1][0] and kc == ks[-1][0]
                            wh, wl = whi[0:rows, r, at:at + w], wlo[0:rows, r, at:at + w]
                            if mod:
                                mm(ps[0:4, bank, 0:w], CThi[:, kc, :], wh, first, False)
                                i = mm(ps[0:4, bank, 0:w], CThi[:, kc, :], wl, False, last)
                            else:
                                for b in range(NB):
                                    i = three(ps[:, bank + b, 0:w], HThi[0:rows, kc, b * P:(b + 1) * P],
                                              HTlo[0:rows, kc, b * P:(b + 1) * P], wh, wl, first, last)
                        i.then_inc(s_used, 1)
                if mod:
                    mod_cols(len(gs) - 2)
                    mod_cols(len(gs) - 1)
                else:
                    for _ in range(min(2, len(gs))):
                        take("group_read")

            def ffn(ph):
                u0, f = ph["u0"], ph["f"]
                n0 = f * GROUPS

                def gu(n, u, k0, lead, last):
                    pe.wait_ge(s_lo, lead * RING + (u + 1))
                    for c in range(4):
                        for b in range(NB):
                            i = three(ps[:, b, :], HThi[:, k0 + c, b * P:(b + 1) * P], HTlo[:, k0 + c, b * P:(b + 1) * P],
                                      whi[:, u % RING, c * 512:(c + 1) * 512], wlo[:, u % RING, c * 512:(c + 1) * 512],
                                      k0 + c == 0, k0 + c == DC - 1)
                    i.then_inc(s_used, 1)

                def turn_act(lead):
                    pe.wait_ge(sem("ffn_act"), lead + (n0 + 1))
                    if n0:
                        pe.wait_ge(sem("ffn_act_lo"), lead + n0)
                    elif not isinstance(lead, int):
                        pe.wait_ge(sem("ffn_act_lo"), lead)
                    for c in range(2):
                        for b in range(NB):
                            i = nc.tensor.transpose(ps[:, 2, c * SEQ + b * P:c * SEQ + (b + 1) * P], av[:, b, c * P:(c + 1) * P], ident)
                    i.then_inc(sem("ffn_turned"), 1)

                def down(u, lead, g, first, last):
                    pe.wait_ge(s_lo, lead * RING + (u + 1))
                    pe.wait_ge(sem("ffn_act_lo"), g + 1)
                    for c in range(2):
                        for b in range(NB):
                            for h in range(2):
                                at = c * D + h * 512
                                i = three(ps[:, 4 + 2 * b + h, :], AThi[:, c, b * P:(b + 1) * P], ATlo[:, c, b * P:(b + 1) * P],
                                          whi[:, u % RING, at:at + 512], wlo[:, u % RING, at:at + 512],
                                          first and c == 0, last and c == 1)
                    i.then_inc(s_used, 1)

                def step(lead, first):
                    pe.wait_ge(sem("ffn_act"), lead + (n0 + 1))
                    gu(0, u0 + 2, 0, lead, False)
                    gu(0, u0 + 3, 4, lead, True)
                    down(u0 + 4, lead, lead + n0, first, False)
                    turn_act(lead + 1)

                gu(0, u0, 0, 0, False)
                gu(0, u0 + 1, 4, 0, True)
                turn_act(0)
                step(0, True)
                with pe.Fori(1, GROUPS - 1) as i:
                    step(i, False)
                down(u0 + 3 * GROUPS - 1, 0, n0 + GROUPS - 1, False, True)

            pe.wait_ge(sem("consts_in"), 16)
            pe.wait_ge(sem("vectors_in"), 16 * len(t["vectors"]))
            for c, rows in enumerate(t["vector_chunks"]):
                i = nc.tensor.transpose(ps[:, c, 0:rows], work[0:rows, c * P:(c + 1) * P], ident[0:rows, 0:rows])
            i.then_inc(sem("vectors_turned"), 1)
            take("vectors_copied")

            for n, ph in enumerate(phases):
                kind = ph["kind"]
                open_phase("pe", pe, n)
                if kind == "norm":
                    take("xn", 2)
                    turn([[xn[:, b, k * P:(k + 1) * P] for b in range(NB)] for k in range(DC)], "h_turned", "h_read")
                elif kind == "turn":
                    turn(ph["src"], "turned", "turned_read")
                elif kind == "ffn":
                    ffn(ph)
                elif kind in ("dense", "modvec"):
                    if kind == "modvec":
                        take("c_split")
                    dense(ph, n)
                elif kind == "latent":
                    mm(ps[:, 7, 0:HF], cc("upto"), fl2[:, 0, :])
                    mm(ps[:, 7, 8:8 + HF], ones, fl2[:, 0, :], True, False)
                    mm(ps[:, 7, 8:8 + HF], cc("upto"), fl2[:, 1, :], False, True)
                    for b in range(NB):
                        i = nc.tensor.transpose(ps[:, 0, b * P:(b + 1) * P], PJ[:, b, CKV:CKV + P], ident)
                    i.then_inc(sem("latent_turned"), 1)
                    take("latent_copied")
                    for b in range(NB):
                        mm(ps[:, 1, b * P:(b + 1) * P], work[:, 512 + b * P:512 + (b + 1) * P], work[:, 1024:1024 + P])
                        i = nc.tensor.transpose(ps[0:HF, 2, b * P:(b + 1) * P], csum[:, b, :], ident)
                    i.then_inc(sem("latent_up"), 1)
                elif kind == "turn_heads":
                    turn(head_chunks(), "heads_turned", "heads_read")
                elif kind == "index":
                    for b in range(NB):
                        n_k = (b + 1) * P
                        for h in range(HI):
                            i = mm(ps[:, 2 * b + h % 2, (h // 2) * SEQ:(h // 2) * SEQ + n_k],
                                   TT[half(h), 16 + h // 2, b * P:(b + 1) * P], TT[half(h), 18, 0:n_k])
                        i.then_inc(sem("index_dots"), 1)
                elif kind == "softmax":
                    run_items(softmax_items())
                elif kind == "near_turn":
                    turn(near_chunks(), "heads_turned", "heads_read")
                    pe.wait_ge(sem("near_in"), 16 * 34)
                    for g in range(4):
                        for s in range(NB):
                            i = mm(ps[:, 4 + g % 2, 0:SEQ], PJ[:, s, 1536 + g * P:1536 + (g + 1) * P], poolA[:, g, s, :], s == 0, s == 1)
                        i.then_inc(sem("pooled"), 1)
                        take("pooled_copied")
                        mm(ps[:, 6 + g % 2, 0:SEQ], poolW[:, g, :], work[:, (g % 2) * SEQ:(g % 2 + 1) * SEQ]).then_inc(sem("pool_mapped"), 1)
                        take("pool_split")
                elif kind == "near":
                    run_items(near_items())
                elif kind == "stick":
                    def z(h):
                        Z = ps[:, h % 2, :]
                        q, k = TT[half(h), 6 + h // 2, :], TT[half(h), 9 + h // 2, :]
                        mm(Z[:, 0:SEQ], k[:, 0:P], q)
                        mm(Z[:, SEQ:SBW], k[:, P:SEQ], q[:, P:SEQ]).then_inc(sem("stick_z"), 1)

                    def acc(h):
                        take("stick_l1")
                        A, l1 = ps[:, 2 + h % 2, :], sb_l1[h % 2]
                        mm(A[:, 0:P], cc("after"), l1[:, 0:P])
                        mm(A[:, P:SEQ], cc("after"), l1[:, P:SEQ], True, False)
                        mm(A[:, P:SEQ], ones, l1[:, SEQ:SBW], False, True)
                        mm(A[:, SEQ:SBW], cc("after"), l1[:, SEQ:SBW]).then_inc(sem("stick_acc"), 1)

                    def pv(h):
                        take("stick_a")
                        a, v = sb_a[h % 2], [PJ[:, c, VB + HD * h:VB + HD * (h + 1)] for c in range(NB)]
                        mm(ps[:, 4, HD * h:HD * (h + 1)], a[:, 0:P], v[0])
                        mm(ps[:, 5, HD * h:HD * (h + 1)], a[:, P:SEQ], v[0], True, False)
                        mm(ps[:, 5, HD * h:HD * (h + 1)], a[:, SEQ:SBW], v[1], False, True).then_inc(sem("stick_pv"), 1)

                    for h in range(HS + 2):
                        if h < HS:
                            z(h)
                        if 1 <= h <= HS:
                            acc(h - 1)
                        if h >= 2:
                            pv(h - 2)
                elif kind == "conv":
                    take("conv_z")
                    for k in range(DC):
                        bank = k % 4
                        if k >= 4:
                            take("conv_split")
                        for b in range(NB):
                            nc.tensor.transpose(ps[:, bank, b * P:(b + 1) * P], GT[:, b, 1024 + k * P:1024 + (k + 1) * P], ident)
                            i = nc.tensor.transpose(ps[:, bank, SEQ + b * P:SEQ + (b + 1) * P], GT[:, b, k * P:(k + 1) * P], ident)
                        i.then_inc(sem("conv_turned"), 1)
                    for _ in range(4):
                        take("conv_split")
                elif kind == "gate":
                    for k in range(DC):
                        i = mm(ps[:, k // 4, (k % 4) * P:(k % 4 + 1) * P],
                               mcol(ph["j"], k, ph["s"]).broadcast_to([P, P]), ident)
                    i.then_inc(sem("gate_rows"), 1)
                close_phase("pe", pe)

        @block.scalar
        def _(act):
            take = taker(act)
            link = linker(act, "act_chain")
            split = Splitter(act, split_hi)
            A = nc.scalar.activation

            def hi_of_turned(dst, done, wait):
                for m in range(0, len(dst), 2):
                    bank = (m // 2) % 4
                    take(wait)
                    for j, (rows, o) in enumerate(dst[m:m + 2]):
                        i = A(o, ps[0:rows, bank, j * SEQ:(j + 1) * SEQ], ACT.Copy)
                    i.then_inc(sem(done), 1)

            def turn_dst(src, tile):
                return [(blocks[0].shape[-1], tile[0:blocks[0].shape[-1], m, :]) for m, blocks in enumerate(src)]

            def exps(items):
                for n, it in enumerate(items):
                    take("item_max")
                    if n >= 2:
                        take("item_turned")
                    A(prob[n % 2][:, 0:it["n"]], ps[:, n % 2, 0:it["n"]], ACT.Exp, bias=nmx[:, n:n + 1], scale=SCALE,
                      accum_out=rsum[:, n:n + 1]).then_inc(sem("item_exp"), 1)
                take("item_turned", min(2, len(items)))

            for n, ph in enumerate(phases):
                kind = ph["kind"]
                split.upto(first_unit[n] + RING - 1)
                open_phase("act", act, n)
                if kind == "norm" or kind == "final":
                    if n == 0:
                        act.wait_ge(sem("x_in"), 16)
                    x = ph.get("x", X)
                    for b in range(NB):
                        i = A(hf.rearrange("p c t -> p (c t)")[:, b * D:(b + 1) * D], x[:, b, :], ACT.Square, accum_out=ssq[:, b:b + 1])
                    i.then_inc(sem("squares"), 1)
                    take("means")
                    A(ssq2[:, 0:2], ssq[:, 0:2], ACT.Sqrt).then_inc(sem("roots"), 1)
                    split.upto(first_unit[n] + RING)
                    if kind == "norm":
                        for m in range(4):
                            take("h_gained")
                            A(HThi[:, 2 * m:2 * m + 2, :], hf[:, 2 * m:2 * m + 2, :], ACT.Copy).then_inc(sem("h_hi"), 1)
                    elif ph["second"]:
                        take("final_done")
                        act.dma_start(out[0].rearrange("(b p) d -> p b d", p=P), xn).then_inc(sem("out_written"), 16)
                        act.wait_ge(sem("out_written"), 16)
                elif kind == "turn":
                    hi_of_turned(turn_dst(ph["src"], HThi), "turned_hi", "turned")
                elif kind == "ffn":
                    split.upto(first_unit[n] + RING)
                    u0, n0 = ph["u0"], ph["f"] * GROUPS

                    def silu(lead):
                        act.wait_ge(s_used, lead * RING + (u0 + 2) if isinstance(lead, int) and lead == 0
                                    else lead * RING + (u0 + 1))
                        for b in range(NB):
                            A(sg[:, b, :], ps[:, b, 0:GW], ACT.Silu).then_inc(sem("ffn_silu"), 1)

                    def act_hi(lead):
                        act.wait_ge(sem("ffn_turned"), lead + (n0 + 1))
                        A(AThi[:], ps[:, 2, :].rearrange("p (c t) -> p c t", c=2), ACT.Copy).then_inc(sem("ffn_act_hi"), 1)

                    def step(lead, first):
                        silu(0 if first else lead)
                        split_hi(act, u0 + 3, lead)
                        act_hi(lead)
                        split_hi(act, u0 + 4, lead)
                        split_hi(act, u0 + 5, lead)

                    step(0, True)
                    with act.Fori(1, GROUPS - 1) as i:
                        step(i, False)
                    split.at = u0 + 3 * GROUPS
                    silu(GROUPS - 1)
                    split.upto(split.at + 1)
                    act_hi(GROUPS - 1)
                elif kind in ("dense", "modvec"):
                    if kind == "modvec":
                        for s, name in enumerate(("c", "c_ctx")):
                            r = VEC_ROWS[name]
                            i = A(csil[:, :, s], vec[:, r:r + DC], ACT.Silu)
                        link(i)
                        link(A(CThi[:, :, 0:2], csil[:], ACT.Copy))
                        act.sem_inc(sem("c_hi"), 1)
                    split.upto(first_unit[n] + RING)
                    for g, (us, w, ev) in enumerate(ph["groups"]):
                        last = us[-1][0]
                        split.upto(last + RING)
                        if ev[0] in ("copy", "sigmoid"):
                            act.wait_ge(s_used, last + 1)
                            for b in range(NB):
                                i = A(ev[1][b], ps[:, 2 * (g % 2) + b, 0:w], ACT.Copy if ev[0] == "copy" else ACT.Sigmoid)
                            i.then_inc(sem("group_read"), 1)
                elif kind == "prepare":
                    take("forget_sum")
                    link(A(fl2[:], fl[:], ACT.Abs))
                    link(A(fl2[:], fl2[:], ACT.Exp, scale=-1.0))
                    A(fl2[:], fl2[:], ACT.Ln, bias=1.0).then_inc(sem("forget_ln"), 1)
                    for b in range(NB):
                        at = 512 + b * (P + HD)
                        A(work[:, at:at + P], PJ[:, b, CKV:CKV + P], ACT.Square, accum_out=ssq[:, b:b + 1])
                        i = A(work[:, at + P:at + P + HD], PJ[:, b, KI:KI + HD], ACT.Square, accum_out=ssq[:, 2 + b:3 + b])
                    i.then_inc(sem("squares"), 1)
                    take("means")
                    A(ssq2[:, 0:4], ssq[:, 0:4], ACT.Sqrt).then_inc(sem("roots"), 1)
                elif kind == "softmax":
                    exps(softmax_items())
                elif kind == "near":
                    exps(near_items())
                elif kind == "near_turn":
                    for g in range(4):
                        take("pool_scaled")
                        A(HThi[:, 4 + g, :], work[:, 512:512 + SEQ], ACT.Copy).then_inc(sem("pool_hi"), 1)
                elif kind == "index":
                    for b in range(NB):
                        take("index_dots")
                        for h2 in range(2):
                            w = (b + 1) * P
                            o = work[:, 1024 + (2 * b + h2) * 512:1024 + (2 * b + h2 + 1) * 512].rearrange("p (h k) -> p h k", h=2)
                            i = A(o[:, :, 0:w], ps[:, 2 * b + h2, :].rearrange("p (h k) -> p h k", h=2)[:, :, 0:w], ACT.Relu)
                        i.then_inc(sem("index_relu"), 1)
                elif kind == "stick":
                    def logs(h):
                        take("stick_z")
                        link(A(sb_abs, ps[:, h % 2, 0:SBW], ACT.Abs, scale=SCALE))
                        link(A(sb_abs, sb_abs, ACT.Exp, scale=-1.0))
                        link(A(sb_L[h % 2], sb_abs, ACT.Ln, bias=1.0))
                        act.sem_inc(sem("stick_L"), 1)

                    def weight(h):
                        take("stick_arg")
                        if h >= 2:
                            take("stick_pv")
                        A(sb_a[h % 2], sb_a[h % 2], ACT.Exp).then_inc(sem("stick_exp"), 1)

                    for h in range(HS + 1):
                        if h < HS:
                            logs(h)
                        if h >= 1:
                            weight(h - 1)
                    take("stick_pv", 2)
                elif kind == "conv":
                    for k in range(DC):
                        take("conv_value")
                        A(HThi[:, k, :], work[:, 1024:1024 + SEQ], ACT.Copy).then_inc(sem("conv_hi"), 1)
                elif kind == "gate":
                    take("gate_rows")
                    A(gateB.rearrange("p (a n) -> p a n", a=2), ps[:, 0:2, :], ACT.Copy, scale=ph["coef"])
                close_phase("act", act)

        @block.vector
        def _(dve):
            take = taker(dve)
            link = linker(dve, "dve_chain")
            split = Splitter(dve, split_lo)
            V = nc.vector

            def lo_of_turned(src):
                for m in range(0, len(src), 2):
                    bank = (m // 2) % 4
                    take("turned_hi")
                    for j, blocks in enumerate(src[m:m + 2]):
                        rows = blocks[0].shape[-1]
                        i = V.tensor_tensor(HTlo[0:rows, m + j, :], ps[0:rows, bank, j * SEQ:(j + 1) * SEQ],
                                            HThi[0:rows, m + j, :].bitcast(F32), ALU.subtract)
                    i.then_inc(sem("turned_read"), 1)

            def copy_turned(src):
                for m in range(0, len(src), 2):
                    bank = (m // 2) % 4
                    take("heads_turned")
                    for j, blocks in enumerate(src[m:m + 2]):
                        rows = blocks[0].shape[-1]
                        i = V.tensor_copy(TT[0:rows, m + j, :], ps[0:rows, bank, j * SEQ:(j + 1) * SEQ])
                    i.then_inc(sem("heads_read"), 1)

            def run_items(items, ys):
                N = len(items)
                for n in range(N + 1):
                    if n < N:
                        take("item_scores")
                        link(V.reduce_max(mx[:, n:n + 1], ps[:, n % 2, 0:items[n]["n"]], AX_X))
                        V.tensor_scalar(nmx[:, n:n + 1], mx[:, n:n + 1], -SCALE, None, ALU.mult).then_inc(sem("item_max"), 1)
                    if n >= 1:
                        m = n - 1
                        take("item_turned")
                        if m >= 2:
                            take("item_pv")
                        w = items[m]["n"]
                        V.tensor_copy(probT[m % 2][:, 0:w], ps[:, 2 + m % 2, 0:w]).then_inc(sem("item_copied"), 1)
                take("item_pv", min(2, N))
                link(V.reciprocal(rinv[:, 0:N], rsum[:, 0:N]))
                for b in range(NB):
                    for o, bank, first, heads in ys:
                        r = rinv[:, first + b:first + 2 * heads:2].unsqueeze(2).broadcast_to([P, heads, HD])
                        V.tensor_tensor(o[b].rearrange("p (h d) -> p h d", d=HD),
                                        ps[:, bank + b, 0:heads * HD].rearrange("p (h d) -> p h d", d=HD), r, ALU.mult)

            def rope(x, heads):
                c = cc("cos").rearrange("p (b n) -> p b n", b=NB)
                s = cc("sin").rearrange("p (b n) -> p b n", b=NB)
                for b in range(NB):
                    cb = c[:, b, :].unsqueeze(1).broadcast_to([P, heads, 8])
                    sn = s[:, b, :].unsqueeze(1).broadcast_to([P, heads, 8])
                    x1, x2 = x[b][:, :, 0:8], x[b][:, :, 8:16]
                    tmp = [work[:, 2048 + 64 * j:2048 + 64 * j + 8 * heads].rearrange("p (h n) -> p h n", n=8) for j in range(4)]
                    V.tensor_tensor(tmp[0], x1, cb, ALU.mult)
                    V.tensor_tensor(tmp[1], x2, sn, ALU.mult)
                    V.tensor_tensor(tmp[2], x2, cb, ALU.mult)
                    link(V.tensor_tensor(tmp[3], x1, sn, ALU.mult))
                    V.tensor_tensor(x1, tmp[0], tmp[1], ALU.subtract)
                    link(V.tensor_tensor(x2, tmp[2], tmp[3], ALU.add))

            def root_means(sizes):
                take("squares")
                for at, size in sizes:
                    i = V.tensor_scalar(ssq[:, at:at + 2], ssq[:, at:at + 2], 1.0 / size, EPS, ALU.mult, ALU.add)
                i.then_inc(sem("means"), 1)
                take("roots")
                link(V.reciprocal(ssq2[:, 0:2 * len(sizes)], ssq2[:, 0:2 * len(sizes)]))

            take("vectors_turned")
            for c, rows in enumerate(t["vector_chunks"]):
                i = V.tensor_copy(vec[:, c * P:c * P + rows], ps[:, c, 0:rows])
            i.then_inc(sem("vectors_copied"), 1)
            dve.wait_ge(sem("consts_in"), 16)

            for n, ph in enumerate(phases):
                kind = ph["kind"]
                split.upto(first_unit[n] + RING - 1)
                open_phase("dve", dve, n)
                if kind in ("norm", "final"):
                    x = ph.get("x", X)
                    root_means([(0, D)])
                    if kind == "norm":
                        for b in range(NB):
                            V.tensor_scalar(xn[:, b, :], x[:, b, :], ssq2[:, b:b + 1], None, ALU.mult).then_inc(sem("xn"), 1)
                        split.upto(first_unit[n] + RING)
                        for m in range(4):
                            take("h_turned")
                            for j in range(2):
                                k = 2 * m + j
                                p = ps[:, m, j * SEQ:(j + 1) * SEQ]
                                if ph["shift"] is None:
                                    i = V.tensor_scalar(hf[:, k, :], p, ph["gain"][k], None, ALU.mult)
                                else:
                                    i = V.tensor_scalar(hf[:, k, :], p, ph["gain"][k], ph["shift"][k], ALU.mult, ALU.add)
                            i.then_inc(sem("h_gained"), 1)
                            if m:
                                take("h_hi")
                                V.tensor_tensor(HTlo[:, 2 * m - 2:2 * m, :], hf[:, 2 * m - 2:2 * m, :],
                                                HThi[:, 2 * m - 2:2 * m, :].bitcast(F32), ALU.subtract).then_inc(sem("h_read"), 1)
                        take("h_hi")
                        V.tensor_tensor(HTlo[:, 6:8, :], hf[:, 6:8, :],
                                        HThi[:, 6:8, :].bitcast(F32), ALU.subtract).then_inc(sem("h_read"), 1)
                    else:
                        take("g_in", 16 if ph["second"] else 32)
                        o = xn if ph["second"] else X
                        for b in range(NB):
                            i = V.scalar_tensor_tensor(out=o[:, b, :], in0=x[:, b, :], scalar=ssq2[:, b:b + 1], in1=gB,
                                                       op0=ALU.mult, op1=ALU.mult)
                        if ph["second"]:
                            i.then_inc(sem("final_done"), 1)
                elif kind == "turn":
                    lo_of_turned(ph["src"])
                elif kind == "ffn":
                    split.upto(first_unit[n] + RING)
                    u0, n0 = ph["u0"], ph["f"] * GROUPS

                    def times_up(lead):
                        for b in range(NB):
                            dve.wait_ge(sem("ffn_silu"), lead * 2 + (2 * n0 + b + 1))
                            i = V.tensor_tensor(av[:, b, :], sg[:, b, :], ps[:, b, GW:2 * GW], ALU.mult)
                        i.then_inc(sem("ffn_act"), 1)

                    def act_lo(lead):
                        dve.wait_ge(sem("ffn_act_hi"), lead + (n0 + 1))
                        V.tensor_tensor(ATlo[:], ps[:, 2, :].rearrange("p (c t) -> p c t", c=2), AThi[:].bitcast(F32),
                                        ALU.subtract).then_inc(sem("ffn_act_lo"), 1)

                    def step(lead):
                        times_up(lead)
                        split_lo(dve, u0 + 3, lead)
                        act_lo(lead)
                        split_lo(dve, u0 + 4, lead)
                        split_lo(dve, u0 + 5, lead)

                    with dve.Fori(0, GROUPS - 1) as i:
                        step(i)
                    split.at = u0 + 3 * GROUPS
                    times_up(GROUPS - 1)
                    split.upto(split.at + 1)
                    act_lo(GROUPS - 1)
                    dve.wait_ge(s_used, u0 + 3 * GROUPS)
                    x, yacc = ph["x"], ps[:, 4:8, :]
                    if not ph["gated"]:
                        for b in range(NB):
                            V.scalar_tensor_tensor(out=x[:, b, :], in0=ps[:, 4 + 2 * b:6 + 2 * b, :].rearrange("p a n -> p (a n)"),
                                                   scalar=0.5, in1=x[:, b, :], op0=ALU.mult, op1=ALU.add)
                    else:
                        for b in range(NB):
                            link(V.tensor_tensor(xn[:, b, :], ps[:, 4 + 2 * b:6 + 2 * b, :].rearrange("p a n -> p (a n)"),
                                                 gateB, ALU.mult))
                        for b in range(NB):
                            V.tensor_tensor(x[:, b, :], x[:, b, :], xn[:, b, :], ALU.add)
                elif kind in ("dense", "modvec"):
                    if kind == "modvec":
                        take("c_hi")
                        link(V.tensor_tensor(csil[:], csil[:], CThi[:, :, 0:2].bitcast(F32), ALU.subtract))
                        V.tensor_copy(CThi[:, :, 2:4], csil[:]).then_inc(sem("c_split"), 1)
                    split.upto(first_unit[n] + RING)

                    def mod_add(g):
                        take("mod_cols")
                        _, l, k0 = ph["groups"][g][2]
                        r = VEC_ROWS["mod_b"] + l * NMOD * DC + k0
                        link(V.tensor_tensor(modc[:, k0:k0 + 4, :], ps[:, 4 + g % 2, 0:8].rearrange("p (k s) -> p k s", s=2),
                                             vec[:, r:r + 4].unsqueeze(2).broadcast_to([P, 4, 2]), ALU.add))

                    for g, (us, w, ev) in enumerate(ph["groups"]):
                        last = us[-1][0]
                        split.upto(last + RING)
                        P2 = 2 * (g % 2)
                        if ev[0] == "mod":
                            if g >= 2:
                                mod_add(g - 2)
                            dve.wait_ge(s_used, last + 1)
                            V.tensor_copy(mrow[g % 2], ps[0:4, P2, 0:w]).then_inc(sem("mod_row"), 1)
                        elif ev[0] == "merge":
                            _, r, n0 = ev
                            dve.wait_ge(s_used, last + 1)
                            for b in range(NB):
                                o = C[:, b, n0:n0 + 512]
                                dst = o if r == 0 else work[:, b * 512:(b + 1) * 512]
                                i = V.tensor_tensor(dst, ps[:, P2 + b, :], GT[:, b, r * D + n0:r * D + n0 + 512], ALU.mult)
                            i.then_inc(sem("group_read"), 1)
                            if r:
                                dve.wait_ge(sem("group_read"), reads_before(n) + g + 1)
                                for b in range(NB):
                                    o = C[:, b, n0:n0 + 512]
                                    link(V.tensor_tensor(o, o, work[:, b * 512:(b + 1) * 512], ALU.add))
                        elif ev[0] in ("add", "addgate"):
                            n0 = ev[1]
                            dve.wait_ge(s_used, last + 1)
                            for b in range(NB):
                                o, p = X[:, b, n0:n0 + 512], ps[:, P2 + b, :]
                                if ev[0] == "add":
                                    i = V.tensor_tensor(o, p, o, ALU.add)
                                else:
                                    gated = work[:, (P2 + b) * 512:(P2 + b + 1) * 512]
                                    link(V.tensor_tensor(gated, p, gateB[:, n0:n0 + 512], ALU.mult))
                                    i = V.tensor_tensor(o, o, gated, ALU.add)
                            i.then_inc(sem("group_read"), 1)
                    if kind == "modvec":
                        mod_add(len(ph["groups"]) - 2)
                        mod_add(len(ph["groups"]) - 1)
                        for s3 in range(3):
                            r = VEC_ROWS["norm_g"] + (ph["l"] * 3 + s3) * DC
                            for s in range(2):
                                m = modc[:, (3 * s3 + 1) * DC:(3 * s3 + 2) * DC, s]
                                V.scalar_tensor_tensor(out=m, in0=m, scalar=1.0, in1=vec[:, r:r + DC], op0=ALU.add, op1=ALU.mult)
                elif kind == "prepare":
                    dve.wait_ge(sem("prep_in"), 64 * (ph["l"] + 1))
                    V.tensor_tensor(fl[:], PJ[:, :, FA:FA + HF], bfr.unsqueeze(1).broadcast_to([P, NB, HF]),
                                    ALU.add).then_inc(sem("forget_sum"), 1)
                    take("forget_ln")
                    V.scalar_tensor_tensor(out=fl2[:], in0=fl[:], scalar=0.0, in1=fl2[:], op0=ALU.min, op1=ALU.subtract)
                    root_means([(0, P), (2, HD)])
                    for b in range(NB):
                        V.scalar_tensor_tensor(out=PJ[:, b, CKV:CKV + P], in0=PJ[:, b, CKV:CKV + P], scalar=ssq2[:, b:b + 1],
                                               in1=work[:, 0:P], op0=ALU.mult, op1=ALU.mult)
                        link(V.scalar_tensor_tensor(out=PJ[:, b, KI:KI + HD], in0=PJ[:, b, KI:KI + HD],
                                                    scalar=ssq2[:, 2 + b:3 + b], in1=work[:, P:P + HD], op0=ALU.mult, op1=ALU.mult))
                    rope([PJ[:, b, QC:QC + HX * HD].rearrange("p (h d) -> p h d", d=HD) for b in range(NB)], HX)
                    rope([PJ[:, b, QI:QI + 5 * HD].rearrange("p (h d) -> p h d", d=HD) for b in range(NB)], 5)
                elif kind == "latent":
                    take("latent_turned")
                    V.tensor_copy(work[:, 512:512 + SEQ], ps[:, 0, 0:SEQ])
                    V.tensor_copy(csum[:], ps[:, 7, 0:16].rearrange("p (b h) -> p b h", b=2)[:, :, 0:HF]).then_inc(sem("latent_copied"), 1)
                    take("latent_up")
                    V.tensor_scalar(csT, ps[0:HF, 2, 0:SEQ], -1.0 / SCALE, None, ALU.mult)
                    link(V.tensor_copy(KV, ps[:, 1, 0:SEQ].rearrange("p (b n) -> p b n", b=NB)))
                    rope([KV[:, b, 0:HD].rearrange("p (h d) -> p h d", d=HD) for b in range(NB)], 1)
                    dup = work[:, 0:512].rearrange("p (j b n) -> p j b n", j=2, b=NB)
                    for e in range(2):
                        V.tensor_copy(dup[:, 0, :, HD * e:HD * (e + 1)], KV[:, :, 0:HD])
                        V.tensor_copy(dup[:, 1, :, HD * e:HD * (e + 1)], PJ[:, :, KI:KI + HD])
                elif kind == "turn_heads":
                    copy_turned(head_chunks())
                elif kind == "index":
                    sc = work[:, 0:SEQ]
                    top = small[:, 448:456]
                    for b in range(NB):
                        w = (b + 1) * P
                        take("index_relu")
                        for h in range(HI):
                            at = 1024 + b * 1024 + (h % 2) * 512 + (h // 2) * SEQ
                            r = work[:, at:at + w]
                            link(V.scalar_tensor_tensor(out=sc[:, 0:w], in0=r, scalar=PJ[:, b, WI + h:WI + h + 1],
                                                        in1=cc(f"chunks{b}") if h == 0 else sc[:, 0:w], op0=ALU.mult, op1=ALU.add))
                        left = work[:, 512:512 + w]
                        for r8 in range(TOPK // 8):
                            src = sc[:, 0:w] if r8 == 0 else left
                            link(V.max(top, src))
                            link(V.match_replace(left, top, src, 2 * NEG))
                        V.tensor_scalar(score_add[:, b, 0:w], left, 1.5 * NEG, NEG, ALU.is_gt, ALU.mult)
                elif kind == "softmax":
                    run_items(softmax_items(), [([PJ[:, b, QA:QA + HF * HD] for b in range(NB)], 4, 0, HF),
                                                ([PJ[:, b, QC:QC + HX * HD] for b in range(NB)], 6, 2 * HF, HX)])
                elif kind == "near_turn":
                    copy_turned(near_chunks())
                    for g in range(4):
                        take("pooled")
                        V.tensor_copy(work[:, (g % 2) * SEQ:(g % 2 + 1) * SEQ], ps[:, 4 + g % 2, 0:SEQ]).then_inc(sem("pooled_copied"), 1)
                        take("pool_mapped")
                        V.tensor_scalar(work[:, 512:512 + SEQ], ps[:, 6 + g % 2, 0:SEQ], vcol("pool_scale", g), None,
                                        ALU.mult).then_inc(sem("pool_scaled"), 1)
                        take("pool_hi")
                        V.tensor_tensor(HTlo[:, 4 + g, :], work[:, 512:512 + SEQ], HThi[:, 4 + g, :].bitcast(F32),
                                        ALU.subtract).then_inc(sem("pool_split"), 1)
                elif kind == "near":
                    run_items(near_items(), [([work[:, 2048 + b * 512:2048 + (b + 1) * 512] for b in range(NB)], 4, 0, NA_H)])
                elif kind == "stick":
                    before = cc("before")

                    def logs(h):
                        take("stick_L")
                        z, L, l1, ls = ps[:, h % 2, 0:SBW], sb_L[h % 2], sb_l1[h % 2], sb_ls[h % 2]
                        link(V.tensor_scalar(ls, z, SCALE, 0.0, ALU.mult, ALU.min))
                        link(V.tensor_tensor(ls, ls, L, ALU.subtract))
                        link(V.scalar_tensor_tensor(out=l1, in0=z, scalar=-SCALE, in1=ls, op0=ALU.mult, op1=ALU.add))
                        V.tensor_tensor(l1[:, 0:P], l1[:, 0:P], before, ALU.mult)
                        V.tensor_tensor(l1[:, SEQ:SBW], l1[:, SEQ:SBW], before, ALU.mult).then_inc(sem("stick_l1"), 1)

                    def weight(h):
                        take("stick_acc")
                        if h >= 2:
                            take("stick_pv")
                        a = sb_a[h % 2]
                        V.tensor_tensor(a, ps[:, 2 + h % 2, 0:SBW], sb_ls[h % 2], ALU.add).then_inc(sem("stick_arg"), 1)
                        take("stick_exp")
                        V.tensor_tensor(a[:, 0:P], a[:, 0:P], before, ALU.mult)
                        V.tensor_tensor(a[:, SEQ:SBW], a[:, SEQ:SBW], before, ALU.mult).then_inc(sem("stick_a"), 1)

                    for h in range(HS + 1):
                        if h < HS:
                            logs(h)
                        if h >= 1:
                            weight(h - 1)
                    take("stick_pv", 2)
                    for b in range(NB):
                        V.tensor_copy(PJ[:, b, QB:QB + HS * HD], ps[:, 4 + b, 0:HS * HD])
                elif kind == "conv":
                    V.memset(work[:, 0:1], 0.0)
                    V.memset(work[:, 1 + SEQ:2 + SEQ], 0.0)
                    V.tensor_tensor(GT[:, :, 1024:2048], GT[:, :, 1024:2048], GT[:, :, 2048:3072], ALU.mult).then_inc(sem("conv_z"), 1)
                    for k in range(DC):
                        bank = k % 4
                        take("conv_turned")
                        w = [vcol("conv_w", j * DC + k) for j in range(3)]
                        y = work[:, 512:512 + SEQ]
                        link(V.tensor_copy(work[:, 1:1 + SEQ], ps[:, bank, 0:SEQ]))
                        link(V.tensor_scalar(y, work[:, 0:SEQ], w[0], None, ALU.mult))
                        link(V.scalar_tensor_tensor(out=y, in0=work[:, 1:1 + SEQ], scalar=w[1], in1=y, op0=ALU.mult, op1=ALU.add))
                        link(V.scalar_tensor_tensor(out=y, in0=work[:, 2:2 + SEQ], scalar=w[2], in1=y, op0=ALU.mult, op1=ALU.add))
                        h = work[:, 1024:1024 + SEQ]
                        V.tensor_tensor(h, ps[:, bank, SEQ:2 * SEQ], y, ALU.mult).then_inc(sem("conv_value"), 1)
                        take("conv_hi")
                        V.tensor_tensor(HTlo[:, k, :], h, HThi[:, k, :].bitcast(F32), ALU.subtract).then_inc(sem("conv_split"), 1)
                close_phase("dve", dve)


_ORDER = [
    "x", "w_ffn1_gu", "w_ffn1_down", "w_in", "b_forget", "g_kv_latent", "w_kv_up", "g_idx_k",
    "w_up_fox", "w_up_sb", "w_up_dsa", "w_out", "w_ffn2_gu", "w_ffn2_down", "g_final", "ctx_2",
    "mod_w_2", "ffn_w13_2", "ffn_w2_2", "even_w_in_2", "even_w_out_2",
    "na_rpb_2", "pool_w_2", "conv_w_in_2", "conv_w_out_2", "final_g_2",
    "g_ffn1", "g_mix", "g_ffn2", "c_2", "c_ctx_2", "mod_b_2", "norm_g_2", "pool_scale_2", "conv_w_2",
]
_VECTORS = [("g_ffn1", "g_ffn1"), ("g_mix", "g_mix"), ("g_ffn2", "g_ffn2"), ("c", "c_2"), ("c_ctx", "c_ctx_2"),
            ("norm_g", "norm_g_2"), ("pool_scale", "pool_scale_2"), ("conv_w", "conv_w_2"), ("mod_b", "mod_b_2")]


def place_vectors(t):
    t["vectors"], t["vector_chunks"] = [], []
    row = 0
    for name, key in _VECTORS:
        ap = t[key]
        while len(ap.shape) > 1:
            ap = ap.rearrange("a b -> (a b)") if len(ap.shape) == 2 else ap.rearrange("a b c -> (a b) c")
        ap = ap.rearrange("(r p) -> r p", p=P)
        VEC_ROWS[name] = row
        at, n = 0, ap.shape[0]
        while at < n:
            k = min(n - at, P - row % P)
            t["vectors"].append((ap[at:at + k], row // P, row % P))
            at += k
            row += k
    t["vector_chunks"] = [min(P, row - c * P) for c in range((row + P - 1) // P)]


def kernel(**inputs):
    import numpy as _np
    import concourse.bacc as _bacc
    from concourse import mybir as _mybir
    from concourse.bass_utils import run_bass_kernel_spmd as _run

    nc = _bacc.Bacc("TRN2", target_bir_lowering=False, num_devices=1)
    arrays, t = {}, {}
    inputs = {n: inputs[n] for n in _ORDER}
    inputs["consts"] = constants()
    inputs["pool_mats"] = pool_matrices()
    for name, a in inputs.items():
        a = _np.ascontiguousarray(a)
        arrays[f"in_{name}_dram"] = a
        t[name] = nc.dram_tensor(f"in_{name}_dram", a.shape, _mybir.dt.from_np(a.dtype), kind="ExternalInput").ap()
    place_vectors(t)
    out = nc.dram_tensor("out_0_dram", (1, SEQ, D), _mybir.dt.float32, kind="ExternalOutput").ap()
    program(nc, t, out)
    r = _run(nc, [arrays], core_ids=[0])
    return r.results[0]["out_0_dram"]
```

```python
from contextlib import ExitStack

import concourse.bass as bass
import numpy as np
from concourse import mybir

ALU = mybir.AluOpType
ACT = mybir.ActivationFunctionType
F32 = mybir.dt.float32
F32R = mybir.dt.float32r
AX_X = mybir.AxisListType.X

P = 128
SEQ = 256
NB = SEQ // P
D = 1024
DC = D // P
DFF = 2816
GW = 256
GROUPS = DFF // GW
DEPTH = 2
EPS = 1e-6
HD = 64
HF, HS, HX = 6, 5, 5
HI = 4
CHUNK = 64
TOPK = 64
NEG = -1e30
UNIT = 2048
RING = 3
QA, KA, VA, FA = 0, 384, 768, 1152
QB, KB, VB = 1158, 1478, 1798
QC, CKV, QI, KI, WI, GATES = 2118, 2438, 2566, 2822, 2886, 2890
NPJ = GATES
NA_H = 8
NMOD = 9
SCALE = HD ** -0.5

CONSTS = {}


def constants():
    i = np.arange(P)
    parts = []

    def add(name, a):
        a = np.asarray(a, np.float32)
        full = np.zeros((P, a.shape[1]), np.float32)
        full[:a.shape[0]] = a
        at = sum(p.shape[1] for p in parts)
        CONSTS[name] = (at, a.shape[1])
        parts.append(full)

    add("ident", np.eye(P))
    add("upto", i[:, None] <= i[None, :])
    add("ones", np.ones((P, P)))
    add("causal", np.where(i[None, :] > i[:, None], NEG, 0.0))
    add("before", i[:, None] < i[None, :])
    add("after", i[:, None] > i[None, :])
    add("flip8", 8.0 * np.kron(np.eye(2), np.eye(64)[::-1]))
    k = np.arange(SEQ)
    for b in range(NB):
        q = b * P + i
        add(f"chunks{b}", np.where(k[None, :(b + 1) * P] // CHUNK > q[:, None] // CHUNK, NEG, 0.0))
    col = np.arange(64)
    start = np.clip(col - 8, 0, 64 - 16)
    ok = (col[None, :] >= start[:, None]) & (col[None, :] < start[:, None] + 16)
    add("window", np.tile(np.where(ok, 0.0, NEG), (2, 4)))
    pos = np.arange(SEQ, dtype=np.float32)
    inv = np.float32(500000.0) ** (-np.arange(0, 16, 2, dtype=np.float32) / np.float32(16))
    ang = (pos[:, None] * inv[None, :].astype(np.float32)).astype(np.float32)
    for name, f in (("cos", np.cos), ("sin", np.sin)):
        t = f(ang).astype(np.float32).reshape(NB, P, 8)
        add(name, t.transpose(1, 0, 2).reshape(P, NB * 8))
    fold = np.zeros((4, 2))
    fold[[0, 2], 0] = fold[[1, 3], 1] = 1.0
    add("fold", fold)
    return np.concatenate(parts, 1)


def pool_matrices():
    t = np.arange(SEQ)
    out = np.zeros((P, 4, NB, SEQ), np.float32)
    for g, w in enumerate((2, 4, 8, 16)):
        lo, hi = np.clip(t - w // 2, 0, SEQ), np.clip(t - w // 2 + w, 0, SEQ)
        s = np.arange(SEQ)
        a = ((s[:, None] >= lo[None]) & (s[:, None] < hi[None])) / (hi - lo)[None].astype(np.float64)
        a = (a - (s[:, None] == t[None])).astype(np.float32)
        out[:, g] = a.reshape(NB, P, SEQ).transpose(1, 0, 2)
    return out.reshape(P, -1)


VEC_ROWS = {}


def program(nc, t, out):
    with ExitStack() as ctx:
        made = {}

        def sem(name):
            if name not in made:
                made[name] = ctx.enter_context(nc.semaphore(name))
            return made[name]

        def sb(name, shape, dt=F32):
            return ctx.enter_context(nc.sbuf_tensor(name, shape, dt))

        ps = ctx.enter_context(nc.psum_tensor("ps", [P, 8, 512], F32))

        raw = sb("raw", [P, RING, UNIT])
        whi = sb("whi", [P, RING, UNIT], F32R)
        wlo = sb("wlo", [P, RING, UNIT], F32R)
        X = sb("X", [P, NB, D])
        C = sb("C", [P, NB, D])
        HThi = sb("HThi", [P, DC + 1, SEQ], F32R)
        HTlo = sb("HTlo", [P, DC + 1, SEQ], F32R)
        AThi = sb("AThi", [P, 2, SEQ], F32R)
        ATlo = sb("ATlo", [P, 2, SEQ], F32R)
        NCST = t["consts"].shape[1]
        cst = sb("cst", [P, NCST])
        W0 = 5120
        arena = sb("arena", [P, W0 + 2 * NPJ + 6 * 1024])
        NV = P * len(t["vector_chunks"])
        vec = sb("vec", [P, NV])
        small = sb("small", [P, 512])
        work = sb("work", [P, 4096])
        modc = sb("modc", [P, DEPTH, NMOD * DC, 2])
        CT = sb("CT", [P, DC, 4], F32R)
        mrow = sb("mrow", [4, 512])

        def cc(name, rows=P):
            at, n = CONSTS[name]
            return cst[0:rows, at:at + n]

        ident, ones = cc("ident"), cc("ones")
        xn = arena[:, 0:2048].rearrange("p (b d) -> p b d", b=NB)
        hf = arena[:, 2048:4096].rearrange("p (c t) -> p c t", c=DC)
        sg = arena[:, 4096:4608].rearrange("p (b f) -> p b f", b=NB)
        av = arena[:, 4608:5120].rearrange("p (b f) -> p b f", b=NB)
        PJ = arena[:, W0:W0 + 2 * NPJ].rearrange("p (b n) -> p b n", b=NB)
        GT = arena[:, W0 + 2 * NPJ:].rearrange("p (b n) -> p b n", b=NB)
        TT = arena[:, 0:20 * 256].rearrange("p (c t) -> p c t", c=20)

        def vcol(name, k=0):
            r = VEC_ROWS[name] + k
            return vec[:, r:r + 1]

        units = []

        def add_unit(*parts):
            units.append(parts)
            return len(units) - 1

        def kn1(w, row0, rows, n0, n):
            return w[row0:row0 + rows, n0:n0 + n]

        def kn(w, k0, nk, n0, n):
            return w[k0 * P:(k0 + nk) * P, n0:n0 + n].rearrange("(c p) n -> p c n", p=P)

        phases = []

        def phase(kind, **kw):
            phases.append(dict(kind=kind, **kw))

        x_writes = [0, 0]

        def ffn(w_gu, w_down, x, rstd=None, gate=None):
            u0 = len(units)
            units.extend([None] * (3 * GROUPS))
            phase("ffn", u0=u0, gu=w_gu, down=w_down, x=x, rstd=rstd, gate=gate,
                  f=sum(p["kind"] == "ffn" for p in phases))
            x_writes[x is C] += NB

        def norm(x, gain, shift=None):
            k = sum(p["kind"] == "norm" for p in phases)
            phase("norm", x=x, gain=gain, shift=shift, writes=x_writes[x is C], k=k)
            return rst[:, 2 * k:2 * k + 2] if shift is None else None

        def wide_group(w, n0, n, evac):
            us = []
            for k0 in (0, 4):
                u = add_unit((kn(w, k0, 4, n0, n), 0, 4, n, P))
                us.append((u, [(k0 + c, P, c * n) for c in range(4)]))
            return us, n, evac

        rst = small[:, 464:492]

        def vcols(name, k):
            r = VEC_ROWS[name] + k
            return vec[:, r:r + DC]

        phase("conditions")
        for l in range(DEPTH):
            rstd = norm(X, vcols("g_ffn1", l * DC))
            ffn(t["w_ffn1_gu"][l], t["w_ffn1_down"][l], X, rstd)
            rstd = norm(X, vcols("g_mix", l * DC))
            w = t["w_in"][l]
            gs = []
            for n0 in range(0, NPJ, 512):
                n = min(512, NPJ - n0)
                gs.append(wide_group(w, n0, n, ("copy", [PJ[:, b, n0:n0 + n] for b in range(NB)])))
            phase("dense", groups=gs, rstd=rstd, after_norm=True)
            steps = []
            for r in range(6):
                us, n, ev = wide_group(w, GATES + r * 512, 512,
                                       ("sigmoid", [GT[:, b, r * 512:(r + 1) * 512] for b in range(NB)], rstd))
                steps += [("unit", us, j, ev) for j in range(2)]
                for m in range(3):
                    n0 = (3 * r + m) * 512
                    us, n, ev = wide_group(t["mod_w_2"][l], n0, 512, ("mod", l, n0 // P))
                    steps += [("unit", us, j, ev) for j in range(2)]
            phase("beside", steps=steps)
            for kind in ("prepare", "latent", "turn_heads", "index", "softmax", "stick"):
                phase(kind, l=l)
            phase("beside_end")
            phase("turn", src=[[PJ[:, b, at + c:at + min(c + P, n)] for b in range(NB)]
                               for at, n in ((QA, HF * HD), (QB, HS * HD), (QC, HX * HD)) for c in range(0, n, P)])
            gs = []
            for n0 in (0, 512):
                for r, (name, rows) in enumerate((("w_up_fox", HF * HD), ("w_up_sb", HS * HD), ("w_up_dsa", HX * HD))):
                    w = t[name][l]
                    full = rows // P
                    parts = [(kn(w, 0, full, n0, 512), 0, full, 512, P)]
                    ks = [(3 * r + c, P, c * 512) for c in range(full)]
                    if rows % P:
                        parts.append((kn1(w, full * P, rows % P, n0, 512), full * 512, 1, 512, rows % P))
                        ks.append((3 * r + full, rows % P, full * 512))
                    gs.append(([(add_unit(*parts), ks)], 512, ("merge", r, n0)))
            phase("dense", groups=gs)
            phase("turn", src=[[C[:, b, k * P:(k + 1) * P] for b in range(NB)] for k in range(DC)])
            phase("dense", groups=[wide_group(t["w_out"][l], n0, 512, ("add", n0)) for n0 in (0, 512)])
            x_writes[0] += NB
            rstd = norm(X, vcols("g_ffn2", l * DC))
            ffn(t["w_ffn2_gu"][l], t["w_ffn2_down"][l], X, rstd)
        phase("final", second=False)
        x_writes[0] += NB

        def mcols(l, j, s):
            return modc[:, l, j * DC:(j + 1) * DC, s]

        for l in range(DEPTH):
            norm(X, mcols(l, 1, 0), mcols(l, 0, 0))
            ffn(t["ffn_w13_2"][l, 0], t["ffn_w2_2"][l, 0], X, gate=(2, l, 0))
            if l == 0:
                norm(C, mcols(l, 1, 1), mcols(l, 0, 1))
                ffn(t["ffn_w13_2"][l, 0], t["ffn_w2_2"][l, 0], C, gate=(2, l, 1))
            norm(X, mcols(l, 4, 0), mcols(l, 3, 0))
            if l == 0:
                w = t["even_w_in_2"][0]
                phase("dense", after_norm=True,
                      groups=[wide_group(w, n0, 512, ("copy", [PJ[:, b, n0:n0 + 512] for b in range(NB)]))
                              for n0 in range(0, 2048, 512)])
                norm(C, mcols(l, 4, 1), mcols(l, 3, 1))
                phase("dense", after_norm=True,
                      groups=[wide_group(w, n0, 512, ("copy", [GT[:, b, n0 - 512:n0] for b in range(NB)]))
                              for n0 in (512, 1024)])
                phase("near_turn")
                phase("near")
                phase("turn", src=[[work[:, 2048 + b * 512 + k * P:2048 + b * 512 + (k + 1) * P] for b in range(NB)]
                                   for k in range(4)])
                wo = t["even_w_out_2"][0]
            else:
                w = t["conv_w_in_2"][0]
                phase("dense", after_norm=True,
                      groups=[wide_group(w, n0, 512, ("copy", [GT[:, b, n0:n0 + 512] for b in range(NB)]))
                              for n0 in range(0, 3072, 512)])
                phase("conv")
                wo = t["conv_w_out_2"][0]
            phase("dense", gate=(5, l, 0), groups=[wide_group(wo, n0, 512, ("addgate", n0)) for n0 in (0, 512)])
            x_writes[0] += NB
            norm(X, mcols(l, 7, 0), mcols(l, 6, 0))
            ffn(t["ffn_w13_2"][l, 1], t["ffn_w2_2"][l, 1], X, gate=(8, l, 0))
        phase("final", second=True)

        NU = len(units)
        s_raw = [sem(f"raw_landed{r}") for r in range(RING)]
        s_hi, s_lo, s_used = sem("unit_hi"), sem("unit_lo"), sem("unit_used")

        first_unit, u = [], 0
        for n, ph in enumerate(phases):
            first_unit.append(u)
            if ph["kind"] == "beside":
                steps = ph["steps"]
            if ph["kind"] == "beside_end":
                ph["steps"] = steps
                u = steps[-1][1][-1][0] + 1
                continue
            if ph["kind"] == "ffn":
                u = ph["u0"] + 3 * GROUPS
            elif "groups" in ph:
                u = ph["groups"][-1][0][-1][0] + 1
        def close_phase(e, eng):
            eng.drain().then_inc(sem(f"phases_{e}"), 1)

        def open_phase(e, eng, n):
            if n and not phases[n]["kind"] in ("norm", "ffn") and not phases[n].get("after_norm"):
                for o in ("pe", "act", "dve"):
                    if o != e:
                        eng.wait_ge(sem(f"phases_{o}"), n)

        def taker(eng):
            seen = {}

            def take(name, n=1):
                seen[name] = seen.get(name, 0) + n
                eng.wait_ge(sem(name), seen[name])
            return take

        def linker(eng, name):
            n = [0]

            def link(i):
                n[0] += 1
                i.then_inc(sem(name), 1)
                eng.wait_ge(sem(name), n[0])
            return link

        def regions(u):
            return [(P, 0, UNIT)] if units[u] is None else [(rows, at, at + c * n) for _, at, c, n, rows in units[u]]

        def raw_count(u):
            return sum(2 if units[v] is None else len(units[v]) for v in range(u % RING, u + 1, RING))

        def reads_before(n):
            return sum(len(p["groups"]) for p in phases[:n]
                       if p["kind"] == "dense" and p["groups"][0][2][0] not in ("add", "addgate"))

        def split_hi(act, u, lead=0):
            r = u % RING
            act.wait_ge(s_raw[r], lead * 32 + 16 * raw_count(u))
            if u >= RING:
                act.wait_ge(s_used, lead * RING + (u - RING + 1))
            for rows, a, b in regions(u):
                i = nc.scalar.activation(whi[0:rows, r, a:b], raw[0:rows, r, a:b], ACT.Copy)
            i.then_inc(s_hi, 1)

        def split_lo(dve, u, lead=0):
            r = u % RING
            dve.wait_ge(s_hi, lead * RING + (u + 1))
            for rows, a, b in regions(u):
                i = nc.vector.tensor_tensor(wlo[0:rows, r, a:b], raw[0:rows, r, a:b],
                                            whi[0:rows, r, a:b].bitcast(F32), ALU.subtract)
            i.then_inc(s_lo, 1)

        class Splitter:
            def __init__(self, eng, fn):
                self.eng, self.fn, self.at = eng, fn, 0

            def upto(self, n):
                while self.at < min(n, NU):
                    self.fn(self.eng, self.at)
                    self.at += 1

        AT_PREPARE, AT_LATENT, AT_HEADS, AT_INDEX, AT_ITEM, AT_STICK = 4, 2, 3, 4, 1, 1

        class Beside:
            def __init__(self, step):
                self.step, self.steps, self.at = step, [], 0

            def begin(self, steps):
                self.steps, self.at = steps, 0

            def go(self, n=None):
                n = len(self.steps) - self.at if n is None else n
                for st in self.steps[self.at:self.at + n]:
                    self.step(st)
                self.at = min(self.at + n, len(self.steps))

        def written(eng, ph, b):
            if ph["writes"]:
                eng.wait_ge(sem("c_written" if ph["x"] is C else "x_written"), ph["writes"] - NB + b + 1)
            elif ph["x"] is C:
                eng.wait_ge(sem("g_in"), 32)
            else:
                eng.wait_ge(sem("x_in"), 16)

        KV = small[:, 0:256].rearrange("p (b n) -> p b n", b=NB)
        mx, nmx, rsum = small[:, 256:288], small[:, 288:320], small[:, 320:352]
        rinv = small[:, 352:384]
        ssq, ssq2 = small[:, 384:392], small[:, 392:400]
        fl = small[:, 400:412].rearrange("p (b h) -> p b h", b=NB)
        fl2 = small[:, 412:424].rearrange("p (b h) -> p b h", b=NB)
        bfr = small[:, 424:430]
        csum = small[:, 436:448].rearrange("p (b h) -> p b h", b=NB)
        score_add = work[:, 3584:4096].rearrange("p (b k) -> p b k", b=NB)
        csT = work[0:HF, 3328:3584]
        prob = [work[:, 0:512], work[:, 512:1024]]
        probT = [work[:, 1024:1536], work[:, 1536:2048]]
        near_bias = [GT.rearrange("p b n -> p (b n)")[:, (1024 if n < 8 else 4096) + (n % 8) * 256:][:, 0:256]
                     for n in range(16)]
        poolA = arena[:, 3072:5120].rearrange("p (g s t) -> p g s t", g=4, s=NB)
        poolW = work[:, 3072:3584].rearrange("p (g f) -> p g f", g=4)

        def rows_of(h):
            return slice(64 * (h % 2), 64 * (h % 2) + 64)

        def softmax_items():
            items = []
            for h in range(HF):
                for b in range(NB):
                    n = (b + 1) * P
                    adds = [(ident, cc("causal"), b * P, P),
                            (ident[0:HF, h:h + 1].broadcast_to([HF, P]), csT[:, 0:n], 0, n)]
                    items.append(dict(q=TT[rows_of(h), h // 2, b * P:(b + 1) * P],
                                      k=[(TT[rows_of(h), 3 + h // 2, 0:n], 0, n)], adds=adds, n=n,
                                      v=[PJ[:, c, VA + HD * h:VA + HD * (h + 1)] for c in range(b + 1)],
                                      y=ps[:, 4 + b, HD * h:HD * (h + 1)]))
            for h in range(HX):
                for b in range(NB):
                    n = (b + 1) * P
                    items.append(dict(q=TT[rows_of(h), 12 + h // 2, b * P:(b + 1) * P],
                                      k=[(TT[rows_of(h), 15, 0:n], 0, n)],
                                      adds=[(ident, score_add[:, b, 0:n], 0, n)], n=n,
                                      v=[KV[:, c, HD:2 * HD] for c in range(b + 1)],
                                      y=ps[:, 4 + b, HD * h:HD * (h + 1)]))
            return items

        def near_items():
            items = []
            for h in range(NA_H):
                for b in range(NB):
                    items.append(dict(q=TT[rows_of(h), h // 2, b * P:(b + 1) * P],
                                      k=[(TT[rows_of(h), 4 + h // 2, :], 0, SEQ), (TT[rows_of(h), 8 + h // 2, :], SEQ, SEQ)],
                                      adds=[(cc("flip8"), near_bias[2 * h + b], 0, SEQ), (ident, cc("window"), 0, SEQ)],
                                      n=2 * SEQ,
                                      v=[PJ[:, c, 1024 + HD * h:1024 + HD * (h + 1)] for c in range(NB)]
                                      + [GT[:, c, 512 + HD * h:512 + HD * (h + 1)] for c in range(NB)],
                                      y=ps[:, 4 + b, HD * h:HD * (h + 1)]))
            return items

        def head_chunks():
            out = []
            for at, n in ((QA, 384), (KA, 384), (QB, 320), (KB, 320), (QC, 320)):
                for c in range(0, n, P):
                    out.append([PJ[:, b, at + c:at + min(c + P, n)] for b in range(NB)])
            dup = work[:, 0:512].rearrange("p (j b n) -> p j b n", j=2, b=NB)
            out.append([dup[:, 0, b, :] for b in range(NB)])
            out += [[PJ[:, b, QI + c:QI + c + P] for b in range(NB)] for c in (0, P)]
            out.append([dup[:, 1, b, :] for b in range(NB)])
            return out

        def near_chunks():
            out = [[PJ[:, b, c:c + P] for b in range(NB)] for c in range(0, 1024, P)]
            return out + [[GT[:, b, c:c + P] for b in range(NB)] for c in range(0, 512, P)]

        SBW = SEQ + P
        sb_abs = work[:, 0:SBW]
        sb_L = [work[:, SBW * (1 + j):SBW * (2 + j)] for j in range(2)]
        sb_l1 = [work[:, SBW * (3 + j):SBW * (4 + j)] for j in range(2)]
        sb_ls = [work[:, SBW * (5 + j):SBW * (6 + j)] for j in range(2)]
        sb_a = [work[:, SBW * (7 + j):SBW * (8 + j)] for j in range(2)]
        gateB = GT.rearrange("p b n -> p (b n)")[:, 5120:6144]
        gB = GT.rearrange("p b n -> p (b n)")[:, 4096:5120]
        csil = small[:, 448:464].rearrange("p (k s) -> p k s", s=2)

        block = ctx.enter_context(nc.Block())

        @block.sync
        def _(sp):
            sp.dma_start(cst[:], t["consts"]).then_inc(sem("consts_in"), 16)
            sp.dma_start(X[:], t["x"][0].rearrange("(b p) d -> p b d", p=P)).then_inc(sem("x_in"), 16)
            for src, chunk, row in t["vectors"]:
                sp.dma_start(work[row:row + src.shape[0], chunk * P:(chunk + 1) * P], src).then_inc(sem("vectors_in"), 16)

            def free(u, lead=0):
                if u >= RING or not isinstance(lead, int):
                    sp.wait_ge(s_lo, lead * RING + (u - RING + 1))

            def load(u):
                free(u)
                for src, at, c, n, rows in units[u]:
                    dst = raw[0:rows, u % RING, at:at + c * n]
                    if c > 1:
                        dst = dst.rearrange("p (c n) -> p c n", c=c)
                    sp.dma_start(dst, src).then_inc(s_raw[u % RING], 16)

            def load_gu(ph, u, h, g0, lead=0):
                free(u, lead)
                src = ph["gu"].rearrange("(c p) (s n) -> p c s n", p=P, s=2)
                dst = raw[:, u % RING, :].rearrange("p (c s n) -> p c s n", c=4, s=2)
                for s in range(2):
                    sp.dma_start(dst[:, :, s, :], src[:, 4 * h:4 * h + 4, s, bass.ds(g0, GW)]).then_inc(s_raw[u % RING], 16)

            def load_down(ph, u, r0, lead=0):
                free(u, lead)
                for c in range(2):
                    sp.dma_start(raw[:, u % RING, c * D:(c + 1) * D],
                                 ph["down"][bass.ds(r0 + c * P, P), :]).then_inc(s_raw[u % RING], 16)

            for ph in phases:
                if ph["kind"] == "ffn":
                    u0 = ph["u0"]
                    load_gu(ph, u0, 0, 0)
                    load_gu(ph, u0 + 1, 1, 0)

                    def load_step(i):
                        load_gu(ph, u0 + 2, 0, i * GW + GW, i)
                        load_gu(ph, u0 + 3, 1, i * GW + GW, i)
                        load_down(ph, u0 + 4, i * GW, i)

                    load_step(0)
                    with sp.Fori(1, GROUPS - 1) as i:
                        load_step(i)
                    load_down(ph, u0 + 3 * GROUPS - 1, DFF - GW)
                elif "groups" in ph:
                    for us, _, _ in ph["groups"]:
                        for u, _ in us:
                            load(u)
                elif ph["kind"] == "beside":
                    for _, us, j, _ in ph["steps"]:
                        load(us[j][0])
            sp.wait_ge(sem("out_written"), 16)

        @block.gpsimd
        def _(pool):
            def bcast(src):
                return src.partition_broadcast(P)

            def through(n):
                for o in ("pe", "act", "dve"):
                    pool.wait_ge(sem(f"phases_{o}"), n)

            for n, ph in enumerate(phases):
                if ph["kind"] == "prepare":
                    l = ph["l"]
                    through(n - 1)
                    pool.dma_start(bfr, bcast(t["b_forget"][l])).then_inc(sem("prep_in"), 16)
                    pool.dma_start(work[:, 0:P], bcast(t["g_kv_latent"][l])).then_inc(sem("prep_in"), 16)
                    pool.dma_start(work[:, P:P + HD], bcast(t["g_idx_k"][l])).then_inc(sem("prep_in"), 16)
                    pool.dma_start(work[:, 1024:1024 + P], t["w_kv_up"][l]).then_inc(sem("prep_in"), 16)
                elif ph["kind"] == "final":
                    through(n - 1)
                    pool.dma_start(gB, bcast(t["final_g_2" if ph["second"] else "g_final"])).then_inc(sem("g_in"), 16)
                    if not ph["second"]:
                        pool.dma_start(C[:], t["ctx_2"][0].rearrange("(b p) d -> p b d", p=P)).then_inc(sem("g_in"), 16)
                elif ph["kind"] == "near_turn":
                    through(n - 3)
                    rpb = t["na_rpb_2"]
                    for m in range(16):
                        h, b = m // 2, m % 2
                        for r in range(2):
                            rq = 2 * b + r
                            at = (h * 15 + 7 - rq) * 31 + 15 - 63
                            src = bass.AP(rpb.tensor, at, [[1, 64], [31, 4], [1, 64]])
                            pool.dma_start(near_bias[m][64 * r:64 * r + 64, :].rearrange("p (k c) -> p k c", k=4),
                                           src).then_inc(sem("near_in"), 16)
                    through(n - 1)
                    pool.dma_start(poolA.rearrange("p g s t -> p (g s t)"), t["pool_mats"]).then_inc(sem("pool_in"), 16)
                    pool.dma_start(poolW, t["pool_w_2"][0].rearrange("g p f -> p g f")).then_inc(sem("pool_in"), 16)

        @block.tensor
        def _(pe):
            take = taker(pe)

            def mm(o, lhsT, rhs, first=True, last=True):
                return nc.tensor.matmul(o, lhsT, rhs, start=first, stop=last)

            def three(o, lh, ll, wh, wl, first, last):
                mm(o, lh, wh, first, False)
                mm(o, ll, wh, False, False)
                return mm(o, lh, wl, False, last)

            def turn(chunks, done, freed, first=0):
                for m, blocks in enumerate(chunks):
                    bank = (m // 2) % 4
                    if m % 2 == 0 and m // 2 >= 4:
                        take(freed)
                    for b, src in enumerate(blocks):
                        w = src.shape[-1]
                        i = nc.tensor.transpose(ps[0:w, bank, (m % 2) * SEQ + b * P:(m % 2) * SEQ + (b + 1) * P], src, ident)
                    if m % 2 or m == len(chunks) - 1:
                        i.then_inc(sem(done), 1)
                for _ in range(min(4, (len(chunks) + 1) // 2)):
                    take(freed)

            owed = []
            row = []

            def settle():
                while owed:
                    owed.pop()
                    take("beside_read")

            def turn_row():
                if row:
                    row.pop()
                    settle()
                    take("row_copied")
                    for j in range(4):
                        i = mm(ps[:, 7, 2 * j:2 * j + 2], mrow[:, j * P:(j + 1) * P], cc("fold", 4))
                    i.then_inc(sem("row_turned"), 1)
                    owed.append(1)

            def beside_step(st):
                _, us, j, ev = st
                turn_row()
                u, ks = us[j]
                r = u % RING
                if j == 0 and (ev[0] != "mod" or not last_mod):
                    settle()
                last_mod[:] = [1] if ev[0] == "mod" else []
                pe.wait_ge(s_lo, u + 1)
                for kc, rows, at in ks:
                    first, last = kc == 0, kc == DC - 1
                    wh, wl = whi[:, r, at:at + 512], wlo[:, r, at:at + 512]
                    if ev[0] == "mod":
                        mm(ps[0:4, 6, :], CT[:, kc, :], wh, first, False)
                        i = mm(ps[0:4, 6, :], CT[:, kc, :], wl, False, last)
                    else:
                        for b in range(NB):
                            i = three(ps[:, 6 + b, :], HThi[:, kc, b * P:(b + 1) * P],
                                      HTlo[:, kc, b * P:(b + 1) * P], wh, wl, first, last)
                i.then_inc(s_used, 1)
                if j == 1:
                    (row if ev[0] == "mod" else owed).append(1)

            last_mod = []
            beside = Beside(beside_step)

            def run_items(items, places=()):
                N = len(items)
                for n in range(N + 2):
                    if n < N:
                        it = items[n]
                        S = ps[:, n % 2, :]
                        for m, (k, at, w) in enumerate(it["k"]):
                            mine = [a for a in it["adds"] if at <= a[2] < at + w]
                            i = mm(S[:, at:at + w], it["q"], k, True, not mine)
                            for j, (lh, rh, o, ow) in enumerate(mine):
                                i = nc.tensor.matmul(S[:, o:o + ow], lh, rh, start=False, stop=j == len(mine) - 1)
                        i.then_inc(sem("item_scores"), 1)
                    if 1 <= n <= N:
                        it = items[n - 1]
                        take("item_exp")
                        T = ps[:, 2 + (n - 1) % 2, :]
                        for c in range(it["n"] // P):
                            i = nc.tensor.transpose(T[:, c * P:(c + 1) * P], prob[(n - 1) % 2][:, c * P:(c + 1) * P], ident)
                        i.then_inc(sem("item_turned"), 1)
                    if n >= 2:
                        it = items[n - 2]
                        take("item_copied")
                        if n - 2 in places:
                            take("sums_read")
                        nk = it["n"] // P
                        for c in range(nk):
                            i = mm(it["y"], probT[n % 2][:, c * P:(c + 1) * P], it["v"][c], c == 0, c == nk - 1)
                        i.then_inc(sem("item_pv"), 1)
                    beside.go(AT_ITEM)

            def gate_rows(ph, half, bank):
                j, l, st = ph["gate"]
                for k in range(4):
                    i = mm(ps[:, bank, k * P:(k + 1) * P],
                           modc[:, l, j * DC + half * 4 + k, st:st + 1].broadcast_to([P, P]), ident)
                i.then_inc(sem("gate_turned"), 1)

            def dense(ph):
                gs = ph["groups"]
                waits = gs[0][2][0] not in ("add", "addgate")
                if ph.get("gate"):
                    for half in range(2):
                        gate_rows(ph, half, 4 + half)
                for g, (us, w, ev) in enumerate(gs):
                    if g >= 2 and waits:
                        take("group_read")
                    bank = 2 * (g % 2)

                    def part(u, ks, blocks):
                        pe.wait_ge(s_lo, u + 1)
                        r = u % RING
                        for kc, rows, at in ks:
                            first = u == us[0][0] and kc == ks[0][0]
                            last = u == us[-1][0] and kc == ks[-1][0]
                            for b in blocks:
                                i = three(ps[:, bank + b, 0:w], HThi[0:rows, kc, b * P:(b + 1) * P],
                                          HTlo[0:rows, kc, b * P:(b + 1) * P],
                                          whi[0:rows, r, at:at + w], wlo[0:rows, r, at:at + w], first, last)
                        return i

                    if g == 0 and ph.get("after_norm"):
                        for b in range(NB):
                            take("h_ready", 2)
                            for u, ks in us:
                                i = part(u, ks, [b])
                                if b == NB - 1:
                                    i.then_inc(s_used, 1)
                    else:
                        for u, ks in us:
                            part(u, ks, range(NB)).then_inc(s_used, 1)
                if waits:
                    for _ in range(min(2, len(gs))):
                        take("group_read")

            def ffn(ph):
                u0, f = ph["u0"], ph["f"]
                n0 = f * GROUPS

                def gu(u, k0, lead, blocks=range(NB)):
                    pe.wait_ge(s_lo, lead * RING + (u + 1))
                    for c in range(4):
                        for b in blocks:
                            i = three(ps[:, b, :], HThi[:, k0 + c, b * P:(b + 1) * P], HTlo[:, k0 + c, b * P:(b + 1) * P],
                                      whi[:, u % RING, c * 512:(c + 1) * 512], wlo[:, u % RING, c * 512:(c + 1) * 512],
                                      k0 + c == 0, k0 + c == DC - 1)
                    if NB - 1 in blocks:
                        i.then_inc(s_used, 1)

                def turn_act(lead):
                    pe.wait_ge(sem("ffn_act"), lead + (n0 + 1))
                    if n0:
                        pe.wait_ge(sem("ffn_act_lo"), lead + n0)
                    elif not isinstance(lead, int):
                        pe.wait_ge(sem("ffn_act_lo"), lead)
                    for c in range(2):
                        for b in range(NB):
                            i = nc.tensor.transpose(ps[:, 2, c * SEQ + b * P:c * SEQ + (b + 1) * P], av[:, b, c * P:(c + 1) * P], ident)
                    i.then_inc(sem("ffn_turned"), 1)

                def down(u, lead, g, first, last):
                    pe.wait_ge(s_lo, lead * RING + (u + 1))
                    pe.wait_ge(sem("ffn_act_lo"), g + 1)
                    for b in range(NB):
                        for c in range(2):
                            for h in range(2):
                                at = c * D + h * 512
                                i = three(ps[:, 4 + 2 * b + h, :], AThi[:, c, b * P:(b + 1) * P], ATlo[:, c, b * P:(b + 1) * P],
                                          whi[:, u % RING, at:at + 512], wlo[:, u % RING, at:at + 512],
                                          first and c == 0, last and c == 1)
                            if last and (b, c) == (0, 1):
                                i.then_inc(sem("ffn_out"), 1)
                    i.then_inc(s_used, 1)

                def step(lead, first):
                    pe.wait_ge(sem("ffn_act"), lead + (n0 + 1))
                    gu(u0 + 2, 0, lead)
                    gu(u0 + 3, 4, lead)
                    down(u0 + 4, lead, lead + n0, first, False)
                    turn_act(lead + 1)

                for b in range(NB):
                    take("h_ready", 2)
                    gu(u0, 0, 0, [b])
                    gu(u0 + 1, 4, 0, [b])
                turn_act(0)
                if ph["gate"]:
                    gate_rows(ph, 0, 3)
                step(0, True)
                if ph["gate"]:
                    take("gate_read")
                    gate_rows(ph, 1, 3)
                with pe.Fori(1, GROUPS - 1) as i:
                    step(i, False)
                down(u0 + 3 * GROUPS - 1, 0, n0 + GROUPS - 1, False, True)
                if ph["gate"]:
                    take("gate_read")

            pe.wait_ge(sem("consts_in"), 16)
            pe.wait_ge(sem("vectors_in"), 16 * len(t["vectors"]))
            for c, rows in enumerate(t["vector_chunks"]):
                i = nc.tensor.transpose(ps[:, c, 0:rows], work[0:rows, c * P:(c + 1) * P], ident[0:rows, 0:rows])
            i.then_inc(sem("vectors_turned"), 1)
            take("vectors_copied")

            for n, ph in enumerate(phases):
                kind = ph["kind"]
                open_phase("pe", pe, n)
                if kind == "norm":
                    for b in range(NB):
                        if ph["shift"] is None:
                            written(pe, ph, b)
                        else:
                            take("xn")
                        src = ph["x"] if ph["shift"] is None else xn
                        for half in range(2):
                            for k in range(4):
                                i = nc.tensor.transpose(ps[:, 4 + 2 * b + half, k * P:(k + 1) * P],
                                                        src[:, b, (4 * half + k) * P:(4 * half + k + 1) * P], ident)
                            i.then_inc(sem("h_turned"), 1)
                elif kind == "turn":
                    turn(ph["src"], "turned", "turned_read")
                elif kind == "ffn":
                    ffn(ph)
                elif kind == "dense":
                    dense(ph)
                elif kind == "beside":
                    beside.begin(ph["steps"])
                elif kind == "beside_end":
                    beside.go()
                    turn_row()
                    settle()
                elif kind == "prepare":
                    beside.go(AT_PREPARE)
                elif kind == "latent":
                    mm(ps[:, 3, 0:HF], cc("upto"), fl2[:, 0, :])
                    mm(ps[:, 3, 8:8 + HF], ones, fl2[:, 0, :], True, False)
                    mm(ps[:, 3, 8:8 + HF], cc("upto"), fl2[:, 1, :], False, True)
                    for b in range(NB):
                        i = nc.tensor.transpose(ps[:, 0, b * P:(b + 1) * P], PJ[:, b, CKV:CKV + P], ident)
                    i.then_inc(sem("latent_turned"), 1)
                    beside.go(AT_LATENT)
                    take("latent_copied")
                    for b in range(NB):
                        mm(ps[:, 1, b * P:(b + 1) * P], work[:, 512 + b * P:512 + (b + 1) * P], work[:, 1024:1024 + P])
                        i = nc.tensor.transpose(ps[0:HF, 2, b * P:(b + 1) * P], csum[:, b, :], ident)
                    i.then_inc(sem("latent_up"), 1)
                elif kind == "turn_heads":
                    turn(head_chunks(), "heads_turned", "heads_read")
                    beside.go(AT_HEADS)
                elif kind == "index":
                    for b in range(NB):
                        n_k = (b + 1) * P
                        for h in range(HI):
                            i = mm(ps[:, 2 * b + h % 2, (h // 2) * SEQ:(h // 2) * SEQ + n_k],
                                   TT[rows_of(h), 16 + h // 2, b * P:(b + 1) * P], TT[rows_of(h), 18, 0:n_k])
                        i.then_inc(sem("index_dots"), 1)
                        beside.go(AT_INDEX)
                elif kind == "softmax":
                    run_items(softmax_items(), [2 * HF])
                elif kind == "near_turn":
                    turn(near_chunks(), "heads_turned", "heads_read")
                    pe.wait_ge(sem("pool_in"), 32)
                    for g in range(4):
                        for s in range(NB):
                            i = mm(ps[:, 4 + g % 2, 0:SEQ], PJ[:, s, 1536 + g * P:1536 + (g + 1) * P], poolA[:, g, s, :], s == 0, s == 1)
                        i.then_inc(sem("pooled"), 1)
                        take("pooled_copied")
                        mm(ps[:, 6 + g % 2, 0:SEQ], poolW[:, g, :], work[:, (g % 2) * SEQ:(g % 2 + 1) * SEQ]).then_inc(sem("pool_mapped"), 1)
                        take("pool_split")
                elif kind == "near":
                    pe.wait_ge(sem("near_in"), 16 * 32)
                    run_items(near_items())
                elif kind == "stick":
                    def z(h):
                        Z = ps[:, h % 2, :]
                        q, k = TT[rows_of(h), 6 + h // 2, :], TT[rows_of(h), 9 + h // 2, :]
                        mm(Z[:, 0:SEQ], k[:, 0:P], q)
                        mm(Z[:, SEQ:SBW], k[:, P:SEQ], q[:, P:SEQ]).then_inc(sem("stick_z"), 1)

                    def acc(h):
                        take("stick_l1")
                        A, l1 = ps[:, 2 + h % 2, :], sb_l1[h % 2]
                        mm(A[:, 0:P], cc("after"), l1[:, 0:P])
                        mm(A[:, P:SEQ], cc("after"), l1[:, P:SEQ], True, False)
                        mm(A[:, P:SEQ], ones, l1[:, SEQ:SBW], False, True)
                        mm(A[:, SEQ:SBW], cc("after"), l1[:, SEQ:SBW]).then_inc(sem("stick_acc"), 1)

                    def pv(h):
                        take("stick_a")
                        a, v = sb_a[h % 2], [PJ[:, c, VB + HD * h:VB + HD * (h + 1)] for c in range(NB)]
                        mm(ps[:, 4, HD * h:HD * (h + 1)], a[:, 0:P], v[0])
                        mm(ps[:, 5, HD * h:HD * (h + 1)], a[:, P:SEQ], v[0], True, False)
                        mm(ps[:, 5, HD * h:HD * (h + 1)], a[:, SEQ:SBW], v[1], False, True).then_inc(sem("stick_pv"), 1)

                    for h in range(HS + 2):
                        if h < HS:
                            z(h)
                        if 1 <= h <= HS:
                            acc(h - 1)
                        if h >= 2:
                            pv(h - 2)
                        beside.go(AT_STICK)
                elif kind == "conv":
                    take("conv_z")
                    for k in range(DC):
                        bank = k % 4
                        if k >= 4:
                            take("conv_split")
                        for b in range(NB):
                            nc.tensor.transpose(ps[:, bank, b * P:(b + 1) * P], GT[:, b, 1024 + k * P:1024 + (k + 1) * P], ident)
                            i = nc.tensor.transpose(ps[:, bank, SEQ + b * P:SEQ + (b + 1) * P], GT[:, b, k * P:(k + 1) * P], ident)
                        i.then_inc(sem("conv_turned"), 1)
                    for _ in range(4):
                        take("conv_split")
                close_phase("pe", pe)

        @block.scalar
        def _(act):
            take = taker(act)
            link = linker(act, "act_chain")
            split = Splitter(act, split_hi)
            A = nc.scalar.activation

            def hi_of_turned(dst, done, wait):
                for m in range(0, len(dst), 2):
                    bank = (m // 2) % 4
                    take(wait)
                    for j, (rows, o) in enumerate(dst[m:m + 2]):
                        i = A(o, ps[0:rows, bank, j * SEQ:(j + 1) * SEQ], ACT.Copy)
                    i.then_inc(sem(done), 1)

            def turn_dst(src, tile):
                return [(blocks[0].shape[-1], tile[0:blocks[0].shape[-1], m, :]) for m, blocks in enumerate(src)]

            def exps(items):
                for n, it in enumerate(items):
                    take("item_max")
                    if n >= 2:
                        take("item_turned")
                    A(prob[n % 2][:, 0:it["n"]], ps[:, n % 2, 0:it["n"]], ACT.Exp, bias=nmx[:, n:n + 1], scale=SCALE,
                      accum_out=rsum[:, n:n + 1]).then_inc(sem("item_exp"), 1)
                    beside.go(AT_ITEM)
                beside.go(2 * AT_ITEM)
                take("item_turned", min(2, len(items)))

            def beside_step(st):
                _, us, j, ev = st
                u = us[j][0]
                split.upto(u + RING)
                if j == 1 and ev[0] == "sigmoid":
                    act.wait_ge(s_used, u + 1)
                    for b in range(NB):
                        i = A(ev[1][b], ps[:, 6 + b, :], ACT.Sigmoid, scale=ev[2][:, b:b + 1])
                    i.then_inc(sem("beside_read"), 1)

            beside = Beside(beside_step)

            def gate_copy(ph, half, bank, coef):
                take("gate_turned")
                A(gateB[:, half * 512:(half + 1) * 512], ps[:, bank, :], ACT.Copy, scale=coef).then_inc(sem("gate_read"), 1)

            for n, ph in enumerate(phases):
                kind = ph["kind"]
                split.upto(first_unit[n] + RING - 1)
                open_phase("act", act, n)
                if kind == "conditions":
                    act.wait_ge(sem("vectors_copied"), 1)
                    for st, name in enumerate(("c", "c_ctx")):
                        r = VEC_ROWS[name]
                        i = A(csil[:, :, st], vec[:, r:r + DC], ACT.Silu)
                    link(i)
                    A(CT[:, :, 0:2], csil[:], ACT.Copy).then_inc(sem("c_hi"), 1)
                elif kind == "norm":
                    for b in range(NB):
                        written(act, ph, b)
                        A(work[:, b * D:(b + 1) * D], ph["x"][:, b, :], ACT.Square, accum_out=ssq[:, b:b + 1]).then_inc(sem("squares"), 1)
                    if ph["shift"] is not None:
                        for b in range(NB):
                            take("means")
                            A(ssq2[:, b:b + 1], ssq[:, b:b + 1], ACT.Sqrt).then_inc(sem("roots"), 1)
                    for b in range(NB):
                        for half in range(2):
                            take("h_gained")
                            A(HThi[:, 4 * half:4 * half + 4, b * P:(b + 1) * P],
                              hf[:, 4 * half:4 * half + 4, b * P:(b + 1) * P], ACT.Copy).then_inc(sem("h_hi"), 1)
                    if ph["shift"] is None:
                        for b in range(NB):
                            take("means")
                            A(ssq2[:, b:b + 1], ssq[:, b:b + 1], ACT.Sqrt).then_inc(sem("roots"), 1)
                    split.upto(first_unit[n] + RING)
                elif kind == "final":
                    x = X
                    for b in range(NB):
                        i = A(hf.rearrange("p c t -> p (c t)")[:, b * D:(b + 1) * D], x[:, b, :], ACT.Square, accum_out=ssq[:, b:b + 1])
                    i.then_inc(sem("squares"), 1)
                    take("means")
                    A(ssq2[:, 0:2], ssq[:, 0:2], ACT.Sqrt).then_inc(sem("roots"), 1)
                    if ph["second"]:
                        take("final_done")
                        act.dma_start(out[0].rearrange("(b p) d -> p b d", p=P), xn).then_inc(sem("out_written"), 16)
                        act.wait_ge(sem("out_written"), 16)
                elif kind == "turn":
                    hi_of_turned(turn_dst(ph["src"], HThi), "turned_hi", "turned")
                elif kind == "ffn":
                    split.upto(first_unit[n] + RING)
                    u0, n0 = ph["u0"], ph["f"] * GROUPS

                    def silu(lead):
                        act.wait_ge(s_used, lead * RING + (u0 + 2) if isinstance(lead, int) and lead == 0
                                    else lead * RING + (u0 + 1))
                        for b in range(NB):
                            scale = 1.0 if ph["rstd"] is None else ph["rstd"][:, b:b + 1]
                            A(sg[:, b, :], ps[:, b, 0:GW], ACT.Silu, scale=scale).then_inc(sem("ffn_silu"), 1)

                    def act_hi(lead):
                        act.wait_ge(sem("ffn_turned"), lead + (n0 + 1))
                        A(AThi[:], ps[:, 2, :].rearrange("p (c t) -> p c t", c=2), ACT.Copy).then_inc(sem("ffn_act_hi"), 1)

                    def step(lead, first):
                        silu(0 if first else lead)
                        split_hi(act, u0 + 3, lead)
                        act_hi(lead)
                        split_hi(act, u0 + 4, lead)
                        split_hi(act, u0 + 5, lead)

                    if ph["rstd"] is not None:
                        take("rstd_ready")
                    step(0, True)
                    if ph["gate"]:
                        gate_copy(ph, 0, 3, 0.5)
                    with act.Fori(1, GROUPS - 1) as i:
                        step(i, False)
                    split.at = u0 + 3 * GROUPS
                    if ph["gate"]:
                        gate_copy(ph, 1, 3, 0.5)
                    silu(GROUPS - 1)
                    split.upto(split.at + 1)
                    act_hi(GROUPS - 1)
                elif kind == "dense":
                    if ph.get("gate"):
                        for half in range(2):
                            gate_copy(ph, half, 4 + half, 1.0)
                    if ph.get("rstd") is not None:
                        take("rstd_ready")
                    split.upto(first_unit[n] + RING)
                    for g, (us, w, ev) in enumerate(ph["groups"]):
                        last = us[-1][0]
                        split.upto(last + RING)
                        if ev[0] == "copy":
                            act.wait_ge(s_used, last + 1)
                            for b in range(NB):
                                scale = 1.0 if ph.get("rstd") is None else ph["rstd"][:, b:b + 1]
                                i = A(ev[1][b], ps[:, 2 * (g % 2) + b, 0:w], ACT.Copy, scale=scale)
                            i.then_inc(sem("group_read"), 1)
                elif kind == "beside":
                    beside.begin(ph["steps"])
                elif kind == "beside_end":
                    beside.go()
                elif kind == "latent":
                    beside.go(AT_LATENT)
                elif kind == "turn_heads":
                    beside.go(AT_HEADS)
                elif kind == "prepare":
                    take("forget_sum")
                    link(A(fl2[:], fl[:], ACT.Abs))
                    link(A(fl2[:], fl2[:], ACT.Exp, scale=-1.0))
                    A(fl2[:], fl2[:], ACT.Ln, bias=1.0).then_inc(sem("forget_ln"), 1)
                    for b in range(NB):
                        at = 512 + b * (P + HD)
                        A(work[:, at:at + P], PJ[:, b, CKV:CKV + P], ACT.Square, accum_out=ssq[:, b:b + 1])
                        i = A(work[:, at + P:at + P + HD], PJ[:, b, KI:KI + HD], ACT.Square, accum_out=ssq[:, 2 + b:3 + b])
                    i.then_inc(sem("squares"), 1)
                    take("means")
                    A(ssq2[:, 0:4], ssq[:, 0:4], ACT.Sqrt).then_inc(sem("roots"), 1)
                    beside.go(AT_PREPARE)
                elif kind == "softmax":
                    exps(softmax_items())
                elif kind == "near":
                    exps(near_items())
                elif kind == "near_turn":
                    for g in range(4):
                        take("pool_scaled")
                        A(HThi[:, 4 + g, :], work[:, 512:512 + SEQ], ACT.Copy).then_inc(sem("pool_hi"), 1)
                elif kind == "index":
                    for b in range(NB):
                        take("index_dots")
                        for h2 in range(2):
                            w = (b + 1) * P
                            o = work[:, 1024 + (2 * b + h2) * 512:1024 + (2 * b + h2 + 1) * 512].rearrange("p (h k) -> p h k", h=2)
                            i = A(o[:, :, 0:w], ps[:, 2 * b + h2, :].rearrange("p (h k) -> p h k", h=2)[:, :, 0:w], ACT.Relu)
                        i.then_inc(sem("index_relu"), 1)
                        beside.go(AT_INDEX)
                elif kind == "stick":
                    def logs(h):
                        take("stick_z")
                        link(A(sb_abs, ps[:, h % 2, 0:SBW], ACT.Abs, scale=SCALE))
                        link(A(sb_abs, sb_abs, ACT.Exp, scale=-1.0))
                        link(A(sb_L[h % 2], sb_abs, ACT.Ln, bias=1.0))
                        act.sem_inc(sem("stick_L"), 1)

                    def weight(h):
                        take("stick_arg")
                        if h >= 2:
                            take("stick_pv")
                        A(sb_a[h % 2], sb_a[h % 2], ACT.Exp).then_inc(sem("stick_exp"), 1)

                    for h in range(HS + 1):
                        if h < HS:
                            logs(h)
                        if h >= 1:
                            weight(h - 1)
                        beside.go(AT_STICK)
                    take("stick_pv", 2)
                    beside.go(AT_STICK)
                elif kind == "conv":
                    for k in range(DC):
                        take("conv_value")
                        A(HThi[:, k, :], work[:, 1024:1024 + SEQ], ACT.Copy).then_inc(sem("conv_hi"), 1)
                close_phase("act", act)

        @block.vector
        def _(dve):
            take = taker(dve)
            link = linker(dve, "dve_chain")
            split = Splitter(dve, split_lo)
            V = nc.vector

            def lo_of_turned(src):
                for m in range(0, len(src), 2):
                    bank = (m // 2) % 4
                    take("turned_hi")
                    for j, blocks in enumerate(src[m:m + 2]):
                        rows = blocks[0].shape[-1]
                        i = V.tensor_tensor(HTlo[0:rows, m + j, :], ps[0:rows, bank, j * SEQ:(j + 1) * SEQ],
                                            HThi[0:rows, m + j, :].bitcast(F32), ALU.subtract)
                    i.then_inc(sem("turned_read"), 1)

            def copy_turned(src):
                for m in range(0, len(src), 2):
                    bank = (m // 2) % 4
                    take("heads_turned")
                    for j, blocks in enumerate(src[m:m + 2]):
                        rows = blocks[0].shape[-1]
                        i = V.tensor_copy(TT[0:rows, m + j, :], ps[0:rows, bank, j * SEQ:(j + 1) * SEQ])
                    i.then_inc(sem("heads_read"), 1)

            pv_seen = [0]

            def run_items(items, ys):
                N = len(items)
                base = pv_seen[0]
                pv_seen[0] += N

                def sums(o, bank, first, heads):
                    last = first + 2 * heads
                    dve.wait_ge(sem("item_pv"), base + last)
                    link(V.reciprocal(rinv[:, first:last], rsum[:, first:last]))
                    for b in range(NB):
                        r = rinv[:, first + b:last:2].unsqueeze(2).broadcast_to([P, heads, HD])
                        i = V.tensor_tensor(o[b].rearrange("p (h d) -> p h d", d=HD),
                                            ps[:, bank + b, 0:heads * HD].rearrange("p (h d) -> p h d", d=HD), r, ALU.mult)
                    if last < N:
                        i.then_inc(sem("sums_read"), 1)

                for n in range(N + 2):
                    if n < N:
                        take("item_scores")
                        link(V.reduce_max(mx[:, n:n + 1], ps[:, n % 2, 0:items[n]["n"]], AX_X))
                        V.tensor_scalar(nmx[:, n:n + 1], mx[:, n:n + 1], -SCALE, None, ALU.mult).then_inc(sem("item_max"), 1)
                    if 1 <= n <= N:
                        m = n - 1
                        take("item_turned")
                        if m >= 2:
                            dve.wait_ge(sem("item_pv"), base + m - 1)
                        w = items[m]["n"]
                        V.tensor_copy(probT[m % 2][:, 0:w], ps[:, 2 + m % 2, 0:w]).then_inc(sem("item_copied"), 1)
                    for y in ys:
                        if n == y[2] + 2 * y[3] + 1:
                            sums(*y)
                    beside.go(AT_ITEM)

            def rope(x, heads):
                c = cc("cos").rearrange("p (b n) -> p b n", b=NB)
                s = cc("sin").rearrange("p (b n) -> p b n", b=NB)
                for b in range(NB):
                    cb = c[:, b, :].unsqueeze(1).broadcast_to([P, heads, 8])
                    sn = s[:, b, :].unsqueeze(1).broadcast_to([P, heads, 8])
                    x1, x2 = x[b][:, :, 0:8], x[b][:, :, 8:16]
                    tmp = [work[:, 2048 + 64 * j:2048 + 64 * j + 8 * heads].rearrange("p (h n) -> p h n", n=8) for j in range(4)]
                    V.tensor_tensor(tmp[0], x1, cb, ALU.mult)
                    V.tensor_tensor(tmp[1], x2, sn, ALU.mult)
                    V.tensor_tensor(tmp[2], x2, cb, ALU.mult)
                    link(V.tensor_tensor(tmp[3], x1, sn, ALU.mult))
                    V.tensor_tensor(x1, tmp[0], tmp[1], ALU.subtract)
                    link(V.tensor_tensor(x2, tmp[2], tmp[3], ALU.add))

            def root_means(sizes):
                take("squares")
                for at, size in sizes:
                    i = V.tensor_scalar(ssq[:, at:at + 2], ssq[:, at:at + 2], 1.0 / size, EPS, ALU.mult, ALU.add)
                i.then_inc(sem("means"), 1)
                take("roots")
                link(V.reciprocal(ssq2[:, 0:2 * len(sizes)], ssq2[:, 0:2 * len(sizes)]))

            take("vectors_turned")
            for c, rows in enumerate(t["vector_chunks"]):
                i = V.tensor_copy(vec[:, c * P:c * P + rows], ps[:, c, 0:rows])
            i.then_inc(sem("vectors_copied"), 1)
            dve.wait_ge(sem("consts_in"), 16)

            pending = []

            def add_bias():
                if pending:
                    _, l, k0 = pending.pop()
                    take("row_turned")
                    r = VEC_ROWS["mod_b"] + l * NMOD * DC + k0
                    V.tensor_tensor(modc[:, l, k0:k0 + 4, :], ps[:, 7, 0:8].rearrange("p (k s) -> p k s", s=2),
                                    vec[:, r:r + 4].unsqueeze(2).broadcast_to([P, 4, 2]), ALU.add).then_inc(sem("beside_read"), 1)

            def beside_step(st):
                _, us, j, ev = st
                u = us[j][0]
                add_bias()
                split.upto(u + RING - 1)
                if j == 1 and ev[0] == "mod":
                    dve.wait_ge(s_used, u + 1)
                    V.tensor_copy(mrow[:], ps[0:4, 6, :]).then_inc(sem("row_copied"), 1)
                    pending.append(ev)

            beside = Beside(beside_step)

            def inverse_root(rstd, b):
                take("squares")
                V.tensor_scalar(ssq[:, b:b + 1], ssq[:, b:b + 1], 1.0 / D, EPS, ALU.mult, ALU.add).then_inc(sem("means"), 1)
                take("roots")
                return V.reciprocal(rstd[:, b:b + 1], ssq2[:, b:b + 1])

            for n, ph in enumerate(phases):
                kind = ph["kind"]
                split.upto(first_unit[n] + RING - 1)
                open_phase("dve", dve, n)
                if kind == "conditions":
                    take("c_hi")
                    link(V.tensor_tensor(csil[:], csil[:], CT[:, :, 0:2].bitcast(F32), ALU.subtract))
                    V.tensor_copy(CT[:, :, 2:4], csil[:])
                elif kind == "norm":
                    x, rstd = ph["x"], rst[:, 2 * ph["k"]:2 * ph["k"] + 2]
                    if ph["shift"] is not None:
                        for b in range(NB):
                            link(inverse_root(rstd, b))
                            V.tensor_scalar(xn[:, b, :], x[:, b, :], rstd[:, b:b + 1], None, ALU.mult).then_inc(sem("xn"), 1)

                    def low(b, half):
                        take("h_hi")
                        at = (slice(None), slice(4 * half, 4 * half + 4), slice(b * P, (b + 1) * P))
                        V.tensor_tensor(HTlo[at], hf[at], HThi[at].bitcast(F32), ALU.subtract).then_inc(sem("h_ready"), 1)

                    before_this = None
                    for b in range(NB):
                        for half in range(2):
                            take("h_turned")
                            p = ps[:, 4 + 2 * b + half, :].rearrange("p (k t) -> p k t", k=4)
                            o = hf[:, 4 * half:4 * half + 4, b * P:(b + 1) * P]
                            g = ph["gain"][:, 4 * half:4 * half + 4]
                            if ph["shift"] is None:
                                V.tensor_tensor(o, p, g.unsqueeze(2).broadcast_to([P, 4, P]), ALU.mult).then_inc(sem("h_gained"), 1)
                            else:
                                for k in range(4):
                                    i = V.tensor_scalar(o[:, k, :], p[:, k, :], g[:, k:k + 1],
                                                        ph["shift"][:, 4 * half + k:4 * half + k + 1], ALU.mult, ALU.add)
                                i.then_inc(sem("h_gained"), 1)
                            if before_this:
                                low(*before_this)
                            before_this = (b, half)
                    low(*before_this)
                    if ph["shift"] is None:
                        for b in range(NB):
                            i = inverse_root(rstd, b)
                        link(i)
                        V.tensor_copy(rstd[:], rstd[:]).then_inc(sem("rstd_ready"), 1)
                    split.upto(first_unit[n] + RING)
                elif kind == "final":
                    x = X
                    root_means([(0, D)])
                    take("g_in", 16 if ph["second"] else 32)
                    o = xn if ph["second"] else X
                    for b in range(NB):
                        i = V.scalar_tensor_tensor(out=o[:, b, :], in0=x[:, b, :], scalar=ssq2[:, b:b + 1], in1=gB,
                                                   op0=ALU.mult, op1=ALU.mult)
                        if not ph["second"]:
                            i.then_inc(sem("x_written"), 1)
                    if ph["second"]:
                        i.then_inc(sem("final_done"), 1)
                    else:
                        for l in range(DEPTH):
                            for s3 in range(3):
                                r = VEC_ROWS["norm_g"] + (l * 3 + s3) * DC
                                for st in range(2):
                                    m = modc[:, l, (3 * s3 + 1) * DC:(3 * s3 + 2) * DC, st]
                                    i = V.scalar_tensor_tensor(out=m, in0=m, scalar=1.0, in1=vec[:, r:r + DC], op0=ALU.add, op1=ALU.mult)
                        link(i)
                elif kind == "turn":
                    lo_of_turned(ph["src"])
                elif kind == "ffn":
                    split.upto(first_unit[n] + RING)
                    u0, n0 = ph["u0"], ph["f"] * GROUPS

                    def times_up(lead):
                        for b in range(NB):
                            dve.wait_ge(sem("ffn_silu"), lead * 2 + (2 * n0 + b + 1))
                            if ph["rstd"] is None:
                                i = V.tensor_tensor(av[:, b, :], sg[:, b, :], ps[:, b, GW:2 * GW], ALU.mult)
                            else:
                                i = V.scalar_tensor_tensor(out=av[:, b, :], in0=ps[:, b, GW:2 * GW], scalar=ph["rstd"][:, b:b + 1],
                                                           in1=sg[:, b, :], op0=ALU.mult, op1=ALU.mult)
                        i.then_inc(sem("ffn_act"), 1)

                    def act_lo(lead):
                        dve.wait_ge(sem("ffn_act_hi"), lead + (n0 + 1))
                        V.tensor_tensor(ATlo[:], ps[:, 2, :].rearrange("p (c t) -> p c t", c=2), AThi[:].bitcast(F32),
                                        ALU.subtract).then_inc(sem("ffn_act_lo"), 1)

                    def step(lead):
                        times_up(lead)
                        split_lo(dve, u0 + 3, lead)
                        act_lo(lead)
                        split_lo(dve, u0 + 4, lead)
                        split_lo(dve, u0 + 5, lead)

                    with dve.Fori(0, GROUPS - 1) as i:
                        step(i)
                    split.at = u0 + 3 * GROUPS
                    times_up(GROUPS - 1)
                    split.upto(split.at + 1)
                    act_lo(GROUPS - 1)
                    x, name = ph["x"], "c_written" if ph["x"] is C else "x_written"
                    if ph["gate"]:
                        take("gate_read", 2)
                    for b in range(NB):
                        if b == 0:
                            take("ffn_out")
                        else:
                            dve.wait_ge(s_used, u0 + 3 * GROUPS)
                        y = ps[:, 4 + 2 * b:6 + 2 * b, :].rearrange("p a n -> p (a n)")
                        if ph["gate"]:
                            link(V.tensor_tensor(xn[:, b, :], y, gateB, ALU.mult))
                            V.tensor_tensor(x[:, b, :], x[:, b, :], xn[:, b, :], ALU.add).then_inc(sem(name), 1)
                        else:
                            V.scalar_tensor_tensor(out=x[:, b, :], in0=y, scalar=0.5, in1=x[:, b, :],
                                                   op0=ALU.mult, op1=ALU.add).then_inc(sem(name), 1)
                elif kind == "beside":
                    beside.begin(ph["steps"])
                elif kind == "beside_end":
                    beside.go()
                    add_bias()
                elif kind == "dense":
                    if ph.get("gate"):
                        take("gate_read", 2)
                    split.upto(first_unit[n] + RING)

                    for g, (us, w, ev) in enumerate(ph["groups"]):
                        last = us[-1][0]
                        split.upto(last + RING)
                        P2 = 2 * (g % 2)
                        if ev[0] == "merge":
                            _, r, n0 = ev
                            dve.wait_ge(s_used, last + 1)
                            for b in range(NB):
                                o = C[:, b, n0:n0 + 512]
                                dst = o if r == 0 else work[:, b * 512:(b + 1) * 512]
                                i = V.tensor_tensor(dst, ps[:, P2 + b, :], GT[:, b, r * D + n0:r * D + n0 + 512], ALU.mult)
                            i.then_inc(sem("group_read"), 1)
                            if r:
                                dve.wait_ge(sem("group_read"), reads_before(n) + g + 1)
                                for b in range(NB):
                                    o = C[:, b, n0:n0 + 512]
                                    link(V.tensor_tensor(o, o, work[:, b * 512:(b + 1) * 512], ALU.add))
                        elif ev[0] in ("add", "addgate"):
                            n0 = ev[1]
                            dve.wait_ge(s_used, last + 1)
                            for b in range(NB):
                                o, p = X[:, b, n0:n0 + 512], ps[:, P2 + b, :]
                                if ev[0] == "add":
                                    i = V.tensor_tensor(o, p, o, ALU.add)
                                else:
                                    gated = work[:, (P2 + b) * 512:(P2 + b + 1) * 512]
                                    link(V.tensor_tensor(gated, p, gateB[:, n0:n0 + 512], ALU.mult))
                                    i = V.tensor_tensor(o, o, gated, ALU.add)
                                if g == len(ph["groups"]) - 1:
                                    i.then_inc(sem("x_written"), 1)
                elif kind == "prepare":
                    dve.wait_ge(sem("prep_in"), 64 * (ph["l"] + 1))
                    V.tensor_tensor(fl[:], PJ[:, :, FA:FA + HF], bfr.unsqueeze(1).broadcast_to([P, NB, HF]),
                                    ALU.add).then_inc(sem("forget_sum"), 1)
                    take("forget_ln")
                    V.scalar_tensor_tensor(out=fl2[:], in0=fl[:], scalar=0.0, in1=fl2[:], op0=ALU.min, op1=ALU.subtract)
                    root_means([(0, P), (2, HD)])
                    for b in range(NB):
                        V.scalar_tensor_tensor(out=PJ[:, b, CKV:CKV + P], in0=PJ[:, b, CKV:CKV + P], scalar=ssq2[:, b:b + 1],
                                               in1=work[:, 0:P], op0=ALU.mult, op1=ALU.mult)
                        link(V.scalar_tensor_tensor(out=PJ[:, b, KI:KI + HD], in0=PJ[:, b, KI:KI + HD],
                                                    scalar=ssq2[:, 2 + b:3 + b], in1=work[:, P:P + HD], op0=ALU.mult, op1=ALU.mult))
                    rope([PJ[:, b, QC:QC + HX * HD].rearrange("p (h d) -> p h d", d=HD) for b in range(NB)], HX)
                    rope([PJ[:, b, QI:QI + 5 * HD].rearrange("p (h d) -> p h d", d=HD) for b in range(NB)], 5)
                    beside.go(AT_PREPARE)
                elif kind == "latent":
                    take("latent_turned")
                    V.tensor_copy(work[:, 512:512 + SEQ], ps[:, 0, 0:SEQ])
                    V.tensor_copy(csum[:], ps[:, 3, 0:16].rearrange("p (b h) -> p b h", b=2)[:, :, 0:HF]).then_inc(sem("latent_copied"), 1)
                    beside.go(AT_LATENT)
                    take("latent_up")
                    V.tensor_scalar(csT, ps[0:HF, 2, 0:SEQ], -1.0 / SCALE, None, ALU.mult)
                    link(V.tensor_copy(KV, ps[:, 1, 0:SEQ].rearrange("p (b n) -> p b n", b=NB)))
                    rope([KV[:, b, 0:HD].rearrange("p (h d) -> p h d", d=HD) for b in range(NB)], 1)
                    dup = work[:, 0:512].rearrange("p (j b n) -> p j b n", j=2, b=NB)
                    for e in range(2):
                        V.tensor_copy(dup[:, 0, :, HD * e:HD * (e + 1)], KV[:, :, 0:HD])
                        V.tensor_copy(dup[:, 1, :, HD * e:HD * (e + 1)], PJ[:, :, KI:KI + HD])
                elif kind == "turn_heads":
                    copy_turned(head_chunks())
                    beside.go(AT_HEADS)
                elif kind == "index":
                    sc = work[:, 0:SEQ]
                    top = small[:, 448:456]
                    for b in range(NB):
                        w = (b + 1) * P
                        take("index_relu")
                        for h in range(HI):
                            at = 1024 + b * 1024 + (h % 2) * 512 + (h // 2) * SEQ
                            r = work[:, at:at + w]
                            link(V.scalar_tensor_tensor(out=sc[:, 0:w], in0=r, scalar=PJ[:, b, WI + h:WI + h + 1],
                                                        in1=cc(f"chunks{b}") if h == 0 else sc[:, 0:w], op0=ALU.mult, op1=ALU.add))
                        left = work[:, 512:512 + w]
                        for r8 in range(TOPK // 8):
                            src = sc[:, 0:w] if r8 == 0 else left
                            link(V.max(top, src))
                            link(V.match_replace(left, top, src, 2 * NEG))
                            if r8 % 2:
                                beside.go(AT_INDEX // 4)
                        V.tensor_scalar(score_add[:, b, 0:w], left, 1.5 * NEG, NEG, ALU.is_gt, ALU.mult)
                elif kind == "softmax":
                    run_items(softmax_items(), [([PJ[:, b, QA:QA + HF * HD] for b in range(NB)], 4, 0, HF),
                                                ([PJ[:, b, QC:QC + HX * HD] for b in range(NB)], 4, 2 * HF, HX)])
                elif kind == "near_turn":
                    copy_turned(near_chunks())
                    for g in range(4):
                        take("pooled")
                        V.tensor_copy(work[:, (g % 2) * SEQ:(g % 2 + 1) * SEQ], ps[:, 4 + g % 2, 0:SEQ]).then_inc(sem("pooled_copied"), 1)
                        take("pool_mapped")
                        V.tensor_scalar(work[:, 512:512 + SEQ], ps[:, 6 + g % 2, 0:SEQ], vcol("pool_scale", g), None,
                                        ALU.mult).then_inc(sem("pool_scaled"), 1)
                        take("pool_hi")
                        V.tensor_tensor(HTlo[:, 4 + g, :], work[:, 512:512 + SEQ], HThi[:, 4 + g, :].bitcast(F32),
                                        ALU.subtract).then_inc(sem("pool_split"), 1)
                elif kind == "near":
                    run_items(near_items(), [([work[:, 2048 + b * 512:2048 + (b + 1) * 512] for b in range(NB)], 4, 0, NA_H)])
                elif kind == "stick":
                    before = cc("before")

                    def logs(h):
                        take("stick_L")
                        z, L, l1, ls = ps[:, h % 2, 0:SBW], sb_L[h % 2], sb_l1[h % 2], sb_ls[h % 2]
                        link(V.tensor_scalar(ls, z, SCALE, 0.0, ALU.mult, ALU.min))
                        link(V.tensor_tensor(ls, ls, L, ALU.subtract))
                        link(V.scalar_tensor_tensor(out=l1, in0=z, scalar=-SCALE, in1=ls, op0=ALU.mult, op1=ALU.add))
                        V.tensor_tensor(l1[:, 0:P], l1[:, 0:P], before, ALU.mult)
                        V.tensor_tensor(l1[:, SEQ:SBW], l1[:, SEQ:SBW], before, ALU.mult).then_inc(sem("stick_l1"), 1)

                    def weight(h):
                        take("stick_acc")
                        if h >= 2:
                            take("stick_pv")
                        a = sb_a[h % 2]
                        V.tensor_tensor(a, ps[:, 2 + h % 2, 0:SBW], sb_ls[h % 2], ALU.add).then_inc(sem("stick_arg"), 1)
                        take("stick_exp")
                        V.tensor_tensor(a[:, 0:P], a[:, 0:P], before, ALU.mult)
                        V.tensor_tensor(a[:, SEQ:SBW], a[:, SEQ:SBW], before, ALU.mult).then_inc(sem("stick_a"), 1)

                    for h in range(HS + 1):
                        if h < HS:
                            logs(h)
                        if h >= 1:
                            weight(h - 1)
                        beside.go(AT_STICK)
                    take("stick_pv", 2)
                    beside.go(AT_STICK)
                    for b in range(NB):
                        V.tensor_copy(PJ[:, b, QB:QB + HS * HD], ps[:, 4 + b, 0:HS * HD])
                elif kind == "conv":
                    V.memset(work[:, 0:1], 0.0)
                    V.memset(work[:, 1 + SEQ:2 + SEQ], 0.0)
                    V.tensor_tensor(GT[:, :, 1024:2048], GT[:, :, 1024:2048], GT[:, :, 2048:3072], ALU.mult).then_inc(sem("conv_z"), 1)
                    for k in range(DC):
                        bank = k % 4
                        take("conv_turned")
                        w = [vcol("conv_w", j * DC + k) for j in range(3)]
                        y = work[:, 512:512 + SEQ]
                        link(V.tensor_copy(work[:, 1:1 + SEQ], ps[:, bank, 0:SEQ]))
                        link(V.tensor_scalar(y, work[:, 0:SEQ], w[0], None, ALU.mult))
                        link(V.scalar_tensor_tensor(out=y, in0=work[:, 1:1 + SEQ], scalar=w[1], in1=y, op0=ALU.mult, op1=ALU.add))
                        link(V.scalar_tensor_tensor(out=y, in0=work[:, 2:2 + SEQ], scalar=w[2], in1=y, op0=ALU.mult, op1=ALU.add))
                        h = work[:, 1024:1024 + SEQ]
                        V.tensor_tensor(h, ps[:, bank, SEQ:2 * SEQ], y, ALU.mult).then_inc(sem("conv_value"), 1)
                        take("conv_hi")
                        V.tensor_tensor(HTlo[:, k, :], h, HThi[:, k, :].bitcast(F32), ALU.subtract).then_inc(sem("conv_split"), 1)
                close_phase("dve", dve)


_ORDER = [
    "x", "w_ffn1_gu", "w_ffn1_down", "w_in", "b_forget", "g_kv_latent", "w_kv_up", "g_idx_k",
    "w_up_fox", "w_up_sb", "w_up_dsa", "w_out", "w_ffn2_gu", "w_ffn2_down", "g_final", "ctx_2",
    "mod_w_2", "ffn_w13_2", "ffn_w2_2", "even_w_in_2", "even_w_out_2",
    "na_rpb_2", "pool_w_2", "conv_w_in_2", "conv_w_out_2", "final_g_2",
    "g_ffn1", "g_mix", "g_ffn2", "c_2", "c_ctx_2", "mod_b_2", "norm_g_2", "pool_scale_2", "conv_w_2",
]
_VECTORS = [("g_ffn1", "g_ffn1"), ("g_mix", "g_mix"), ("g_ffn2", "g_ffn2"), ("c", "c_2"), ("c_ctx", "c_ctx_2"),
            ("norm_g", "norm_g_2"), ("pool_scale", "pool_scale_2"), ("conv_w", "conv_w_2"), ("mod_b", "mod_b_2")]


def place_vectors(t):
    t["vectors"], t["vector_chunks"] = [], []
    row = 0
    for name, key in _VECTORS:
        ap = t[key]
        while len(ap.shape) > 1:
            ap = ap.rearrange("a b -> (a b)") if len(ap.shape) == 2 else ap.rearrange("a b c -> (a b) c")
        ap = ap.rearrange("(r p) -> r p", p=P)
        VEC_ROWS[name] = row
        at, n = 0, ap.shape[0]
        while at < n:
            k = min(n - at, P - row % P)
            t["vectors"].append((ap[at:at + k], row // P, row % P))
            at += k
            row += k
    t["vector_chunks"] = [min(P, row - c * P) for c in range((row + P - 1) // P)]


def kernel(**inputs):
    import numpy as _np
    import concourse.bacc as _bacc
    from concourse import mybir as _mybir
    from concourse.bass_utils import run_bass_kernel_spmd as _run

    nc = _bacc.Bacc("TRN2", target_bir_lowering=False, num_devices=1)
    arrays, t = {}, {}
    inputs = {n: inputs[n] for n in _ORDER}
    inputs["consts"] = constants()
    inputs["pool_mats"] = pool_matrices()
    for name, a in inputs.items():
        a = _np.ascontiguousarray(a)
        arrays[f"in_{name}_dram"] = a
        t[name] = nc.dram_tensor(f"in_{name}_dram", a.shape, _mybir.dt.from_np(a.dtype), kind="ExternalInput").ap()
    place_vectors(t)
    out = nc.dram_tensor("out_0_dram", (1, SEQ, D), _mybir.dt.float32, kind="ExternalOutput").ap()
    program(nc, t, out)
    r = _run(nc, [arrays], core_ids=[0])
    return r.results[0]["out_0_dram"]
```

```python
from contextlib import ExitStack

import concourse.bass as bass
import numpy as np
from concourse import mybir

ALU = mybir.AluOpType
ACT = mybir.ActivationFunctionType
F32 = mybir.dt.float32
F32R = mybir.dt.float32r
AX_X = mybir.AxisListType.X

P = 128
SEQ = 256
NB = SEQ // P
D = 1024
DC = D // P
DFF = 2816
GW = 256
GROUPS = DFF // GW
DEPTH = 2
EPS = 1e-6
HD = 64
HF, HS, HX = 6, 5, 5
HI = 4
CHUNK = 64
TOPK = 64
NEG = -1e30
UNIT = 2048
RING = 3
QA, KA, VA, FA = 0, 384, 768, 1152
QB, KB, VB = 1158, 1478, 1798
QC, CKV, QI, KI, WI, GATES = 2118, 2438, 2566, 2822, 2886, 2890
NPJ = GATES
NA_H = 8
NMOD = 9
POOL_WORDS = 896
BESIDE = "GmmmGmmmmmmmmmmmmmmmGGGG"
SCALE = HD ** -0.5

CONSTS = {}


def constants():
    i = np.arange(P)
    parts = []

    def add(name, a):
        a = np.asarray(a, np.float32)
        full = np.zeros((P, a.shape[1]), np.float32)
        full[:a.shape[0]] = a
        at = sum(p.shape[1] for p in parts)
        CONSTS[name] = (at, a.shape[1])
        parts.append(full)

    add("ident", np.eye(P))
    add("upto", i[:, None] <= i[None, :])
    add("ones", np.ones((P, P)))
    add("causal", np.where(i[None, :] > i[:, None], NEG, 0.0))
    add("before", i[:, None] < i[None, :])
    add("after", i[:, None] > i[None, :])
    add("flip8", 8.0 * np.kron(np.eye(2), np.eye(64)[::-1]))
    k = np.arange(SEQ)
    for b in range(NB):
        q = b * P + i
        add(f"chunks{b}", np.where(k[None, :(b + 1) * P] // CHUNK > q[:, None] // CHUNK, NEG, 0.0))
    col = np.arange(64)
    start = np.clip(col - 8, 0, 64 - 16)
    ok = (col[None, :] >= start[:, None]) & (col[None, :] < start[:, None] + 16)
    add("window", np.tile(np.where(ok, 0.0, NEG), (2, 4)))
    pos = np.arange(SEQ, dtype=np.float32)
    inv = np.float32(500000.0) ** (-np.arange(0, 16, 2, dtype=np.float32) / np.float32(16))
    ang = (pos[:, None] * inv[None, :].astype(np.float32)).astype(np.float32)
    for name, f in (("cos", np.cos), ("sin", np.sin)):
        t = f(ang).astype(np.float32).reshape(NB, P, 8)
        add(name, t.transpose(1, 0, 2).reshape(P, NB * 8))
    fold = np.zeros((4, 2))
    fold[[0, 2], 0] = fold[[1, 3], 1] = 1.0
    add("fold", fold)
    return np.concatenate(parts, 1)


def pool_matrices():
    t = np.arange(SEQ)
    out = np.zeros((P, 4, NB, SEQ), np.float32)
    for g, w in enumerate((2, 4, 8, 16)):
        lo, hi = np.clip(t - w // 2, 0, SEQ), np.clip(t - w // 2 + w, 0, SEQ)
        s = np.arange(SEQ)
        a = ((s[:, None] >= lo[None]) & (s[:, None] < hi[None])) / (hi - lo)[None].astype(np.float64)
        a = (a - (s[:, None] == t[None])).astype(np.float32)
        out[:, g] = a.reshape(NB, P, SEQ).transpose(1, 0, 2)
    return out.reshape(P, -1)


VEC_ROWS = {}


def program(nc, t, out):
    with ExitStack() as ctx:
        made = {}

        def sem(name):
            if name not in made:
                made[name] = ctx.enter_context(nc.semaphore(name))
            return made[name]

        def sb(name, shape, dt=F32):
            return ctx.enter_context(nc.sbuf_tensor(name, shape, dt))

        ps = ctx.enter_context(nc.psum_tensor("ps", [P, 8, 512], F32))

        raw = sb("raw", [P, RING, UNIT])
        whi = sb("whi", [P, RING, UNIT], F32R)
        wlo = sb("wlo", [P, RING, UNIT], F32R)
        X = sb("X", [P, NB, D])
        C = sb("C", [P, NB, D])
        HThi = sb("HThi", [P, DC + 1, SEQ], F32R)
        HTlo = sb("HTlo", [P, DC + 1, SEQ], F32R)
        AT = [(sb(f"AThi{j}", [P, 2, SEQ], F32R), sb(f"ATlo{j}", [P, 2, SEQ], F32R)) for j in range(2)]
        NCST = t["consts"].shape[1]
        cst = sb("cst", [P, NCST])
        W0 = 5120
        arena = sb("arena", [P, W0 + 2 * NPJ + 6 * 1024])
        NV = P * len(t["vector_chunks"])
        vec = sb("vec", [P, NV])
        small = sb("small", [P, 512])
        work = sb("work", [P, 4096])
        modc = sb("modc", [P, DEPTH, NMOD * DC, 2])
        CT = sb("CT", [P, DC, 4], F32R)
        mrow = C[0:4, 0, 0:512]

        def cc(name, rows=P):
            at, n = CONSTS[name]
            return cst[0:rows, at:at + n]

        ident, ones = cc("ident"), cc("ones")
        xn = arena[:, 0:2048].rearrange("p (b d) -> p b d", b=NB)
        hf = arena[:, 2048:4096].rearrange("p (c t) -> p c t", c=DC)
        sg = arena[:, 4096:4608].rearrange("p (b f) -> p b f", b=NB)
        av = arena[:, 4608:5120].rearrange("p (b f) -> p b f", b=NB)
        PJ = arena[:, W0:W0 + 2 * NPJ].rearrange("p (b n) -> p b n", b=NB)
        GT = arena[:, W0 + 2 * NPJ:].rearrange("p (b n) -> p b n", b=NB)
        TT = arena[:, 0:20 * 256].rearrange("p (c t) -> p c t", c=20)

        def vcol(name, k=0):
            r = VEC_ROWS[name] + k
            return vec[:, r:r + 1]

        units = []

        pool_units = []

        def add_unit(*parts):
            units.append(parts)
            return len(units) - 1

        def kn1(w, row0, rows, n0, n):
            return w[row0:row0 + rows, n0:n0 + n]

        def kn(w, k0, nk, n0, n):
            return w[k0 * P:(k0 + nk) * P, n0:n0 + n].rearrange("(c p) n -> p c n", p=P)

        phases = []

        def phase(kind, **kw):
            phases.append(dict(kind=kind, **kw))

        x_writes = [0, 0]

        def ffn(w_gu, w_down, x, rstd=None, gate=None):
            u0 = len(units)
            units.extend([None] * (3 * GROUPS))
            phase("ffn", u0=u0, gu=w_gu, down=w_down, x=x, rstd=rstd, gate=gate,
                  f=sum(p["kind"] == "ffn" for p in phases))
            x_writes[x is C] += NB

        def norm(x, gain, shift=None):
            k = sum(p["kind"] == "norm" for p in phases)
            phase("norm", x=x, gain=gain, shift=shift, writes=x_writes[x is C], k=k)
            return rst[:, 2 * k:2 * k + 2] if shift is None else None

        def wide_group(w, n0, n, evac):
            us = []
            for k0 in (0, 4):
                u = add_unit((kn(w, k0, 4, n0, n), 0, 4, n, P))
                us.append((u, [(k0 + c, P, c * n) for c in range(4)]))
            return us, n, evac

        rst = small[:, 464:492]
        scrap = small[:, 492:493]
        eps = small[:, 493:494]
        unit_rms = [work[:, 3584 + b * P:3584 + (b + 1) * P] for b in range(NB)]

        def vcols(name, k):
            r = VEC_ROWS[name] + k
            return vec[:, r:r + DC]

        for l in range(DEPTH):
            rstd = norm(X, vcols("g_ffn1", l * DC))
            ffn(t["w_ffn1_gu"][l], t["w_ffn1_down"][l], X, rstd)
            rstd = norm(X, vcols("g_mix", l * DC))
            w = t["w_in"][l]
            gs = []
            for n0 in range(0, NPJ, 512):
                n = min(512, NPJ - n0)
                gs.append(wide_group(w, n0, n, ("copy", [PJ[:, b, n0:n0 + n] for b in range(NB)])))
            phase("dense", groups=gs, rstd=rstd, after_norm=True, conditions=l == 0)
            steps = []
            at = dict(G=0, m=0)
            for what in BESIDE:
                r = at[what]
                at[what] += 1
                if what == "G":
                    us, n, ev = wide_group(w, GATES + r * 512, 512,
                                           ("sigmoid", [GT[:, b, r * 512:(r + 1) * 512] for b in range(NB)], rstd))
                else:
                    us, n, ev = wide_group(t["mod_w_2"][l], r * 512, 512, ("mod", l, r * 512 // P))
                pool_units.extend(u for u, _ in us)
                steps += [("unit", us, j, ev) for j in range(2)]
            phase("beside", steps=steps)
            for kind in ("prepare", "latent", "turn_heads", "index", "softmax", "stick"):
                phase(kind, l=l)
            phase("beside_end")
            phase("turn", src=[[PJ[:, b, at + c:at + min(c + P, n)] for b in range(NB)]
                               for at, n in ((QA, HF * HD), (QB, HS * HD), (QC, HX * HD)) for c in range(0, n, P)])
            gs = []
            for n0 in (0, 512):
                for r, (name, rows) in enumerate((("w_up_fox", HF * HD), ("w_up_sb", HS * HD), ("w_up_dsa", HX * HD))):
                    w = t[name][l]
                    full = rows // P
                    parts = [(kn(w, 0, full, n0, 512), 0, full, 512, P)]
                    ks = [(3 * r + c, P, c * 512) for c in range(full)]
                    if rows % P:
                        parts.append((kn1(w, full * P, rows % P, n0, 512), full * 512, 1, 512, rows % P))
                        ks.append((3 * r + full, rows % P, full * 512))
                    gs.append(([(add_unit(*parts), ks)], 512, ("merge", r, n0)))
            phase("dense", groups=gs)
            phase("turn", src=[[C[:, b, k * P:(k + 1) * P] for b in range(NB)] for k in range(DC)])
            phase("dense", groups=[wide_group(t["w_out"][l], n0, 512, ("add", n0)) for n0 in (0, 512)])
            x_writes[0] += NB
            rstd = norm(X, vcols("g_ffn2", l * DC))
            ffn(t["w_ffn2_gu"][l], t["w_ffn2_down"][l], X, rstd)
        phases[-1]["gains"] = True
        phase("final", second=False, x=X, writes=x_writes[0])
        x_writes[0] += NB

        def mcols(l, j, s):
            return modc[:, l, j * DC:(j + 1) * DC, s]

        for l in range(DEPTH):
            norm(X, mcols(l, 1, 0), mcols(l, 0, 0))
            ffn(t["ffn_w13_2"][l, 0], t["ffn_w2_2"][l, 0], X, gate=(2, l, 0))
            if l == 0:
                norm(C, mcols(l, 1, 1), mcols(l, 0, 1))
                ffn(t["ffn_w13_2"][l, 0], t["ffn_w2_2"][l, 0], C, gate=(2, l, 1))
            norm(X, mcols(l, 4, 0), mcols(l, 3, 0))
            if l == 0:
                w = t["even_w_in_2"][0]
                phase("dense", after_norm=True,
                      groups=[wide_group(w, n0, 512, ("copy", [PJ[:, b, n0:n0 + 512] for b in range(NB)]))
                              for n0 in range(0, 2048, 512)])
                norm(C, mcols(l, 4, 1), mcols(l, 3, 1))
                phase("dense", after_norm=True,
                      groups=[wide_group(w, n0, 512, ("copy", [GT[:, b, n0 - 512:n0] for b in range(NB)]))
                              for n0 in (512, 1024)])
                phase("near_turn")
                phase("near")
                phase("turn", src=[[work[:, 2048 + b * 512 + k * P:2048 + b * 512 + (k + 1) * P] for b in range(NB)]
                                   for k in range(4)])
                wo = t["even_w_out_2"][0]
            else:
                w = t["conv_w_in_2"][0]
                phase("dense", after_norm=True,
                      groups=[wide_group(w, n0, 512, ("copy", [GT[:, b, n0:n0 + 512] for b in range(NB)]))
                              for n0 in range(0, 3072, 512)])
                phase("conv")
                wo = t["conv_w_out_2"][0]
            phase("dense", gate=(5, l, 0), groups=[wide_group(wo, n0, 512, ("addgate", n0)) for n0 in (0, 512)])
            x_writes[0] += NB
            norm(X, mcols(l, 7, 0), mcols(l, 6, 0))
            ffn(t["ffn_w13_2"][l, 1], t["ffn_w2_2"][l, 1], X, gate=(8, l, 0))
        phase("final", second=True, x=X, writes=x_writes[0])

        NU = len(units)
        s_raw = [sem(f"raw_landed{r}") for r in range(RING)]
        s_hi, s_used = sem("unit_hi"), sem("unit_used")
        s_lo, s_lo_pool = sem("unit_lo"), sem("unit_lo_by_pool")

        first_unit, u = [], 0
        for n, ph in enumerate(phases):
            first_unit.append(u)
            if ph["kind"] == "beside":
                steps = ph["steps"]
            if ph["kind"] == "beside_end":
                ph["steps"] = steps
                u = steps[-1][1][-1][0] + 1
                continue
            if ph["kind"] == "ffn":
                u = ph["u0"] + 3 * GROUPS
            elif "groups" in ph:
                u = ph["groups"][-1][0][-1][0] + 1
        def close_phase(e, eng):
            eng.drain().then_inc(sem(f"phases_{e}"), 1)

        def open_phase(e, eng, n):
            if n and not phases[n]["kind"] in ("norm", "ffn", "final") and not phases[n].get("after_norm"):
                for o in ("pe", "act", "dve"):
                    if o != e:
                        eng.wait_ge(sem(f"phases_{o}"), n)

        def taker(eng):
            seen = {}

            def take(name, n=1):
                seen[name] = seen.get(name, 0) + n
                eng.wait_ge(sem(name), seen[name])
            return take

        def turned_copier(eng, take, copy, read):
            def copy_turned(src, odd):
                behind = 0
                for m in range(0, len(src), 2):
                    behind += 1
                    if (m // 2) % 2 == odd:
                        take("heads_turned", behind)
                        behind = 0
                        for j, blocks in enumerate(src[m:m + 2]):
                            rows = blocks[0].shape[-1]
                            i = copy(TT[0:rows, m + j, :], ps[0:rows, (m // 2) % 4, j * SEQ:(j + 1) * SEQ])
                        i.then_inc(sem(read), 1)
                if behind:
                    take("heads_turned", behind)
            return copy_turned

        def linker(eng, name):
            n = [0]

            def link(i):
                n[0] += 1
                i.then_inc(sem(name), 1)
                eng.wait_ge(sem(name), n[0])
            return link

        def regions(u):
            return [(P, 0, UNIT)] if units[u] is None else [(rows, at, at + c * n) for _, at, c, n, rows in units[u]]

        def raw_count(u):
            return sum(2 if units[v] is None else len(units[v]) for v in range(u % RING, u + 1, RING))

        def reads_before(n):
            return sum(len(p["groups"]) for p in phases[:n]
                       if p["kind"] == "dense" and p["groups"][0][2][0] not in ("add", "addgate"))

        def split_hi(act, u, lead=0):
            r = u % RING
            act.wait_ge(s_raw[r], lead * 32 + 16 * raw_count(u))
            if u >= RING:
                act.wait_ge(s_used, lead * RING + (u - RING + 1))
            for rows, a, b in regions(u):
                i = nc.scalar.activation(whi[0:rows, r, a:b], raw[0:rows, r, a:b], ACT.Copy)
            i.then_inc(s_hi, 1)

        def wait_lo(eng, u, lead=0):
            eng.wait_ge(s_lo, lead * RING + (u + 1))
            if u in pool_units:
                eng.wait_ge(s_lo_pool, pool_units.index(u) + 1)

        def split_lo(dve, u, lead=0):
            r = u % RING
            dve.wait_ge(s_hi, lead * RING + (u + 1))
            for rows, a, b in [(P, 0, UNIT - POOL_WORDS)] if u in pool_units else regions(u):
                i = nc.vector.tensor_tensor(wlo[0:rows, r, a:b], raw[0:rows, r, a:b],
                                            whi[0:rows, r, a:b].bitcast(F32), ALU.subtract)
            i.then_inc(s_lo, 1)

        class Splitter:
            def __init__(self, eng, fn):
                self.eng, self.fn, self.at = eng, fn, 0

            def upto(self, n):
                while self.at < min(n, NU):
                    self.fn(self.eng, self.at)
                    self.at += 1

        AT_PREPARE, AT_LATENT, AT_HEADS, AT_INDEX, AT_ITEM, AT_STICK = 4, 2, 3, 4, 1, 1

        class Beside:
            def __init__(self, step):
                self.step, self.steps, self.at = step, [], 0

            def begin(self, steps):
                self.steps, self.at = steps, 0

            def go(self, n=None):
                n = len(self.steps) - self.at if n is None else n
                for st in self.steps[self.at:self.at + n]:
                    self.step(st)
                self.at = min(self.at + n, len(self.steps))

        def written(eng, ph, b):
            if ph["writes"]:
                eng.wait_ge(sem("c_written" if ph["x"] is C else "x_written"), ph["writes"] - NB + b + 1)
            elif ph["x"] is C:
                eng.wait_ge(sem("g_in"), 32)
            else:
                eng.wait_ge(sem("x_in"), 16)

        def follows(n):
            nx = phases[n + 1] if n + 1 < len(phases) else dict(kind=None)
            if n < 0:
                return None
            ph = phases[n]
            own = ph["x"] if ph["kind"] == "ffn" else X if ph["kind"] == "dense" and ph["groups"][0][2][0] in ("add", "addgate") else None
            return nx if nx["kind"] == "norm" and nx["x"] is own else None

        KV = small[:, 0:256].rearrange("p (b n) -> p b n", b=NB)
        mx, nmx, rsum = small[:, 256:288], small[:, 288:320], small[:, 320:352]
        rinv = small[:, 352:384]
        ssq, ssq2 = small[:, 384:392], small[:, 392:400]
        fl = small[:, 400:412].rearrange("p (b h) -> p b h", b=NB)
        fl2 = small[:, 412:424].rearrange("p (b h) -> p b h", b=NB)
        bfr = small[:, 424:430]
        g_latent, g_index, w_kv = work[:, 2304:2304 + P], work[:, 2432:2432 + HD], work[:, 2560:2560 + P]
        csum = small[:, 436:448].rearrange("p (b h) -> p b h", b=NB)
        score_add = work[:, 3584:4096].rearrange("p (b k) -> p b k", b=NB)
        csT = work[0:HF, 3328:3584]
        prob = [work[:, 0:512], work[:, 512:1024]]
        probT = [work[:, 1024:1536], work[:, 1536:2048]]
        near_bias = [GT.rearrange("p b n -> p (b n)")[:, (1024 if n < 8 else 4096) + (n % 8) * 256:][:, 0:256]
                     for n in range(16)]
        poolA = arena[:, 3072:5120].rearrange("p (g s t) -> p g s t", g=4, s=NB)
        poolW = work[:, 3072:3584].rearrange("p (g f) -> p g f", g=4)

        def rows_of(h):
            return slice(64 * (h % 2), 64 * (h % 2) + 64)

        def softmax_items():
            items = []
            for h in range(HF):
                for b in range(NB):
                    n = (b + 1) * P
                    adds = [(ident, cc("causal"), b * P, P),
                            (ident[0:HF, h:h + 1].broadcast_to([HF, P]), csT[:, 0:n], 0, n)]
                    items.append(dict(q=TT[rows_of(h), h // 2, b * P:(b + 1) * P],
                                      k=[(TT[rows_of(h), 3 + h // 2, 0:n], 0, n)], adds=adds, n=n,
                                      v=[PJ[:, c, VA + HD * h:VA + HD * (h + 1)] for c in range(b + 1)],
                                      y=ps[:, 4 + b, HD * h:HD * (h + 1)]))
            for h in range(HX):
                for b in range(NB):
                    n = (b + 1) * P
                    items.append(dict(q=TT[rows_of(h), 12 + h // 2, b * P:(b + 1) * P],
                                      k=[(TT[rows_of(h), 15, 0:n], 0, n)],
                                      adds=[(ident, score_add[:, b, 0:n], 0, n)], n=n,
                                      v=[KV[:, c, HD:2 * HD] for c in range(b + 1)],
                                      y=ps[:, 4 + b, HD * h:HD * (h + 1)]))
            return items

        def near_items():
            items = []
            for h in range(NA_H):
                for b in range(NB):
                    items.append(dict(q=TT[rows_of(h), h // 2, b * P:(b + 1) * P],
                                      k=[(TT[rows_of(h), 4 + h // 2, :], 0, SEQ), (TT[rows_of(h), 8 + h // 2, :], SEQ, SEQ)],
                                      adds=[(cc("flip8"), near_bias[2 * h + b], 0, SEQ), (ident, cc("window"), 0, SEQ)],
                                      n=2 * SEQ,
                                      v=[PJ[:, c, 1024 + HD * h:1024 + HD * (h + 1)] for c in range(NB)]
                                      + [GT[:, c, 512 + HD * h:512 + HD * (h + 1)] for c in range(NB)],
                                      y=ps[:, 4 + b, HD * h:HD * (h + 1)]))
            return items

        def head_chunks():
            out = []
            for at, n in ((QA, 384), (KA, 384), (QB, 320), (KB, 320), (QC, 320)):
                for c in range(0, n, P):
                    out.append([PJ[:, b, at + c:at + min(c + P, n)] for b in range(NB)])
            dup = work[:, 0:512].rearrange("p (j b n) -> p j b n", j=2, b=NB)
            out.append([dup[:, 0, b, :] for b in range(NB)])
            out += [[PJ[:, b, QI + c:QI + c + P] for b in range(NB)] for c in (0, P)]
            out.append([dup[:, 1, b, :] for b in range(NB)])
            return out

        def near_chunks():
            out = [[PJ[:, b, c:c + P] for b in range(NB)] for c in range(0, 1024, P)]
            return out + [[GT[:, b, c:c + P] for b in range(NB)] for c in range(0, 512, P)]

        SBW = SEQ + P
        sb_abs = work[:, 0:SBW]
        sb_L = [work[:, SBW * (1 + j):SBW * (2 + j)] for j in range(2)]
        sb_l1 = [work[:, SBW * (3 + j):SBW * (4 + j)] for j in range(2)]
        sb_ls = [work[:, SBW * (5 + j):SBW * (6 + j)] for j in range(2)]
        sb_a = [work[:, SBW * (7 + j):SBW * (8 + j)] for j in range(2)]
        pool_out = [work[:, 512 + j * SEQ:512 + (j + 1) * SEQ] for j in range(2)]
        conv_in = [work[:, j * 512:j * 512 + SEQ + 2] for j in range(2)]
        conv_y = [work[:, 1024 + j * SEQ:1024 + (j + 1) * SEQ] for j in range(2)]
        conv_out = [work[:, 1536 + j * SEQ:1536 + (j + 1) * SEQ] for j in range(2)]
        gateB = GT.rearrange("p b n -> p (b n)")[:, 5120:6144]
        gB = GT.rearrange("p b n -> p (b n)")[:, 4096:5120]
        csil = small[:, 448:464].rearrange("p (k s) -> p k s", s=2)

        block = ctx.enter_context(nc.Block())

        @block.sync
        def _(sp):
            sp.dma_start(cst[:], t["consts"]).then_inc(sem("consts_in"), 16)
            sp.dma_start(X[:], t["x"][0].rearrange("(b p) d -> p b d", p=P)).then_inc(sem("x_in"), 16)
            for src, chunk, row in t["vectors"]:
                sp.dma_start(work[row:row + src.shape[0], chunk * P:(chunk + 1) * P], src).then_inc(sem("vectors_in"), 16)

            def free(u, lead=0):
                if u >= RING or not isinstance(lead, int):
                    wait_lo(sp, u - RING, lead)

            def load(u):
                free(u)
                for src, at, c, n, rows in units[u]:
                    dst = raw[0:rows, u % RING, at:at + c * n]
                    if c > 1:
                        dst = dst.rearrange("p (c n) -> p c n", c=c)
                    sp.dma_start(dst, src).then_inc(s_raw[u % RING], 16)

            def load_gu(ph, u, h, g0, lead=0):
                free(u, lead)
                src = ph["gu"].rearrange("(c p) (s n) -> p c s n", p=P, s=2)
                dst = raw[:, u % RING, :].rearrange("p (c s n) -> p c s n", c=4, s=2)
                for s in range(2):
                    sp.dma_start(dst[:, :, s, :], src[:, 4 * h:4 * h + 4, s, bass.ds(g0, GW)]).then_inc(s_raw[u % RING], 16)

            def load_down(ph, u, r0, lead=0):
                free(u, lead)
                for c in range(2):
                    sp.dma_start(raw[:, u % RING, c * D:(c + 1) * D],
                                 ph["down"][bass.ds(r0 + c * P, P), :]).then_inc(s_raw[u % RING], 16)

            for ph in phases:
                if ph["kind"] == "ffn":
                    u0 = ph["u0"]
                    load_gu(ph, u0, 0, 0)
                    load_gu(ph, u0 + 1, 1, 0)

                    def load_step(i):
                        load_gu(ph, u0 + 2, 0, i * GW + GW, i)
                        load_gu(ph, u0 + 3, 1, i * GW + GW, i)
                        load_down(ph, u0 + 4, i * GW, i)

                    load_step(0)
                    with sp.Fori(1, GROUPS - 1) as i:
                        load_step(i)
                    load_down(ph, u0 + 3 * GROUPS - 1, DFF - GW)
                elif "groups" in ph:
                    for us, _, _ in ph["groups"]:
                        for u, _ in us:
                            load(u)
                elif ph["kind"] == "beside":
                    for _, us, j, _ in ph["steps"]:
                        load(us[j][0])
            sp.wait_ge(sem("out_written"), 16 * NB)

        @block.gpsimd
        def _(pool):
            def bcast(src):
                return src.partition_broadcast(P)

            def through(n):
                for o in ("pe", "act", "dve"):
                    pool.wait_ge(sem(f"phases_{o}"), n)

            for n, ph in enumerate(phases):
                if ph["kind"] == "beside_end":
                    for _, us, j, _ in ph["steps"]:
                        u = us[j][0]
                        pool.wait_ge(s_hi, u + 1)
                        at = (slice(None), u % RING, slice(UNIT - POOL_WORDS, UNIT))
                        nc.gpsimd.tensor_tensor(wlo[at], raw[at], whi[at].bitcast(F32), ALU.subtract).then_inc(s_lo_pool, 1)
                elif ph["kind"] == "prepare":
                    l = ph["l"]
                    through(n - 3)
                    pool.dma_start(bfr, bcast(t["b_forget"][l])).then_inc(sem("prep_in"), 16)
                    pool.dma_start(g_latent, bcast(t["g_kv_latent"][l])).then_inc(sem("prep_in"), 16)
                    pool.dma_start(g_index, bcast(t["g_idx_k"][l])).then_inc(sem("prep_in"), 16)
                    pool.dma_start(w_kv, t["w_kv_up"][l]).then_inc(sem("prep_in"), 16)
                elif ph["kind"] == "final":
                    through(n - 1)
                    pool.dma_start(gB, bcast(t["final_g_2" if ph["second"] else "g_final"])).then_inc(sem("g_in"), 16)
                    if not ph["second"]:
                        pool.dma_start(C[:], t["ctx_2"][0].rearrange("(b p) d -> p b d", p=P)).then_inc(sem("g_in"), 16)
                elif ph["kind"] == "near_turn":
                    through(n - 3)
                    rpb = t["na_rpb_2"]
                    for m in range(16):
                        h, b = m // 2, m % 2
                        for r in range(2):
                            rq = 2 * b + r
                            at = (h * 15 + 7 - rq) * 31 + 15 - 63
                            src = bass.AP(rpb.tensor, at, [[1, 64], [31, 4], [1, 64]])
                            pool.dma_start(near_bias[m][64 * r:64 * r + 64, :].rearrange("p (k c) -> p k c", k=4),
                                           src).then_inc(sem("near_in"), 16)
                    through(n - 1)
                    pool.dma_start(poolA.rearrange("p g s t -> p (g s t)"), t["pool_mats"]).then_inc(sem("pool_in"), 16)
                    pool.dma_start(poolW, t["pool_w_2"][0].rearrange("g p f -> p g f")).then_inc(sem("pool_in"), 16)

        @block.tensor
        def _(pe):
            take = taker(pe)

            def mm(o, lhsT, rhs, first=True, last=True):
                return nc.tensor.matmul(o, lhsT, rhs, start=first, stop=last)

            def three(o, lh, ll, wh, wl, first, last):
                mm(o, lh, wh, first, False)
                mm(o, ll, wh, False, False)
                return mm(o, lh, wl, False, last)

            def turn(chunks, done, freed, first=0):
                for m, blocks in enumerate(chunks):
                    bank = (m // 2) % 4
                    if m % 2 == 0 and m // 2 >= 4:
                        take(freed[(m // 2) % 2])
                    for b, src in enumerate(blocks):
                        w = src.shape[-1]
                        i = nc.tensor.transpose(ps[0:w, bank, (m % 2) * SEQ + b * P:(m % 2) * SEQ + (b + 1) * P], src, ident)
                    if m % 2 or m == len(chunks) - 1:
                        i.then_inc(sem(done), 1)
                pairs = (len(chunks) + 1) // 2
                for m in range(max(0, pairs - 4), pairs):
                    take(freed[m % 2])

            owed = []
            row = []

            def settle():
                while owed:
                    owed.pop()
                    take("beside_read")

            def turn_row():
                if row:
                    row.pop()
                    settle()
                    take("row_copied")
                    for j in range(4):
                        i = mm(ps[:, 7, 2 * j:2 * j + 2], mrow[:, j * P:(j + 1) * P], cc("fold", 4))
                    i.then_inc(sem("row_turned"), 1)
                    owed.append(1)

            def beside_step(st):
                _, us, j, ev = st
                turn_row()
                u, ks = us[j]
                r = u % RING
                if j == 0 and (ev[0] != "mod" or not last_mod):
                    settle()
                last_mod[:] = [1] if ev[0] == "mod" else []
                wait_lo(pe, u)
                for kc, rows, at in ks:
                    first, last = kc == 0, kc == DC - 1
                    wh, wl = whi[:, r, at:at + 512], wlo[:, r, at:at + 512]
                    if ev[0] == "mod":
                        mm(ps[0:4, 6, :], CT[:, kc, :], wh, first, False)
                        i = mm(ps[0:4, 6, :], CT[:, kc, :], wl, False, last)
                    else:
                        for b in range(NB):
                            i = three(ps[:, 6 + b, :], HThi[:, kc, b * P:(b + 1) * P],
                                      HTlo[:, kc, b * P:(b + 1) * P], wh, wl, first, last)
                i.then_inc(s_used, 1)
                if j == 1:
                    (row if ev[0] == "mod" else owed).append(1)

            last_mod = []
            beside = Beside(beside_step)

            def run_items(items, places=()):
                N = len(items)
                for n in range(N + 2):
                    if n < N:
                        it = items[n]
                        S = ps[:, n % 2, :]
                        for m, (k, at, w) in enumerate(it["k"]):
                            mine = [a for a in it["adds"] if at <= a[2] < at + w]
                            i = mm(S[:, at:at + w], it["q"], k, True, not mine)
                            for j, (lh, rh, o, ow) in enumerate(mine):
                                i = nc.tensor.matmul(S[:, o:o + ow], lh, rh, start=False, stop=j == len(mine) - 1)
                        i.then_inc(sem("item_scores"), 1)
                    if 1 <= n <= N:
                        it = items[n - 1]
                        take("item_exp")
                        T = ps[:, 2 + (n - 1) % 2, :]
                        for c in range(it["n"] // P):
                            i = nc.tensor.transpose(T[:, c * P:(c + 1) * P], prob[(n - 1) % 2][:, c * P:(c + 1) * P], ident)
                        i.then_inc(sem("item_turned"), 1)
                    if n >= 2:
                        it = items[n - 2]
                        take("item_copied")
                        if n - 2 in places:
                            take("sums_read")
                        nk = it["n"] // P
                        for c in range(nk):
                            i = mm(it["y"], probT[n % 2][:, c * P:(c + 1) * P], it["v"][c], c == 0, c == nk - 1)
                        i.then_inc(sem("item_pv"), 1)
                    beside.go(AT_ITEM)

            def gate_rows(ph, half, bank):
                j, l, st = ph["gate"]
                for k in range(4):
                    i = mm(ps[:, bank, k * P:(k + 1) * P],
                           modc[:, l, j * DC + half * 4 + k, st:st + 1].broadcast_to([P, P]), ident)
                i.then_inc(sem("gate_turned"), 1)

            def dense(ph, nx, nb):
                gs = ph["groups"]
                waits = gs[0][2][0] not in ("add", "addgate")
                if ph.get("gate"):
                    for half in range(2):
                        gate_rows(ph, half, 4 + half)
                for g, (us, w, ev) in enumerate(gs):
                    if g >= 2 and waits:
                        take("group_read")
                    bank = 2 * (g % 2)

                    def part(u, ks, blocks):
                        wait_lo(pe, u)
                        r = u % RING
                        for kc, rows, at in ks:
                            first = u == us[0][0] and kc == ks[0][0]
                            last = u == us[-1][0] and kc == ks[-1][0]
                            for b in blocks:
                                i = three(ps[:, bank + b, 0:w], HThi[0:rows, kc, b * P:(b + 1) * P],
                                          HTlo[0:rows, kc, b * P:(b + 1) * P],
                                          whi[0:rows, r, at:at + w], wlo[0:rows, r, at:at + w], first, last)
                        return i

                    if g == 0 and ph.get("after_norm"):
                        for b in range(NB):
                            for u, ks in us:
                                take("h_ready")
                                i = part(u, ks, [b])
                                if b == NB - 1:
                                    i.then_inc(s_used, 1)
                                elif nb and u == us[0][0]:
                                    norm_turn(nb, 1)
                    elif nx and g == len(gs) - 1:
                        for u, ks in us:
                            i = part(u, ks, [0])
                        i.then_inc(sem("block_out"), 1)
                        (u, ks), (u2, ks2) = us
                        part(u, ks, [1]).then_inc(s_used, 1)
                        if nx["shift"] is None:
                            norm_turn(nx, 0)
                        part(u2, ks2, [1]).then_inc(s_used, 1)
                    else:
                        for u, ks in us:
                            part(u, ks, range(NB)).then_inc(s_used, 1)
                if waits:
                    for _ in range(min(2, len(gs))):
                        take("group_read")

            def norm_turn(ph, b):
                plain = ph["shift"] is None
                if plain:
                    written(pe, ph, b)
                else:
                    take("rms_ready")
                for half in range(2):
                    for k in range(4):
                        o = ps[:, 4 + 2 * b + half, k * P:(k + 1) * P]
                        src = ph["x"][:, b, (4 * half + k) * P:(4 * half + k + 1) * P]
                        i = nc.tensor.transpose(o, src, ident) if plain else mm(o, src, unit_rms[b])
                    i.then_inc(sem("h_turned" if plain or half else "h_scaled"), 1)

            def ffn(ph, nx, nb):
                u0, f = ph["u0"], ph["f"]
                n0 = f * GROUPS

                def gu(u, k0, lead, blocks=range(NB)):
                    wait_lo(pe, u, lead)
                    for c in range(4):
                        for b in blocks:
                            i = three(ps[:, b, :], HThi[:, k0 + c, b * P:(b + 1) * P], HTlo[:, k0 + c, b * P:(b + 1) * P],
                                      whi[:, u % RING, c * 512:(c + 1) * 512], wlo[:, u % RING, c * 512:(c + 1) * 512],
                                      k0 + c == 0, k0 + c == DC - 1)
                    if NB - 1 in blocks:
                        i.then_inc(s_used, 1)

                def turn_act(lead, ahead=False):
                    pe.wait_ge(sem("ffn_act"), lead + (n0 + 1))
                    if not ahead:
                        if n0:
                            pe.wait_ge(sem("ffn_act_lo"), lead + n0)
                        elif not isinstance(lead, int):
                            pe.wait_ge(sem("ffn_act_lo"), lead)
                    for c in range(2):
                        for b in range(NB):
                            i = nc.tensor.transpose(ps[:, 2, c * SEQ + b * P:c * SEQ + (b + 1) * P], av[:, b, c * P:(c + 1) * P], ident)
                    i.then_inc(sem("ffn_turned"), 1)

                def down(u, b, c, own, first=False, last=False):
                    for h in range(2):
                        at = c * D + h * 512
                        i = three(ps[:, 4 + 2 * b + h, :], AT[own][0][:, c, b * P:(b + 1) * P], AT[own][1][:, c, b * P:(b + 1) * P],
                                  whi[:, u % RING, at:at + 512], wlo[:, u % RING, at:at + 512], first, last)
                    return i

                def down_ready(u, lead, g):
                    wait_lo(pe, u, lead)
                    pe.wait_ge(sem("ffn_act_lo"), g + 1)

                def step(lead, first):
                    pe.wait_ge(sem("ffn_act"), lead + (n0 + 1))
                    gu(u0 + 2, 0, lead)
                    gu(u0 + 3, 4, lead)
                    down_ready(u0 + 4, lead, lead + n0)
                    for c in range(2):
                        for b in range(NB):
                            i = down(u0 + 4, b, c, 0, first and c == 0)
                    i.then_inc(s_used, 1)
                    turn_act(lead + 1)

                for b in range(NB):
                    take("h_ready")
                    gu(u0, 0, 0, [b])
                    if b == 0 and nb:
                        norm_turn(nb, 1)
                    take("h_ready")
                    gu(u0 + 1, 4, 0, [b])
                turn_act(0)
                if ph["gate"]:
                    gate_rows(ph, 0, 3)
                step(0, True)
                if ph["gate"]:
                    take("gate_read")
                    gate_rows(ph, 1, 3)
                with pe.Fori(1, GROUPS - 2) as i:
                    step(i, False)
                L, d9, d10 = GROUPS - 2, u0 + 3 * GROUPS - 2, u0 + 3 * GROUPS - 1
                pe.wait_ge(sem("ffn_act"), L + n0 + 1)
                gu(u0 + 2, 0, L)
                gu(u0 + 3, 4, L)
                down_ready(d9, 0, L + n0)
                down(d9, 0, 0, 0)
                down(d9, 0, 1, 0)
                turn_act(L + 1, ahead=True)
                down(d9, 1, 0, 0)
                down_ready(d10, 0, L + 1 + n0)
                down(d10, 0, 0, 1)
                down(d10, 0, 1, 1, last=True).then_inc(sem("ffn_out"), 1)
                down(d9, 1, 1, 0).then_inc(s_used, 1)
                if nx and nx["shift"] is None:
                    norm_turn(nx, 0)
                down(d10, 1, 0, 1)
                down(d10, 1, 1, 1, last=True).then_inc(s_used, 1)
                if ph["gate"]:
                    take("gate_read")

            pe.wait_ge(sem("consts_in"), 16)
            pe.wait_ge(sem("vectors_in"), 16 * len(t["vectors"]))
            for c, rows in enumerate(t["vector_chunks"]):
                i = nc.tensor.transpose(ps[:, c, 0:rows], work[0:rows, c * P:(c + 1) * P], ident[0:rows, 0:rows])
            i.then_inc(sem("vectors_turned"), 1)

            for n, ph in enumerate(phases):
                kind = ph["kind"]
                open_phase("pe", pe, n)
                if n == 1:
                    take("vectors_copied")
                nb = phases[n - 1] if n and phases[n - 1]["kind"] == "norm" and phases[n - 1]["shift"] is not None else None
                if kind == "norm":
                    plain = ph["shift"] is None
                    for b in range(1 if follows(n - 1) and plain else 0, NB if plain else 1):
                        norm_turn(ph, b)
                elif kind == "turn":
                    turn(ph["src"], "turned", ("turned_read", "turned_read"))
                elif kind == "ffn":
                    ffn(ph, follows(n), nb)
                elif kind == "dense":
                    dense(ph, follows(n), nb)
                elif kind == "beside":
                    beside.begin(ph["steps"])
                elif kind == "beside_end":
                    beside.go()
                    turn_row()
                    settle()
                elif kind == "prepare":
                    beside.go(AT_PREPARE)
                elif kind == "latent":
                    mm(ps[:, 3, 0:HF], cc("upto"), fl2[:, 0, :])
                    mm(ps[:, 3, 8:8 + HF], ones, fl2[:, 0, :], True, False)
                    mm(ps[:, 3, 8:8 + HF], cc("upto"), fl2[:, 1, :], False, True)
                    for b in range(NB):
                        i = nc.tensor.transpose(ps[:, 0, b * P:(b + 1) * P], PJ[:, b, CKV:CKV + P], ident)
                    i.then_inc(sem("latent_turned"), 1)
                    beside.go(AT_LATENT)
                    take("latent_copied")
                    for b in range(NB):
                        mm(ps[:, 1, b * P:(b + 1) * P], work[:, 512 + b * P:512 + (b + 1) * P], w_kv)
                        i = nc.tensor.transpose(ps[0:HF, 2, b * P:(b + 1) * P], csum[:, b, :], ident)
                    i.then_inc(sem("latent_up"), 1)
                elif kind == "turn_heads":
                    turn(head_chunks(), "heads_turned", ("heads_read_dve", "heads_read_act"))
                    beside.go(AT_HEADS)
                elif kind == "index":
                    for b in range(NB):
                        n_k = (b + 1) * P
                        for h in range(HI):
                            i = mm(ps[:, 2 * b + h % 2, (h // 2) * SEQ:(h // 2) * SEQ + n_k],
                                   TT[rows_of(h), 16 + h // 2, b * P:(b + 1) * P], TT[rows_of(h), 18, 0:n_k])
                        i.then_inc(sem("index_dots"), 1)
                        beside.go(AT_INDEX)
                elif kind == "softmax":
                    run_items(softmax_items(), [2 * HF])
                elif kind == "near_turn":
                    turn(near_chunks(), "heads_turned", ("heads_read_dve", "heads_read_act"))
                    pe.wait_ge(sem("pool_in"), 32)
                    for n_g in range(5):
                        if n_g < 4:
                            g = n_g
                            for s in range(NB):
                                i = mm(ps[:, 4 + g % 2, 0:SEQ], PJ[:, s, 1536 + g * P:1536 + (g + 1) * P], poolA[:, g, s, :], s == 0, s == 1)
                            i.then_inc(sem("pooled"), 1)
                        if n_g >= 1:
                            g = n_g - 1
                            take("pooled_copied")
                            if g >= 2:
                                take("pool_split")
                            mm(ps[:, 6 + g % 2, 0:SEQ], poolW[:, g, :], work[:, (g % 2) * SEQ:(g % 2 + 1) * SEQ]).then_inc(sem("pool_mapped"), 1)
                    take("pool_split", 2)
                elif kind == "near":
                    pe.wait_ge(sem("near_in"), 16 * 32)
                    run_items(near_items())
                elif kind == "stick":
                    def z(h):
                        Z = ps[:, h % 2, :]
                        q, k = TT[rows_of(h), 6 + h // 2, :], TT[rows_of(h), 9 + h // 2, :]
                        mm(Z[:, 0:SEQ], k[:, 0:P], q)
                        mm(Z[:, SEQ:SBW], k[:, P:SEQ], q[:, P:SEQ]).then_inc(sem("stick_z"), 1)

                    def acc(h):
                        take("stick_l1")
                        A, l1 = ps[:, 2 + h % 2, :], sb_l1[h % 2]
                        mm(A[:, 0:P], cc("after"), l1[:, 0:P])
                        mm(A[:, P:SEQ], cc("after"), l1[:, P:SEQ], True, False)
                        mm(A[:, P:SEQ], ones, l1[:, SEQ:SBW], False, True)
                        mm(A[:, SEQ:SBW], cc("after"), l1[:, SEQ:SBW]).then_inc(sem("stick_acc"), 1)

                    def pv(h):
                        take("stick_a")
                        a, v = sb_a[h % 2], [PJ[:, c, VB + HD * h:VB + HD * (h + 1)] for c in range(NB)]
                        mm(ps[:, 4, HD * h:HD * (h + 1)], a[:, 0:P], v[0])
                        mm(ps[:, 5, HD * h:HD * (h + 1)], a[:, P:SEQ], v[0], True, False)
                        mm(ps[:, 5, HD * h:HD * (h + 1)], a[:, SEQ:SBW], v[1], False, True).then_inc(sem("stick_pv"), 1)

                    for h in range(HS + 2):
                        if h < HS:
                            z(h)
                        if 1 <= h <= HS:
                            acc(h - 1)
                        if h >= 2:
                            pv(h - 2)
                        beside.go(AT_STICK)
                elif kind == "conv":
                    for k in range(DC):
                        bank = k % 4
                        if k % 4 == 0:
                            take("conv_z")
                        if k >= 4:
                            take("conv_split")
                        for b in range(NB):
                            nc.tensor.transpose(ps[:, bank, b * P:(b + 1) * P], GT[:, b, 1024 + k * P:1024 + (k + 1) * P], ident)
                            i = nc.tensor.transpose(ps[:, bank, SEQ + b * P:SEQ + (b + 1) * P], GT[:, b, k * P:(k + 1) * P], ident)
                        i.then_inc(sem("conv_turned"), 1)
                    for _ in range(4):
                        take("conv_split")
                close_phase("pe", pe)

        @block.scalar
        def _(act):
            take = taker(act)
            link = linker(act, "act_chain")
            split = Splitter(act, split_hi)
            A = nc.scalar.activation

            copy_turned = turned_copier(act, take, lambda o, x: A(o, x, ACT.Copy), "heads_read_act")

            def hi_of_turned(dst, done, wait):
                for m in range(0, len(dst), 2):
                    bank = (m // 2) % 4
                    take(wait)
                    for j, (rows, o) in enumerate(dst[m:m + 2]):
                        i = A(o, ps[0:rows, bank, j * SEQ:(j + 1) * SEQ], ACT.Copy)
                    i.then_inc(sem(done), 1)

            def turn_dst(src, tile):
                return [(blocks[0].shape[-1], tile[0:blocks[0].shape[-1], m, :]) for m, blocks in enumerate(src)]

            def exps(items):
                for n, it in enumerate(items):
                    take("item_max")
                    if n >= 2:
                        take("item_turned")
                    A(prob[n % 2][:, 0:it["n"]], ps[:, n % 2, 0:it["n"]], ACT.Exp, bias=nmx[:, n:n + 1], scale=SCALE,
                      accum_out=rsum[:, n:n + 1]).then_inc(sem("item_exp"), 1)
                    beside.go(AT_ITEM)
                beside.go(2 * AT_ITEM)
                take("item_turned", min(2, len(items)))

            summed = []

            def gates():
                if summed:
                    u, ev = summed.pop()
                    act.wait_ge(s_used, u + 1)
                    for b in range(NB):
                        i = A(ev[1][b], ps[:, 6 + b, :], ACT.Sigmoid, scale=ev[2][:, b:b + 1])
                    i.then_inc(sem("beside_read"), 1)

            def beside_step(st):
                _, us, j, ev = st
                u = us[j][0]
                gates()
                split.upto(u + RING)
                if j == 1 and ev[0] == "sigmoid":
                    summed.append((u, ev))

            beside = Beside(beside_step)

            def square(ph, b):
                written(act, ph, b)
                link(A(work[:, b * D:(b + 1) * D], ph["x"][:, b, :], ACT.Square, accum_out=ssq[:, b:b + 1]))

            def root(b):
                A(ssq2[:, b:b + 1], ssq[:, b:b + 1], ACT.Sqrt, scale=1.0 / D, bias=eps).then_inc(sem("root"), 1)

            def norm_block(ph, b):
                if ph["shift"] is not None:
                    square(ph, b)
                    root(b)
                for half in range(2):
                    if ph["shift"] is not None and half == 0:
                        take("h_scaled")
                        for k in range(4 * half, 4 * half + 4):
                            i = A(hf[:, k, b * P:(b + 1) * P], ps[:, 4 + 2 * b + half, (k % 4) * P:(k % 4 + 1) * P],
                                  ACT.Identity, scale=ph["gain"][:, k:k + 1], bias=ph["shift"][:, k:k + 1])
                        link(i)
                    else:
                        take("h_gained")
                    A(HThi[:, 4 * half:4 * half + 4, b * P:(b + 1) * P],
                      hf[:, 4 * half:4 * half + 4, b * P:(b + 1) * P], ACT.Copy).then_inc(sem("h_hi"), 1)

            def gate_copy(ph, half, bank, coef):
                take("gate_turned")
                A(gateB[:, half * 512:(half + 1) * 512], ps[:, bank, :], ACT.Copy, scale=coef).then_inc(sem("gate_read"), 1)

            for n, ph in enumerate(phases):
                kind = ph["kind"]
                split.upto(first_unit[n] + RING - 1 if n else 0)
                open_phase("act", act, n)
                if ph.get("conditions"):
                    for st, name in enumerate(("c", "c_ctx")):
                        r = VEC_ROWS[name]
                        i = A(csil[:, :, st], vec[:, r:r + DC], ACT.Silu)
                    link(i)
                    A(CT[:, :, 0:2], csil[:], ACT.Copy).then_inc(sem("c_hi"), 1)
                if kind == "norm":
                    for b in range(1 if follows(n - 1) else 0, NB):
                        norm_block(ph, b)
                        split.upto(first_unit[n] + b + 1)
                    if ph["shift"] is None:
                        for b in range(NB):
                            square(ph, b)
                        for b in range(NB):
                            root(b)
                    split.upto(first_unit[n] + RING)
                elif kind == "final":
                    for b in range(NB):
                        square(ph, b)
                        root(b)
                        if ph["second"]:
                            take("final_done")
                            act.dma_start(out[0, b * P:(b + 1) * P, :], xn[:, b, :]).then_inc(sem("out_written"), 16)
                    if ph["second"]:
                        act.wait_ge(sem("out_written"), 16 * NB)
                elif kind == "turn":
                    hi_of_turned(turn_dst(ph["src"], HThi), "turned_hi", "turned")
                elif kind == "ffn":
                    split.upto(first_unit[n] + RING)
                    u0, n0 = ph["u0"], ph["f"] * GROUPS

                    def silu(lead):
                        act.wait_ge(s_used, lead * RING + (u0 + 2) if isinstance(lead, int) and lead == 0
                                    else lead * RING + (u0 + 1))
                        for b in range(NB):
                            scale = 1.0 if ph["rstd"] is None else ph["rstd"][:, b:b + 1]
                            A(sg[:, b, :], ps[:, b, 0:GW], ACT.Silu, scale=scale).then_inc(sem("ffn_silu"), 1)

                    def act_hi(lead, own=0):
                        act.wait_ge(sem("ffn_turned"), lead + (n0 + 1))
                        A(AT[own][0][:], ps[:, 2, :].rearrange("p (c t) -> p c t", c=2), ACT.Copy).then_inc(sem("ffn_act_hi"), 1)

                    def step(lead, first):
                        silu(0 if first else lead)
                        split_hi(act, u0 + 3, lead)
                        act_hi(lead)
                        split_hi(act, u0 + 4, lead)
                        split_hi(act, u0 + 5, lead)

                    if ph["rstd"] is not None:
                        take("rstd_ready")
                    step(0, True)
                    if ph["gate"]:
                        gate_copy(ph, 0, 3, 0.5)
                    with act.Fori(1, GROUPS - 1) as i:
                        step(i, False)
                    split.at = u0 + 3 * GROUPS
                    if ph["gate"]:
                        gate_copy(ph, 1, 3, 0.5)
                    silu(GROUPS - 1)
                    act_hi(GROUPS - 1, 1)
                    split.upto(split.at + 1)
                    if follows(n) and follows(n)["shift"] is not None:
                        A(scrap[:], ones[:, 0:1], ACT.Sqrt)
                        split.upto(split.at + 1)
                    if follows(n):
                        norm_block(follows(n), 0)
                elif kind == "dense":
                    if ph.get("gate"):
                        for half in range(2):
                            gate_copy(ph, half, 4 + half, 1.0)
                    if ph.get("rstd") is not None:
                        take("rstd_ready")
                    split.upto(first_unit[n] + RING)
                    for g, (us, w, ev) in enumerate(ph["groups"]):
                        last = us[-1][0]
                        split.upto(last + (RING - 1 if follows(n) and g == len(ph["groups"]) - 1 else RING))
                        if ev[0] == "copy":
                            act.wait_ge(s_used, last + 1)
                            for b in range(NB):
                                scale = 1.0 if ph.get("rstd") is None else ph["rstd"][:, b:b + 1]
                                i = A(ev[1][b], ps[:, 2 * (g % 2) + b, 0:w], ACT.Copy, scale=scale)
                            i.then_inc(sem("group_read"), 1)
                    if follows(n):
                        norm_block(follows(n), 0)
                elif kind == "beside":
                    beside.begin(ph["steps"])
                elif kind == "beside_end":
                    beside.go()
                    gates()
                elif kind == "latent":
                    beside.go(AT_LATENT)
                elif kind == "turn_heads":
                    copy_turned(head_chunks(), 1)
                    beside.go(AT_HEADS)
                elif kind == "prepare":
                    for b in range(NB):
                        at = 512 + b * (P + HD)
                        A(work[:, at:at + P], PJ[:, b, CKV:CKV + P], ACT.Square, accum_out=ssq[:, b:b + 1])
                        i = A(work[:, at + P:at + P + HD], PJ[:, b, KI:KI + HD], ACT.Square, accum_out=ssq[:, 2 + b:3 + b])
                    link(i)
                    for at, size in ((0, P), (2, HD)):
                        A(ssq2[:, at:at + 2], ssq[:, at:at + 2], ACT.Sqrt, scale=1.0 / size, bias=eps).then_inc(sem("root"), 1)
                    take("forget_sum")
                    link(A(fl2[:], fl[:], ACT.Abs))
                    link(A(fl2[:], fl2[:], ACT.Exp, scale=-1.0))
                    A(fl2[:], fl2[:], ACT.Ln, bias=1.0).then_inc(sem("forget_ln"), 1)
                    beside.go(AT_PREPARE)
                elif kind == "softmax":
                    exps(softmax_items())
                elif kind == "near":
                    exps(near_items())
                elif kind == "near_turn":
                    copy_turned(near_chunks(), 1)
                    for g in range(4):
                        take("pool_scaled")
                        A(HThi[:, 4 + g, :], pool_out[g % 2], ACT.Copy).then_inc(sem("pool_hi"), 1)
                elif kind == "index":
                    for b in range(NB):
                        take("index_dots")
                        for h2 in range(2):
                            w = (b + 1) * P
                            o = work[:, 1024 + (2 * b + h2) * 512:1024 + (2 * b + h2 + 1) * 512].rearrange("p (h k) -> p h k", h=2)
                            i = A(o[:, :, 0:w], ps[:, 2 * b + h2, :].rearrange("p (h k) -> p h k", h=2)[:, :, 0:w], ACT.Relu)
                        i.then_inc(sem("index_relu"), 1)
                        beside.go(AT_INDEX)
                elif kind == "stick":
                    def logs(h):
                        take("stick_z")
                        link(A(sb_abs, ps[:, h % 2, 0:SBW], ACT.Abs, scale=SCALE))
                        link(A(sb_abs, sb_abs, ACT.Exp, scale=-1.0))
                        link(A(sb_L[h % 2], sb_abs, ACT.Ln, bias=1.0))
                        act.sem_inc(sem("stick_L"), 1)

                    def weight(h):
                        take("stick_arg")
                        if h >= 2:
                            take("stick_pv")
                        A(sb_a[h % 2], sb_a[h % 2], ACT.Exp).then_inc(sem("stick_exp"), 1)

                    for h in range(HS + 1):
                        if h < HS:
                            logs(h)
                        gates()
                        if h >= 1:
                            weight(h - 1)
                        beside.go(AT_STICK)
                    take("stick_pv", 2)
                    beside.go(AT_STICK)
                    gates()
                elif kind == "conv":
                    for k in range(DC + 1):
                        if k < DC:
                            take("conv_turned")
                            link(A(conv_in[k % 2][:, 1:1 + SEQ], ps[:, k % 4, 0:SEQ], ACT.Copy))
                            A(conv_y[k % 2], conv_in[k % 2][:, 0:SEQ], ACT.Copy, scale=vcol("conv_w", k)).then_inc(sem("conv_tap"), 1)
                        if k:
                            take("conv_value")
                            A(HThi[:, k - 1, :], conv_out[(k - 1) % 2], ACT.Copy).then_inc(sem("conv_hi"), 1)
                close_phase("act", act)

        @block.vector
        def _(dve):
            take = taker(dve)
            link = linker(dve, "dve_chain")
            split = Splitter(dve, split_lo)
            V = nc.vector

            def lo_of_turned(src):
                for m in range(0, len(src), 2):
                    bank = (m // 2) % 4
                    take("turned_hi")
                    for j, blocks in enumerate(src[m:m + 2]):
                        rows = blocks[0].shape[-1]
                        i = V.tensor_tensor(HTlo[0:rows, m + j, :], ps[0:rows, bank, j * SEQ:(j + 1) * SEQ],
                                            HThi[0:rows, m + j, :].bitcast(F32), ALU.subtract)
                    i.then_inc(sem("turned_read"), 1)

            copy_turned = turned_copier(dve, take, V.tensor_copy, "heads_read_dve")

            pv_seen = [0]

            def run_items(items, ys):
                N = len(items)
                base = pv_seen[0]
                pv_seen[0] += N

                def sums(o, bank, first, heads):
                    last = first + 2 * heads
                    dve.wait_ge(sem("item_pv"), base + last)
                    link(V.reciprocal(rinv[:, first:last], rsum[:, first:last]))
                    for b in range(NB):
                        r = rinv[:, first + b:last:2].unsqueeze(2).broadcast_to([P, heads, HD])
                        i = V.tensor_tensor(o[b].rearrange("p (h d) -> p h d", d=HD),
                                            ps[:, bank + b, 0:heads * HD].rearrange("p (h d) -> p h d", d=HD), r, ALU.mult)
                    if last < N:
                        i.then_inc(sem("sums_read"), 1)

                for n in range(N + 2):
                    if n < N:
                        take("item_scores")
                        link(V.reduce_max(mx[:, n:n + 1], ps[:, n % 2, 0:items[n]["n"]], AX_X))
                        V.tensor_scalar(nmx[:, n:n + 1], mx[:, n:n + 1], -SCALE, None, ALU.mult).then_inc(sem("item_max"), 1)
                    if 1 <= n <= N:
                        m = n - 1
                        take("item_turned")
                        if m >= 2:
                            dve.wait_ge(sem("item_pv"), base + m - 1)
                        w = items[m]["n"]
                        V.tensor_copy(probT[m % 2][:, 0:w], ps[:, 2 + m % 2, 0:w]).then_inc(sem("item_copied"), 1)
                    for y in ys:
                        if n == y[2] + 2 * y[3] + 1:
                            sums(*y)
                    beside.go(AT_ITEM)

            def rope(x, heads):
                c = cc("cos").rearrange("p (b n) -> p b n", b=NB)
                s = cc("sin").rearrange("p (b n) -> p b n", b=NB)
                for b in range(NB):
                    cb = c[:, b, :].unsqueeze(1).broadcast_to([P, heads, 8])
                    sn = s[:, b, :].unsqueeze(1).broadcast_to([P, heads, 8])
                    x1, x2 = x[b][:, :, 0:8], x[b][:, :, 8:16]
                    tmp = [work[:, 2048 + 64 * j:2048 + 64 * j + 8 * heads].rearrange("p (h n) -> p h n", n=8) for j in range(4)]
                    V.tensor_tensor(tmp[0], x1, cb, ALU.mult)
                    V.tensor_tensor(tmp[1], x2, sn, ALU.mult)
                    V.tensor_tensor(tmp[2], x2, cb, ALU.mult)
                    link(V.tensor_tensor(tmp[3], x1, sn, ALU.mult))
                    V.tensor_tensor(x1, tmp[0], tmp[1], ALU.subtract)
                    link(V.tensor_tensor(x2, tmp[2], tmp[3], ALU.add))

            V.memset(eps, EPS)
            take("vectors_turned")
            for c, rows in enumerate(t["vector_chunks"]):
                i = V.tensor_copy(vec[:, c * P:c * P + rows], ps[:, c, 0:rows])
            i.then_inc(sem("vectors_copied"), 1)
            dve.wait_ge(sem("vectors_copied"), 1)
            dve.wait_ge(sem("consts_in"), 16)

            pending = []

            def add_bias():
                if pending:
                    _, l, k0 = pending.pop()
                    take("row_turned")
                    r = VEC_ROWS["mod_b"] + l * NMOD * DC + k0
                    V.tensor_tensor(modc[:, l, k0:k0 + 4, :], ps[:, 7, 0:8].rearrange("p (k s) -> p k s", s=2),
                                    vec[:, r:r + 4].unsqueeze(2).broadcast_to([P, 4, 2]), ALU.add).then_inc(sem("beside_read"), 1)

            def beside_step(st):
                _, us, j, ev = st
                u = us[j][0]
                add_bias()
                split.upto(u + RING - 1)
                if j == 1 and ev[0] == "mod":
                    dve.wait_ge(s_used, u + 1)
                    V.tensor_copy(mrow, ps[0:4, 6, :]).then_inc(sem("row_copied"), 1)
                    pending.append(ev)

            beside = Beside(beside_step)

            def inverse_root(rstd, b):
                take("root")
                return V.reciprocal(rstd[:, b:b + 1], ssq2[:, b:b + 1])

            def norm_scale(ph, b):
                if ph["shift"] is not None:
                    rstd = rst[:, 2 * ph["k"]:2 * ph["k"] + 2]
                    link(inverse_root(rstd, b))
                    V.tensor_scalar(unit_rms[b], ident, rstd[:, b:b + 1], None, ALU.mult).then_inc(sem("rms_ready"), 1)

            def norm_parts(ph, b):
                if ph["shift"] is None:
                    for half in range(2):
                        take("h_turned")
                        V.tensor_tensor(hf[:, 4 * half:4 * half + 4, b * P:(b + 1) * P],
                                        ps[:, 4 + 2 * b + half, :].rearrange("p (k t) -> p k t", k=4),
                                        ph["gain"][:, 4 * half:4 * half + 4].unsqueeze(2).broadcast_to([P, 4, P]),
                                        ALU.mult).then_inc(sem("h_gained"), 1)
                else:
                    take("h_turned")
                    for k in range(4, 8):
                        i = V.tensor_scalar(hf[:, k, b * P:(b + 1) * P], ps[:, 5 + 2 * b, (k - 4) * P:(k - 3) * P],
                                            ph["gain"][:, k:k + 1], ph["shift"][:, k:k + 1], ALU.mult, ALU.add)
                    i.then_inc(sem("h_gained"), 1)
                for half in range(2):
                    take("h_hi")
                    at = (slice(None), slice(4 * half, 4 * half + 4), slice(b * P, (b + 1) * P))
                    V.tensor_tensor(HTlo[at], hf[at], HThi[at].bitcast(F32), ALU.subtract).then_inc(sem("h_ready"), 1)

            def norm_first(ph, b):
                if b == 0:
                    norm_scale(ph, 0)
                if b == (0 if ph["shift"] is None else 1):
                    norm_parts(ph, 0)

            for n, ph in enumerate(phases):
                kind = ph["kind"]
                split.upto(first_unit[n] + RING - 1 if n else 0)
                open_phase("dve", dve, n)
                if ph.get("conditions"):
                    take("c_hi")
                    link(V.tensor_tensor(csil[:], csil[:], CT[:, :, 0:2].bitcast(F32), ALU.subtract))
                    V.tensor_copy(CT[:, :, 2:4], csil[:])
                if kind == "norm":
                    for b in range(1 if follows(n - 1) else 0, NB):
                        norm_scale(ph, b)
                        norm_parts(ph, b)
                        split.upto(first_unit[n] + b + 1)
                    if ph["shift"] is None:
                        rstd = rst[:, 2 * ph["k"]:2 * ph["k"] + 2]
                        for b in range(NB):
                            i = inverse_root(rstd, b)
                        link(i)
                        V.tensor_copy(rstd[:], rstd[:]).then_inc(sem("rstd_ready"), 1)
                    split.upto(first_unit[n] + RING)
                elif kind == "final":
                    take("g_in", 16 if ph["second"] else 32)
                    for b in range(NB):
                        take("root")
                        link(V.reciprocal(ssq2[:, b:b + 1], ssq2[:, b:b + 1]))
                        V.scalar_tensor_tensor(out=(xn if ph["second"] else X)[:, b, :], in0=X[:, b, :], scalar=ssq2[:, b:b + 1],
                                               in1=gB, op0=ALU.mult, op1=ALU.mult
                                               ).then_inc(sem("final_done" if ph["second"] else "x_written"), 1)
                elif kind == "turn":
                    lo_of_turned(ph["src"])
                elif kind == "ffn":
                    split.upto(first_unit[n] + RING)
                    u0, n0 = ph["u0"], ph["f"] * GROUPS
                    if ph.get("gains"):
                        for l in range(DEPTH):
                            for s3 in range(3):
                                r = VEC_ROWS["norm_g"] + (l * 3 + s3) * DC
                                for st in range(2):
                                    m = modc[:, l, (3 * s3 + 1) * DC:(3 * s3 + 2) * DC, st]
                                    V.scalar_tensor_tensor(out=m, in0=m, scalar=1.0, in1=vec[:, r:r + DC], op0=ALU.add, op1=ALU.mult)

                    def times_up(lead):
                        for b in range(NB):
                            dve.wait_ge(sem("ffn_silu"), lead * 2 + (2 * n0 + b + 1))
                            if ph["rstd"] is None:
                                i = V.tensor_tensor(av[:, b, :], sg[:, b, :], ps[:, b, GW:2 * GW], ALU.mult)
                            else:
                                i = V.scalar_tensor_tensor(out=av[:, b, :], in0=ps[:, b, GW:2 * GW], scalar=ph["rstd"][:, b:b + 1],
                                                           in1=sg[:, b, :], op0=ALU.mult, op1=ALU.mult)
                        i.then_inc(sem("ffn_act"), 1)

                    def act_lo(lead, own=0):
                        dve.wait_ge(sem("ffn_act_hi"), lead + (n0 + 1))
                        V.tensor_tensor(AT[own][1][:], ps[:, 2, :].rearrange("p (c t) -> p c t", c=2), AT[own][0][:].bitcast(F32),
                                        ALU.subtract).then_inc(sem("ffn_act_lo"), 1)

                    def step(lead):
                        times_up(lead)
                        split_lo(dve, u0 + 3, lead)
                        act_lo(lead)
                        split_lo(dve, u0 + 4, lead)
                        split_lo(dve, u0 + 5, lead)

                    with dve.Fori(0, GROUPS - 1) as i:
                        step(i)
                    split.at = u0 + 3 * GROUPS
                    times_up(GROUPS - 1)
                    act_lo(GROUPS - 1, 1)
                    split.upto(split.at + 1)
                    x, name = ph["x"], "c_written" if ph["x"] is C else "x_written"
                    if ph["gate"]:
                        take("gate_read", 2)
                    for b in range(NB):
                        if b == 0:
                            take("ffn_out")
                        else:
                            dve.wait_ge(s_used, u0 + 3 * GROUPS)
                        y = ps[:, 4 + 2 * b:6 + 2 * b, :].rearrange("p a n -> p (a n)")
                        if ph["gate"]:
                            link(V.tensor_tensor(xn[:, b, :], y, gateB, ALU.mult))
                            V.tensor_tensor(x[:, b, :], x[:, b, :], xn[:, b, :], ALU.add).then_inc(sem(name), 1)
                        else:
                            V.scalar_tensor_tensor(out=x[:, b, :], in0=y, scalar=0.5, in1=x[:, b, :],
                                                   op0=ALU.mult, op1=ALU.add).then_inc(sem(name), 1)
                        if follows(n):
                            norm_first(follows(n), b)
                elif kind == "beside":
                    beside.begin(ph["steps"])
                elif kind == "beside_end":
                    beside.go()
                    add_bias()
                elif kind == "dense":
                    if ph.get("gate"):
                        take("gate_read", 2)
                    split.upto(first_unit[n] + RING)

                    for g, (us, w, ev) in enumerate(ph["groups"]):
                        last = us[-1][0]
                        if g < len(ph["groups"]) - 1 or ev[0] == "copy":
                            split.upto(last + RING)
                        elif follows(n):
                            split.upto(last + RING - 1)
                        P2 = 2 * (g % 2)
                        if ev[0] == "merge":
                            _, r, n0 = ev
                            dve.wait_ge(s_used, last + 1)
                            for b in range(NB):
                                o = C[:, b, n0:n0 + 512]
                                dst = o if r == 0 else work[:, b * 512:(b + 1) * 512]
                                i = V.tensor_tensor(dst, ps[:, P2 + b, :], GT[:, b, r * D + n0:r * D + n0 + 512], ALU.mult)
                            i.then_inc(sem("group_read"), 1)
                            if r:
                                dve.wait_ge(sem("group_read"), reads_before(n) + g + 1)
                                for b in range(NB):
                                    o = C[:, b, n0:n0 + 512]
                                    link(V.tensor_tensor(o, o, work[:, b * 512:(b + 1) * 512], ALU.add))
                        elif ev[0] in ("add", "addgate"):
                            n0 = ev[1]
                            final = g == len(ph["groups"]) - 1
                            for b in range(NB):
                                if final and b == 0 and follows(n):
                                    take("block_out")
                                else:
                                    dve.wait_ge(s_used, last + 1)
                                o, p = X[:, b, n0:n0 + 512], ps[:, P2 + b, :]
                                if ev[0] == "add":
                                    i = V.tensor_tensor(o, p, o, ALU.add)
                                else:
                                    gated = work[:, (P2 + b) * 512:(P2 + b + 1) * 512]
                                    link(V.tensor_tensor(gated, p, gateB[:, n0:n0 + 512], ALU.mult))
                                    i = V.tensor_tensor(o, o, gated, ALU.add)
                                if final:
                                    i.then_inc(sem("x_written"), 1)
                                    if follows(n):
                                        norm_first(follows(n), b)
                elif kind == "prepare":
                    dve.wait_ge(sem("prep_in"), 64 * (ph["l"] + 1))
                    V.tensor_tensor(fl[:], PJ[:, :, FA:FA + HF], bfr.unsqueeze(1).broadcast_to([P, NB, HF]),
                                    ALU.add).then_inc(sem("forget_sum"), 1)
                    take("root", 2)
                    link(V.reciprocal(ssq2[:, 0:4], ssq2[:, 0:4]))
                    for b in range(NB):
                        V.scalar_tensor_tensor(out=PJ[:, b, CKV:CKV + P], in0=PJ[:, b, CKV:CKV + P], scalar=ssq2[:, b:b + 1],
                                               in1=g_latent, op0=ALU.mult, op1=ALU.mult)
                        link(V.scalar_tensor_tensor(out=PJ[:, b, KI:KI + HD], in0=PJ[:, b, KI:KI + HD],
                                                    scalar=ssq2[:, 2 + b:3 + b], in1=g_index, op0=ALU.mult, op1=ALU.mult))
                    rope([PJ[:, b, QC:QC + HX * HD].rearrange("p (h d) -> p h d", d=HD) for b in range(NB)], HX)
                    rope([PJ[:, b, QI:QI + 5 * HD].rearrange("p (h d) -> p h d", d=HD) for b in range(NB)], 5)
                    beside.go(2)
                    take("forget_ln")
                    V.scalar_tensor_tensor(out=fl2[:], in0=fl[:], scalar=0.0, in1=fl2[:], op0=ALU.min, op1=ALU.subtract)
                    beside.go(AT_PREPARE - 2)
                elif kind == "latent":
                    take("latent_turned")
                    V.tensor_copy(work[:, 512:512 + SEQ], ps[:, 0, 0:SEQ])
                    V.tensor_copy(csum[:], ps[:, 3, 0:16].rearrange("p (b h) -> p b h", b=2)[:, :, 0:HF]).then_inc(sem("latent_copied"), 1)
                    beside.go(AT_LATENT)
                    take("latent_up")
                    V.tensor_scalar(csT, ps[0:HF, 2, 0:SEQ], -1.0 / SCALE, None, ALU.mult)
                    link(V.tensor_copy(KV, ps[:, 1, 0:SEQ].rearrange("p (b n) -> p b n", b=NB)))
                    rope([KV[:, b, 0:HD].rearrange("p (h d) -> p h d", d=HD) for b in range(NB)], 1)
                    dup = work[:, 0:512].rearrange("p (j b n) -> p j b n", j=2, b=NB)
                    for e in range(2):
                        V.tensor_copy(dup[:, 0, :, HD * e:HD * (e + 1)], KV[:, :, 0:HD])
                        V.tensor_copy(dup[:, 1, :, HD * e:HD * (e + 1)], PJ[:, :, KI:KI + HD])
                elif kind == "turn_heads":
                    copy_turned(head_chunks(), 0)
                    beside.go(AT_HEADS)
                elif kind == "index":
                    sc = work[:, 0:SEQ]
                    top = small[:, 448:456]
                    for b in range(NB):
                        w = (b + 1) * P
                        take("index_relu")
                        for h in range(HI):
                            at = 1024 + b * 1024 + (h % 2) * 512 + (h // 2) * SEQ
                            r = work[:, at:at + w]
                            link(V.scalar_tensor_tensor(out=sc[:, 0:w], in0=r, scalar=PJ[:, b, WI + h:WI + h + 1],
                                                        in1=cc(f"chunks{b}") if h == 0 else sc[:, 0:w], op0=ALU.mult, op1=ALU.add))
                        left = work[:, 512:512 + w]
                        for r8 in range(TOPK // 8):
                            src = sc[:, 0:w] if r8 == 0 else left
                            link(V.max(top, src))
                            link(V.match_replace(left, top, src, 2 * NEG))
                            if r8 % 2:
                                beside.go(AT_INDEX // 4)
                        V.tensor_scalar(score_add[:, b, 0:w], left, 1.5 * NEG, NEG, ALU.is_gt, ALU.mult)
                elif kind == "softmax":
                    run_items(softmax_items(), [([PJ[:, b, QA:QA + HF * HD] for b in range(NB)], 4, 0, HF),
                                                ([PJ[:, b, QC:QC + HX * HD] for b in range(NB)], 4, 2 * HF, HX)])
                elif kind == "near_turn":
                    copy_turned(near_chunks(), 0)
                    for n_g in range(6):
                        if n_g < 4:
                            g = n_g
                            take("pooled")
                            V.tensor_copy(work[:, (g % 2) * SEQ:(g % 2 + 1) * SEQ], ps[:, 4 + g % 2, 0:SEQ]).then_inc(sem("pooled_copied"), 1)
                        if 1 <= n_g < 5:
                            g = n_g - 1
                            take("pool_mapped")
                            V.tensor_scalar(pool_out[g % 2], ps[:, 6 + g % 2, 0:SEQ], vcol("pool_scale", g), None,
                                            ALU.mult).then_inc(sem("pool_scaled"), 1)
                        if n_g >= 2:
                            g = n_g - 2
                            take("pool_hi")
                            V.tensor_tensor(HTlo[:, 4 + g, :], pool_out[g % 2], HThi[:, 4 + g, :].bitcast(F32),
                                            ALU.subtract).then_inc(sem("pool_split"), 1)
                elif kind == "near":
                    run_items(near_items(), [([work[:, 2048 + b * 512:2048 + (b + 1) * 512] for b in range(NB)], 4, 0, NA_H)])
                elif kind == "stick":
                    before = cc("before")

                    def logs(h):
                        take("stick_L")
                        z, L, l1, ls = ps[:, h % 2, 0:SBW], sb_L[h % 2], sb_l1[h % 2], sb_ls[h % 2]
                        link(V.tensor_scalar(ls, z, SCALE, 0.0, ALU.mult, ALU.min))
                        link(V.tensor_tensor(ls, ls, L, ALU.subtract))
                        link(V.scalar_tensor_tensor(out=l1, in0=z, scalar=-SCALE, in1=ls, op0=ALU.mult, op1=ALU.add))
                        V.tensor_tensor(l1[:, 0:P], l1[:, 0:P], before, ALU.mult)
                        V.tensor_tensor(l1[:, SEQ:SBW], l1[:, SEQ:SBW], before, ALU.mult).then_inc(sem("stick_l1"), 1)

                    def weight(h):
                        take("stick_acc")
                        if h >= 2:
                            take("stick_pv")
                        a = sb_a[h % 2]
                        V.tensor_tensor(a, ps[:, 2 + h % 2, 0:SBW], sb_ls[h % 2], ALU.add).then_inc(sem("stick_arg"), 1)
                        take("stick_exp")
                        V.tensor_tensor(a[:, 0:P], a[:, 0:P], before, ALU.mult)
                        V.tensor_tensor(a[:, SEQ:SBW], a[:, SEQ:SBW], before, ALU.mult).then_inc(sem("stick_a"), 1)

                    for h in range(HS + 1):
                        if h < HS:
                            logs(h)
                        if h >= 1:
                            weight(h - 1)
                        beside.go(AT_STICK)
                    take("stick_pv", 2)
                    beside.go(AT_STICK)
                    for b in range(NB):
                        V.tensor_copy(PJ[:, b, QB:QB + HS * HD], ps[:, 4 + b, 0:HS * HD])
                elif kind == "conv":
                    for z in conv_in:
                        V.memset(z[:, 0:1], 0.0)
                        V.memset(z[:, 1 + SEQ:2 + SEQ], 0.0)
                    for h in range(2):
                        c = 1024 + h * 512
                        V.tensor_tensor(GT[:, :, c:c + 512], GT[:, :, c:c + 512], GT[:, :, c + 1024:c + 1536],
                                        ALU.mult).then_inc(sem("conv_z"), 1)
                    for k in range(DC + 1):
                        if k < DC:
                            z, y = conv_in[k % 2], conv_y[k % 2]
                            take("conv_tap")
                            for j in (1, 2):
                                link(V.scalar_tensor_tensor(out=y, in0=z[:, j:j + SEQ], scalar=vcol("conv_w", j * DC + k), in1=y,
                                                            op0=ALU.mult, op1=ALU.add))
                            V.tensor_tensor(conv_out[k % 2], ps[:, k % 4, SEQ:2 * SEQ], y, ALU.mult).then_inc(sem("conv_value"), 1)
                        if k:
                            take("conv_hi")
                            V.tensor_tensor(HTlo[:, k - 1, :], conv_out[(k - 1) % 2], HThi[:, k - 1, :].bitcast(F32),
                                            ALU.subtract).then_inc(sem("conv_split"), 1)
                close_phase("dve", dve)


_ORDER = [
    "x", "w_ffn1_gu", "w_ffn1_down", "w_in", "b_forget", "g_kv_latent", "w_kv_up", "g_idx_k",
    "w_up_fox", "w_up_sb", "w_up_dsa", "w_out", "w_ffn2_gu", "w_ffn2_down", "g_final", "ctx_2",
    "mod_w_2", "ffn_w13_2", "ffn_w2_2", "even_w_in_2", "even_w_out_2",
    "na_rpb_2", "pool_w_2", "conv_w_in_2", "conv_w_out_2", "final_g_2",
    "g_ffn1", "g_mix", "g_ffn2", "c_2", "c_ctx_2", "mod_b_2", "norm_g_2", "pool_scale_2", "conv_w_2",
]
_VECTORS = [("g_ffn1", "g_ffn1"), ("g_mix", "g_mix"), ("g_ffn2", "g_ffn2"), ("c", "c_2"), ("c_ctx", "c_ctx_2"),
            ("norm_g", "norm_g_2"), ("pool_scale", "pool_scale_2"), ("conv_w", "conv_w_2"), ("mod_b", "mod_b_2")]


def place_vectors(t):
    t["vectors"], t["vector_chunks"] = [], []
    row = 0
    for name, key in _VECTORS:
        ap = t[key]
        while len(ap.shape) > 1:
            ap = ap.rearrange("a b -> (a b)") if len(ap.shape) == 2 else ap.rearrange("a b c -> (a b) c")
        ap = ap.rearrange("(r p) -> r p", p=P)
        VEC_ROWS[name] = row
        at, n = 0, ap.shape[0]
        while at < n:
            k = min(n - at, P - row % P)
            t["vectors"].append((ap[at:at + k], row // P, row % P))
            at += k
            row += k
    t["vector_chunks"] = [min(P, row - c * P) for c in range((row + P - 1) // P)]


def kernel(**inputs):
    import numpy as _np
    import concourse.bacc as _bacc
    from concourse import mybir as _mybir
    from concourse.bass_utils import run_bass_kernel_spmd as _run

    nc = _bacc.Bacc("TRN2", target_bir_lowering=False, num_devices=1)
    arrays, t = {}, {}
    inputs = {n: inputs[n] for n in _ORDER}
    inputs["consts"] = constants()
    inputs["pool_mats"] = pool_matrices()
    for name, a in inputs.items():
        a = _np.ascontiguousarray(a)
        arrays[f"in_{name}_dram"] = a
        t[name] = nc.dram_tensor(f"in_{name}_dram", a.shape, _mybir.dt.from_np(a.dtype), kind="ExternalInput").ap()
    place_vectors(t)
    out = nc.dram_tensor("out_0_dram", (1, SEQ, D), _mybir.dt.float32, kind="ExternalOutput").ap()
    program(nc, t, out)
    r = _run(nc, [arrays], core_ids=[0])
    return r.results[0]["out_0_dram"]
```
